# Optimizing a Trainium2 kernel written in Bass

```python
import jax, jax.numpy as jnp
from jax import lax
import numpy as np

D_MODEL = 1024
BATCH = 1
SEQ = 1024
DEPTH = 2

GRID_W = 64
CTX_LEN = 256
CONV_W = 3
EPS = 1e-6
SC_CH = 512
FT_CH = 512
FT_GROUPS = 4
FT_GROUP_CH = FT_CH // FT_GROUPS
EVEN_IN = 3 * SC_CH + FT_CH
EVEN_OUT = SC_CH + FT_CH
ATT_HEADS = 8
ATT_KV_HEADS = 2
ATT_GROUP = ATT_HEADS // ATT_KV_HEADS
HEAD_DIM = 64
ATT_SCALE = HEAD_DIM ** -0.5
WINDOW = 128
BLOCK = 128
ROPE_THETA = 10000.0
ML_HEADS = 4
ML_QK_DIM = 64
ML_V_DIM = 128
ML_CHUNK = 64
ATT_Q = ATT_HEADS * HEAD_DIM
ATT_KV = ATT_KV_HEADS * HEAD_DIM
ML_QK = ML_HEADS * ML_QK_DIM
ML_V = ML_HEADS * ML_V_DIM
ODD_IN = ATT_Q + 2 * ATT_KV + 2 * ML_QK + 2 * ML_V + 4 * ML_HEADS
ODD_OUT = ATT_Q + ML_V
D_FF = 2816
N_EVEN = (DEPTH + 1) // 2
N_ODD = DEPTH // 2

kernel_name = "hybrid_conv_fourier_swa_mlstm_dit"

def rms_norm(x, g):
    xf = x.astype(jnp.float32)
    y = xf * lax.rsqrt(jnp.mean(xf * xf, axis=-1, keepdims=True) + EPS)
    return (y * g.astype(jnp.float32)).astype(x.dtype)

def modulation(cv, w, b):
    mod = (jax.nn.silu(cv) @ w + b)[..., None, :]
    return jnp.split(mod, 6, axis=-1)

def dwconv3(x, w):
    xp = jnp.pad(x, ((0, 0), (1, 1), (0, 0)))
    return xp[:, :-2] * w[0] + xp[:, 1:-1] * w[1] + xp[:, 2:] * w[2]

def short_conv_mix(u, w_conv):
    b_gate, c_gate, xv = jnp.split(u, 3, axis=-1)
    return b_gate * dwconv3(c_gate * xv, w_conv)

def fourier_mix(u):
    B_, L, _ = u.shape
    ug = u.reshape(B_, L, FT_GROUPS, FT_GROUP_CH).astype(jnp.float32)
    y = jnp.fft.fft2(ug, axes=(1, 3), norm="ortho").real
    return y.reshape(B_, L, FT_CH).astype(u.dtype)

def even_mixer(h, w_in, w_conv, w_out):
    u = h @ w_in
    y_conv = short_conv_mix(u[..., :3 * SC_CH], w_conv)
    y_four = fourier_mix(u[..., 3 * SC_CH:])
    return jnp.concatenate([y_conv, y_four], axis=-1) @ w_out

def axial_rope_tables(L):
    rows = L // GRID_W
    row = jnp.repeat(jnp.arange(rows, dtype=jnp.float32), GRID_W)
    col = jnp.tile(jnp.arange(GRID_W, dtype=jnp.float32), rows)
    axis_dim = HEAD_DIM // 2
    inv_freq = ROPE_THETA ** (-jnp.arange(0, axis_dim, 2, dtype=jnp.float32) / axis_dim)
    ang = jnp.stack([row, col])[:, :, None] * inv_freq
    return jnp.cos(ang), jnp.sin(ang)

def apply_axial_rope(x, cos, sin):
    lead = (slice(None),) + (None,) * (x.ndim - 3)
    outs = []
    for a, xa in enumerate(jnp.split(x, 2, axis=-1)):
        x1, x2 = jnp.split(xa, 2, axis=-1)
        cs = cos[a][lead].astype(x.dtype)
        sn = sin[a][lead].astype(x.dtype)
        outs += [x1 * cs - x2 * sn, x1 * sn + x2 * cs]
    return jnp.concatenate(outs, axis=-1)

def odd_project(h, w_in, gate_b, q_g, k_g):
    B_, L, _ = h.shape
    u = h @ w_in
    idx = np.cumsum([ATT_Q, ATT_KV, ATT_KV, ML_QK, ML_QK, ML_V, ML_V]).tolist()
    q_a, k_a, v_a, q_m, k_m, v_m, o_m, g = jnp.split(u, idx, axis=-1)
    q_a = rms_norm(q_a.reshape(B_, L, ATT_KV_HEADS, ATT_GROUP, HEAD_DIM), q_g)
    k_a = rms_norm(k_a.reshape(B_, L, ATT_KV_HEADS, HEAD_DIM), k_g)
    v_a = v_a.reshape(B_, L, ATT_KV_HEADS, HEAD_DIM)
    q_m = q_m.reshape(B_, L, ML_HEADS, ML_QK_DIM)
    k_m = k_m.reshape(B_, L, ML_HEADS, ML_QK_DIM) * (ML_QK_DIM ** -0.5)
    v_m = v_m.reshape(B_, L, ML_HEADS, ML_V_DIM)
    g = g.astype(jnp.float32).reshape(B_, L, 4, ML_HEADS) + gate_b
    gates = (g[:, :, 0], jax.nn.log_sigmoid(g[:, :, 1]), g[:, :, 2], jax.nn.log_sigmoid(g[:, :, 3]))
    return q_a, k_a, v_a, (q_m, k_m, v_m, gates), o_m

def windowed_sink_attention(q, k, v, k_ctx, v_ctx, sink):
    B_, L = q.shape[:2]
    nb = L // BLOCK
    qb = q.reshape(B_, nb, BLOCK, ATT_KV_HEADS, ATT_GROUP, HEAD_DIM)

    def band(a):
        ap = jnp.pad(a, ((0, 0), (BLOCK, BLOCK), (0, 0), (0, 0))).reshape(B_, nb + 2, BLOCK, ATT_KV_HEADS, HEAD_DIM)
        return jnp.concatenate([ap[:, :-2], ap[:, 1:-1], ap[:, 2:]], axis=2)

    kb, vb = band(k), band(v)
    qi = jnp.arange(BLOCK)[:, None] + BLOCK
    kj = jnp.arange(3 * BLOCK)[None, :]
    key_pos = (jnp.arange(nb)[:, None, None] - 1) * BLOCK + kj
    mask = (jnp.abs(kj - qi) <= WINDOW)[None] & (key_pos >= 0) & (key_pos < L)
    s_loc = jnp.einsum("bnqhgd,bnkhd->bnhgqk", qb, kb).astype(jnp.float32)
    s_loc = jnp.where(mask[None, :, None, None], s_loc, -jnp.inf)
    s_ctx = jnp.einsum("bnqhgd,bkhd->bnhgqk", qb, k_ctx).astype(jnp.float32)
    sk = sink.astype(jnp.float32).reshape(1, 1, ATT_KV_HEADS, ATT_GROUP, 1)
    m = jnp.maximum(jnp.maximum(jnp.max(s_loc, axis=-1), jnp.max(s_ctx, axis=-1)), sk)
    p_loc = jnp.exp(s_loc - m[..., None])
    p_ctx = jnp.exp(s_ctx - m[..., None])
    inv = (1.0 / (jnp.sum(p_loc, axis=-1) + jnp.sum(p_ctx, axis=-1) + jnp.exp(sk - m)))[..., None]
    o = (jnp.einsum("bnhgqk,bnkhd->bnqhgd", p_loc * inv, vb.astype(jnp.float32))
         + jnp.einsum("bnhgqk,bkhd->bnqhgd", p_ctx * inv, v_ctx.astype(jnp.float32)))
    return o.reshape(B_, L, ATT_Q).astype(v.dtype)

def context_sink_attention(q, k, v, sink):
    B_, C = q.shape[:2]
    s = jnp.einsum("bqhgd,bkhd->bhgqk", q, k).astype(jnp.float32)
    sk = sink.astype(jnp.float32).reshape(1, ATT_KV_HEADS, ATT_GROUP, 1)
    m = jnp.maximum(jnp.max(s, axis=-1), sk)
    p = jnp.exp(s - m[..., None])
    p = p / (jnp.sum(p, axis=-1) + jnp.exp(sk - m))[..., None]
    o = jnp.einsum("bhgqk,bkhd->bqhgd", p, v.astype(jnp.float32))
    return o.reshape(B_, C, ATT_Q).astype(v.dtype)

def mlstm_chunk_scan(q, k, v, ig, lf, state, with_output):
    B_, L = q.shape[:2]
    nc = L // ML_CHUNK

    def chunks(a):
        a = a.astype(jnp.float32)
        return jnp.moveaxis(a.reshape((B_, nc, ML_CHUNK) + a.shape[2:]), 1, 0)

    xs = (chunks(q), chunks(k), chunks(v), chunks(ig), chunks(lf))
    past_mask = jnp.tril(jnp.ones((ML_CHUNK, ML_CHUNK), dtype=bool))[None, :, :, None]

    def body(carry, xc):
        C, n, m = carry
        qc, kc, vc, ic, fc = xc
        b = jnp.cumsum(fc, axis=1)
        b_end = b[:, -1]
        w_end = b_end[:, None] - b + ic
        m_new = jnp.maximum(b_end + m, jnp.max(w_end, axis=1))
        decay = jnp.exp(b_end + m - m_new)
        wu = jnp.exp(w_end - m_new[:, None])
        C_new = decay[..., None, None] * C + jnp.einsum("bth,bthv,bthk->bhvk", wu, vc, kc)
        n_new = decay[..., None] * n + jnp.einsum("bth,bthk->bhk", wu, kc)
        new = (C_new, n_new, m_new)
        if not with_output:
            return new, None
        log_d = jnp.where(past_mask, b[:, :, None] - b[:, None] + ic[:, None], -jnp.inf)
        m_t = jnp.maximum(b + m[:, None], jnp.max(log_d, axis=2))
        inter = jnp.exp(b + m[:, None] - m_t)
        qk = jnp.einsum("bthk,bshk->btsh", qc, kc) * jnp.exp(log_d - m_t[:, :, None])
        num = jnp.einsum("btsh,bshv->bthv", qk, vc) + inter[..., None] * jnp.einsum("bhvk,bthk->bthv", C, qc)
        den = jnp.sum(qk, axis=2) + inter * jnp.einsum("bhk,bthk->bth", n, qc)
        h = num / jnp.maximum(jnp.abs(den), jnp.exp(-m_t))[..., None]
        return new, h

    state, hs = lax.scan(body, state, xs)
    if with_output:
        hs = jnp.moveaxis(hs, 0, 1).reshape(B_, L, ML_HEADS, ML_V_DIM)
    return state, hs

def bidir_mlstm(lat, ctx, need_ctx_out):
    q_l, k_l, v_l, (i_lf, f_lf, i_lb, f_lb) = lat
    q_c, k_c, v_c, (i_cf, f_cf, i_cb, f_cb) = ctx
    B_ = q_l.shape[0]
    zero = (jnp.zeros((B_, ML_HEADS, ML_V_DIM, ML_QK_DIM), jnp.float32),
            jnp.zeros((B_, ML_HEADS, ML_QK_DIM), jnp.float32),
            jnp.zeros((B_, ML_HEADS), jnp.float32))
    rev = lambda a: a[:, ::-1]
    st, hc_f = mlstm_chunk_scan(q_c, k_c, v_c, i_cf, f_cf, zero, need_ctx_out)
    _, hl_f = mlstm_chunk_scan(q_l, k_l, v_l, i_lf, f_lf, st, True)
    st, hc_b = mlstm_chunk_scan(rev(q_c), rev(k_c), rev(v_c), rev(i_cb), rev(f_cb), zero, need_ctx_out)
    _, hl_b = mlstm_chunk_scan(rev(q_l), rev(k_l), rev(v_l), rev(i_lb), rev(f_lb), st, True)
    h_lat = hl_f + rev(hl_b)
    h_ctx = hc_f + rev(hc_b) if need_ctx_out else None
    return h_lat, h_ctx

def odd_mixer(h_lat, h_ctx, rope, w_in, gate_b, q_g, k_g, sink, w_out, need_ctx_out):
    cos, sin = rope
    qa, ka, va, ml_lat, o_lat = odd_project(h_lat, w_in, gate_b, q_g, k_g)
    qc, kc, vc, ml_ctx, o_ctx = odd_project(h_ctx, w_in, gate_b, q_g, k_g)
    qa = apply_axial_rope(qa, cos, sin) * ATT_SCALE
    ka = apply_axial_rope(ka, cos, sin)
    att_lat = windowed_sink_attention(qa, ka, va, kc, vc, sink)
    hm_lat, hm_ctx = bidir_mlstm(ml_lat, ml_ctx, need_ctx_out)
    B_, L = h_lat.shape[:2]
    ml_out = hm_lat.reshape(B_, L, ML_V).astype(h_lat.dtype) * jax.nn.sigmoid(o_lat)
    y_lat = jnp.concatenate([att_lat, ml_out], axis=-1) @ w_out
    y_ctx = None
    if need_ctx_out:
        att_ctx = context_sink_attention(qc * ATT_SCALE, kc, vc, sink)
        C = h_ctx.shape[1]
        ml_ctx_out = hm_ctx.reshape(B_, C, ML_V).astype(h_ctx.dtype) * jax.nn.sigmoid(o_ctx)
        y_ctx = jnp.concatenate([att_ctx, ml_ctx_out], axis=-1) @ w_out
    return y_lat, y_ctx

def conv_ffn(h, w_up, w_conv, w_down):
    g, val = jnp.split(h @ w_up, 2, axis=-1)
    return (jax.nn.silu(dwconv3(g, w_conv)) * val) @ w_down

def setup_inputs(seed: int = 0) -> dict:
    key = jax.random.key(seed)
    ks = jax.random.split(key, 20)
    nrm = lambda k, shape, scale: jax.random.normal(k, shape, jnp.float32) * scale
    return {
        "x": nrm(ks[0], (BATCH, SEQ, D_MODEL), 1.0),
        "c": nrm(ks[1], (BATCH, D_MODEL), 1.0),
        "ctx": nrm(ks[2], (BATCH, CTX_LEN, D_MODEL), 1.0),
        "c_ctx": nrm(ks[3], (D_MODEL,), 1.0),
        "ada_w": nrm(ks[4], (DEPTH, D_MODEL, 6 * D_MODEL), 0.5 * D_MODEL ** -0.5),
        "ada_b": nrm(ks[5], (DEPTH, 6 * D_MODEL), 0.02),
        "norm_g": 1.0 + nrm(ks[6], (DEPTH, 2, D_MODEL), 0.02),
        "even_w_in": nrm(ks[7], (N_EVEN, D_MODEL, EVEN_IN), D_MODEL ** -0.5),
        "even_conv": nrm(ks[8], (N_EVEN, CONV_W, SC_CH), CONV_W ** -0.5),
        "even_w_out": nrm(ks[9], (N_EVEN, EVEN_OUT, D_MODEL), EVEN_OUT ** -0.5),
        "odd_w_in": nrm(ks[10], (N_ODD, D_MODEL, ODD_IN), D_MODEL ** -0.5),
        "odd_gate_b": jnp.array([0.0, 3.0, 0.0, 3.0], jnp.float32)[None, :, None] + nrm(ks[11], (N_ODD, 4, ML_HEADS), 0.1),
        "odd_q_g": 1.0 + nrm(ks[12], (N_ODD, HEAD_DIM), 0.02),
        "odd_k_g": 1.0 + nrm(ks[13], (N_ODD, HEAD_DIM), 0.02),
        "odd_sink": nrm(ks[14], (N_ODD, ATT_HEADS), 0.5),
        "odd_w_out": nrm(ks[15], (N_ODD, ODD_OUT, D_MODEL), ODD_OUT ** -0.5),
        "ffn_w_up": nrm(ks[16], (DEPTH, D_MODEL, 2 * D_FF), D_MODEL ** -0.5),
        "ffn_conv": nrm(ks[17], (DEPTH, CONV_W, D_FF), CONV_W ** -0.5),
        "ffn_w_down": nrm(ks[18], (DEPTH, D_FF, D_MODEL), D_FF ** -0.5),
    }

def reference(x, c, ctx, c_ctx, ada_w, ada_b, norm_g, even_w_in, even_conv, even_w_out, odd_w_in, odd_gate_b,
              odd_q_g, odd_k_g, odd_sink, odd_w_out, ffn_w_up, ffn_conv, ffn_w_down):
    L = x.shape[1]
    rope = axial_rope_tables(L)
    xl, xc = x, ctx
    for layer in range(DEPTH):
        last = layer == DEPTH - 1
        j = layer // 2
        sh1, sc1, g1, sh2, sc2, g2 = modulation(c, ada_w[layer], ada_b[layer])
        csh1, csc1, cg1, csh2, csc2, cg2 = modulation(c_ctx, ada_w[layer], ada_b[layer])
        hl = rms_norm(xl, norm_g[layer, 0]) * (1 + sc1) + sh1
        hc = rms_norm(xc, norm_g[layer, 0]) * (1 + csc1) + csh1
        if layer % 2 == 0:
            yl = even_mixer(hl, even_w_in[j], even_conv[j], even_w_out[j])
            yc = None if last else even_mixer(hc, even_w_in[j], even_conv[j], even_w_out[j])
        else:
            yl, yc = odd_mixer(hl, hc, rope, odd_w_in[j], odd_gate_b[j], odd_q_g[j], odd_k_g[j], odd_sink[j],
                               odd_w_out[j], not last)
        xl = xl + g1 * yl
        xl = xl + g2 * conv_ffn(rms_norm(xl, norm_g[layer, 1]) * (1 + sc2) + sh2,
                                ffn_w_up[layer], ffn_conv[layer], ffn_w_down[layer])
        if not last:
            xc = xc + cg1 * yc
            xc = xc + cg2 * conv_ffn(rms_norm(xc, norm_g[layer, 1]) * (1 + csc2) + csh2,
                                     ffn_w_up[layer], ffn_conv[layer], ffn_w_down[layer])
    return xl


_drawn_inputs = setup_inputs


def setup_inputs(seed=0):
    import zlib

    import numpy as np

    out = dict(_drawn_inputs(seed))
    spreads = {}
    factors = {'odd_q_g': 8.0, 'odd_k_g': 8.0, 'odd_sink': 8.0}
    for name, (base, spread) in spreads.items():
        noise = np.random.default_rng([zlib.crc32(name.encode()), seed]).standard_normal(out[name].shape)
        drawn = base * np.exp(spread * noise) if base else spread * noise
        out[name] = __import__('jax').numpy.asarray(drawn.astype(out[name].dtype))
    for name, factor in factors.items():
        out[name] = (out[name] * factor).astype(out[name].dtype)
    return out
```

```python
import math
from contextlib import ExitStack

import numpy as np
import concourse.bass as bass
from concourse import mybir

F32 = mybir.dt.float32
F32R = mybir.dt.float32r
ALU = mybir.AluOpType
ACT = mybir.ActivationFunctionType
AX = mybir.AxisListType

P = 128
DM, KT = 1024, 8
SEQ, CTX = 1024, 256
TOK = SEQ + CTX
NT = TOK // P
BLOCKS = [(0, 512, 0), (512, 512, 0), (1024, 256, 1)]
DFF, FT = 2816, 22
EPS = 1e-6
ADA = 48
SH1, SC1, G1, SH2, SC2, G2 = (8 * i for i in range(6))


def program(nc, a):
    es = ExitStack()
    with es:
        def sb(name, shape, dt=F32, stack=None):
            return (stack or es).enter_context(nc.sbuf_tensor(name, shape, dt))

        def sem(name):
            return es.enter_context(nc.semaphore(name))

        cols = sb("cols", [P, 288])
        ident = sb("ident", [P, P])
        ones = sb("ones", [P, P])
        eps_t = sb("eps_t", [P, 1])
        cT = sb("cT", [P, KT, 32])
        pick = sb("pick", [P, 2])
        mod = sb("mod", [P, 2 * ADA, 2])
        gsc = sb("gsc", [P, 4, 2, KT])
        ada_sb = sb("ada_sb", [P, 2, P])
        gcol = sb("gcol", [P, 30, 8])
        dec_bc = sb("dec_bc", [P, 4, 10])
        m_rows = sb("m_rows", [64, 3, 10])
        sink = sb("sink", [P, 8])
        head_g = sb("head_g", [P, 2])
        gate_b = sb("gate_b", [P, 1])
        st8 = sb("st8", [P, 8, 6])
        tick = sb("tick", [P, 8])
        den = sb("den", [P, 2, 4, 2])
        w_hi = sb("w_hi", [P, 2, KT, P], F32R)
        w_lo = sb("w_lo", [P, 2, KT, P], F32R)
        stage = sb("stage", [P, 2, KT * P])
        xbase = ExitStack()
        X = sb("X", [P, KT, TOK], F32, xbase)
        ada_st = sb("ada_st", [P, 2, KT, P], F32, xbase)

        with ExitStack() as s0:
            x_in = sb("x_in", [P, NT, DM], F32, s0)
            rows = sb("rows", [P, 3, P], F32, s0)
        s1 = ExitStack()
        h_hi = sb("h_hi", [P, KT, TOK], F32R, s1)
        h_lo = sb("h_lo", [P, KT, TOK], F32R, s1)
        with ExitStack() as s2:
            sq = sb("sq", [P, 2, 512], F32, s2)
            ssum = sb("ssum", [P, 512], F32, s2)
            root = sb("root", [P, 512], F32, s2)
            rinv = sb("rinv", [P, 512], F32, s2)
            xn = sb("xn", [P, 2, 512], F32, s2)
        with ExitStack() as s2:
            Y = sb("Y", [P, KT, TOK], F32, s2)
            gpad = sb("gpad", [P, TOK + 3], F32, s2)
        with ExitStack() as s2:
            d_hi = sb("d_hi", [P, 2, DM], F32R, s2)
            d_lo = sb("d_lo", [P, 2, DM], F32R, s2)
            a_hi = sb("a_hi", [P, 2, TOK], F32R, s2)
            a_lo = sb("a_lo", [P, 2, TOK], F32R, s2)
            fpad = sb("fpad", [P, TOK + 3], F32, s2)
            fcv = sb("fcv", [P, TOK + 1], F32, s2)
        s1.close()
        with ExitStack() as s2:
            out_tm = sb("out_tm", [P, 8, DM], F32, s2)
        xbase.close()
        so = ExitStack()
        with so:
            qA = sb("qA", [P, 4, SEQ], F32, so)
            kM = sb("kM", [P, 2, TOK], F32, so)
            vMt = sb("vMt", [P, NT, 4, 129], F32, so)
            sb("fill0", [P, 12288 - 4096 - 2560 - 5160], F32, so)
            with ExitStack() as s2:
                sb("fill1", [P, 2 * KT * TOK], F32, s2)
                qM = sb("qM", [P, 2, SEQ], F32, s2)
                oM = sb("oM", [P, 4, SEQ], F32, s2)
                with ExitStack() as s3:
                    kA = sb("kA", [P, TOK], F32, s3)
                    vAt = sb("vAt", [P, 12, P], F32, s3)
                    G = sb("G", [P, TOK], F32, s3)
                    vtmp = sb("vtmp", [P, TOK], F32, s3)
                with ExitStack() as s3:
                    gw = sb("gw", [P, KT, P], F32, s3)
                with ExitStack() as s3:
                    k_s = sb("k_s", [P, 640], F32, s3)
                    v_s = sb("v_s", [P, 5, P], F32, s3)
                    sb("fill2", [P, 1536 + 1280], F32, s3)
                    q_s = sb("q_s", [P, 4, P], F32, s3)
                with ExitStack() as s3:
                    C = sb("C", [P, 4, 129], F32, s3)
                    sel = sb("sel", [64, 12, P], F32, s3)
                    mm_mask = sb("mm_mask", [P, 2, P], F32, s3)
                    sb("fill3", [P, 2816 - 516 - 1536 - 256], F32, s3)
                    XE = sb("XE", [P, 2, 4, P], F32, s3)
                    WT = sb("WT", [P, 2, 4, P], F32, s3)
                    qt = sb("qt", [P, 2, 2, P], F32, s3)
                    wv = sb("wv", [P, 2, 4, 129], F32, s3)
            sb("fill4", [P, 4 * TOK], F32, so)
            with ExitStack() as s2:
                rtab = sb("rtab", [P, 2304], F32, s2)
                kP = sb("kP", [P, 1536], F32, s2)
                pr = sb("pr", [P, 2, 640], F32, s2)
                sb("fill5", [P, 4 * TOK], F32, s2)
                with ExitStack() as s3:
                    rt = [sb(f"rt{n}", [P, 512], F32, s3) for n in range(5)]
                with ExitStack() as s3:
                    pT = sb("pT", [P, 2, 5, 256], F32, s3)
                    amask = sb("amask", [P, 3, 640], F32, s3)
            with ExitStack() as s2:
                R_rst = sb("R_rst", [P, TOK], F32, s2)
                R_fl = sb("R_fl", [P, TOK], F32, s2)
                R_b = sb("R_b", [P, TOK], F32, s2)
                R_del = sb("R_del", [P, TOK], F32, s2)
                sb("fill6", [P, 4 * TOK], F32, s2)
                R_a = sb("R_a", [P, TOK], F32, s2)
                R_m = sb("R_m", [P, TOK], F32, s2)
                kMt = sb("kMt", [P, NT, 256], F32, s2)
        hsum = qA[:, :, :].rearrange("p a b -> p (a b)").rearrange("p (c v) -> p c v", c=8)
        COS, SIN = rtab[:, 0:1024], rtab[:, 1024:2048]
        ROT, BD = rtab[:, 2048:2176], rtab[:, 2176:2304]
        PS = es.enter_context(nc.psum_tensor("PS", [P, 8, 512], F32))

        xf = X[:, :, :].rearrange("p k t -> p (k t)")
        at = 0

        def cut(n):
            nonlocal at
            at += n
            return xf[:, at - n:at]
        CC, CS = cut(P), cut(P)
        CL = cut(4 * 512).rearrange("p (j k) -> p j k", j=4)
        SL = cut(4 * 512).rearrange("p (j k) -> p j k", j=4)
        CX, SX, ALT = cut(P), cut(P), cut(2)
        n_tab = at
        U, FE, FO = cut(TOK), cut(648), cut(640)
        conv_e = xf[:, at - 1288:at]
        TA = cut(5 * P).rearrange("p (j c) -> p j c", j=5)
        TB = cut(5 * P).rearrange("p (j c) -> p j c", j=5)
        TT, QS = cut(P), cut(640)
        TAIL = cut(642)
        xs = nc.dram_tensor("x_spill", [P, KT, TOK], F32).ap()

        s_in = [sem(f"x_loaded{t}") for t in range(NT)]
        s_rows = sem("rows_loaded")
        s_const = sem("constants_written")
        s_rowT = sem("rows_transposed")
        s_cols = sem("cols_copied")
        s_ct = sem("silu_c_written")
        s_xT = sem("x_transposed")
        s_xcA = sem("x_copied_scalar")
        s_xcV = sem("x_copied_vector")
        s_stage = [sem("stage_loaded0"), sem("stage_loaded1")]
        s_hi = sem("weights_hi")
        s_lo = sem("weights_lo")
        s_al = [sem("ada_loaded0"), sem("ada_loaded1")]
        s_amm = sem("ada_partials")
        s_aev = sem("ada_partials_copied")
        s_asel = sem("ada_summed")
        s_mod = sem("mod_written")
        s_sq = sem("norm_squares")
        s_sqa = sem("norm_square_added")
        s_nmm = sem("norm_sum_broadcast")
        s_root = sem("norm_root")
        s_rinv = sem("norm_root_inverted")
        s_xn = sem("norm_scaled")
        s_hhi = sem("h_hi_written")
        s_hlo = sem("h_lo_written")
        s_spill = sem("x_spilled")
        s_back = sem("x_reloaded")
        s_tab = sem("dft_tables_loaded")
        s_proj = sem("proj_psum_ready")
        s_pevA = sem("proj_psum_read_scalar")
        s_pevV = sem("proj_psum_read_vector")
        s_fold = sem("fourier_folded")
        s_ch = sem("channel_dft_ready")
        s_chA = sem("channel_dft_copied")
        s_ld = sem("seq_dft_ready")
        s_qs = sem("seq_dft_sine_copied")
        s_fy = sem("fourier_written")
        s_mhi = sem("mix_hi")
        s_mlo = sem("mix_lo")
        s_res = sem("residual_added")
        s_v = sem("vector_chain")
        s_out = sem("out_stored")
        s_fg = sem("ffn_gate_copied")
        s_fc = sem("ffn_conv_done")
        s_fs = sem("ffn_silu_done")
        s_fp = sem("ffn_product")
        s_ahi = sem("ffn_act_hi")
        s_alo = sem("ffn_act_lo")
        s_down = sem("down_psum_ready")

        def cols_of(w, c):
            return w[:, c * P:(c + 1) * P].rearrange("(k p) c -> p k c", p=P)

        even_tiles = [12, 13, 14, 15]
        for j in range(4):
            even_tiles += [4 + j, 8 + j, j]
        NEV = len(even_tiles)
        J_OUT0, J_FFN0 = NEV, NEV + KT
        PAIRS = FT // 2
        FY = 6
        st3 = [stage[:, s, :].rearrange("p (k c) -> p k c", k=KT) for s in range(2)]
        RES_OUT0 = 3 * KT
        RES_FFN0 = RES_OUT0 + PAIRS * KT * 3

        class Ffn:
            def __init__(s, layer, job, blocks, proj, res, down, tiles, ws):
                s.layer, s.job, s.blocks, s.nb = layer, job, blocks, len(blocks)
                s.proj, s.res, s.down = proj, res, down
                s.tiles = tiles
                s.ws = ws
                s.sp = job % 2
        F0 = Ffn(0, J_FFN0, BLOCKS, 3 * J_FFN0, RES_OUT0, 0, (0, 0), J_FFN0 % 2)


        block = es.enter_context(nc.Block())

        def load_job(sp, j, src):
            if j >= 2:
                sp.wait_ge(s_lo, j - 1)
            sp.dma_start(st3[j % 2], src).then_inc(s_stage[j % 2], 16)

        def ffn_loads(sp, F):
            up, down = a["ffn_w_up"][F.layer], a["ffn_w_down"][F.layer]

            def up_view(c):
                return up[:, bass.ds(c, P)].rearrange("(k p) c -> p k c", p=P)

            def one(j, n, dst, view):
                sp.wait_ge(s_lo, j - 1)
                slot = (F.sp + n) % 2
                sp.dma_start(dst[slot], view).then_inc(s_stage[slot], 16)
            one(F.job, 0, st3, up_view(0))
            st2 = [stage[:, s, :] for s in range(2)]
            with sp.Fori(0, PAIRS) as i:
                j = i * 6 + (F.job + 1)
                one(j, 1, st3, up_view(i * 256 + DFF))
                one(j + 1, 2, st3, up_view(i * 256 + P))
                one(j + 2, 3, st3, up_view(i * 256 + (DFF + P)))
                one(j + 3, 4, st2, down[bass.ds(i * 256, P), :])
                one(j + 4, 5, st2, down[bass.ds(i * 256 + P, P), :])
                one(j + 5, 6, st3, up_view(i * 256 + 256))

        CONST = 10

        def block_mm(pe, blk, bank, wslot):
            c0, w, _ = blk
            for k in range(KT):
                for q, (wt, ht) in enumerate(((w_hi, h_hi), (w_hi, h_lo), (w_lo, h_hi))):
                    last = nc.tensor.matmul(PS[:, bank, 0:w], wt[:, wslot, k, :], ht[:, k, c0:c0 + w],
                                            start=(k == 0 and q == 0), stop=(k == KT - 1 and q == 2))
            last.then_inc(s_proj, 1)

        def ada_step(pe, j, loaded, slot, sum_last=True):
            pe.wait_ge(s_al[slot], loaded)
            if not (isinstance(j, int) and j < 2):
                pe.wait_ge(s_mod, j - 1)
            for k in range(KT):
                q = k % 4
                last = nc.tensor.matmul(PS[32 * q:32 * q + 32, 6 + slot, 0:P], cT[:, k, :], ada_st[:, slot, k, :],
                                        start=(k < 4), stop=(k >= 4), tile_position=(0, 32 * q))
            last.then_inc(s_amm, 1)
            if sum_last:
                ada_sum(pe, j - 1, 1 - slot)

        def ada_at(pe, j, sum_last=True):
            ada_step(pe, j, 16 * (j // 2 + 1), j % 2, sum_last)

        def ada_sum(pe, j, slot):
            pe.wait_ge(s_aev, j + 1)
            nc.tensor.matmul(PS[:, 6 + slot, P:P + 2], ada_sb[:, slot, :], pick[:, :],
                             start=True, stop=True).then_inc(s_asel, 1)

        def norm_pe(pe, q, mods):
            nb = NORM_NB[q]
            for n in range(nb):
                w = BLOCKS[n][1]
                pe.wait_ge(s_sqa, (NORM_AT[q] + n + 1) * KT)
                if n == 0:
                    pe.wait_ge(s_mod, mods)
                if NORM_AT[q] + n:
                    pe.wait_ge(s_root, NORM_AT[q] + n)
                nc.tensor.matmul(PS[:, 7, 0:w], ones[:, :], ssum[:, 0:w], start=True, stop=True).then_inc(s_nmm, 1)
        NORM_NB = (3, 3, 3, 2)
        NORM_AT = (0, 3, 6, 9)

        def fourier_pe(pe, g):
            if g == 0:
                pe.wait_ge(s_tab, 32)
                pe.wait_ge(s_root, 3)
            pe.wait_ge(s_fold, g + 1)
            if g >= 1:
                pe.wait_ge(s_fy, FY * g)
                pe.wait_ge(s_qs, 2 * g)
            for half, (src, tab) in enumerate(((FE, CC), (FO, CS))):
                if half:
                    pe.wait_ge(s_chA, 5 * g + 3)
                for j in range(5):
                    c0 = j * P if j < 4 else (516 if half == 0 else 512)
                    dst = PS[:, 6, j * P:(j + 1) * P] if j < 4 else PS[:, 7, 0:P]
                    last = nc.tensor.matmul(dst, src[:, c0:c0 + P], tab, start=True, stop=True)
                if half == 0:
                    last = nc.tensor.matmul(PS[0:2, 7, P:2 * P], FE[:, 512:645:132], CC, start=True, stop=True)
                last.then_inc(s_ch, 1)
            pe.wait_ge(s_chA, 5 * g + 5)
            for j in range(4):
                nc.tensor.matmul(PS[:, 6, :], TA[:, j, :], CL[:, j, :], start=(j == 0), stop=False)
            nc.tensor.matmul(PS[:, 6, :], TT[0:2, :], TAIL[0:2, 0:512], start=False, stop=True)
            for j in range(4):
                last = nc.tensor.matmul(PS[:, 7, :], TB[:, j, :], SL[:, j, :], start=(j == 0), stop=(j == 3))
            last.then_inc(s_ld, 1)
            pe.wait_ge(s_fy, FY * g + 2)
            pe.wait_ge(s_qs, 2 * g + 1)
            nc.tensor.matmul(PS[:, 6, 0:P], TA[:, 4, :], CX, start=True, stop=False)
            nc.tensor.matmul(PS[:, 6, 0:P], TT[0:2, :], TAIL[0:2, 512:640], start=False, stop=True)
            for j in range(4):
                nc.tensor.matmul(PS[:, 6, P:P + 1], TA[:, j, :], ALT[:, 0:1], start=(j == 0), stop=False)
            nc.tensor.matmul(PS[:, 6, P:P + 1], TT[0:2, :], TAIL[0:2, 640:641], start=False, stop=True)
            nc.tensor.matmul(PS[:, 6, P + 1:P + 2], TA[:, 4, :], ALT[:, 1:2], start=True, stop=False)
            nc.tensor.matmul(PS[:, 6, P + 1:P + 2], TT[0:2, :], TAIL[0:2, 641:642], start=False, stop=True)
            nc.tensor.matmul(PS[:, 7, 0:P], TB[:, 4, :], SX, start=True, stop=True).then_inc(s_ld, 1)

        def ffn_pe(pe, F, h_from, ada_from=None):
            nb = F.nb

            def tile(job, wslot, bank0, free, hready=False):
                pe.wait_ge(s_lo, job + 1)
                for n in range(nb):
                    if free is not None:
                        pe.wait_ge(free[0], free[1] + (n + 1))
                    if hready:
                        pe.wait_ge(s_hlo, (NORM_AT[2 * F.layer + 1] + n + 1) * KT)
                    block_mm(pe, F.blocks[n], bank0 + n, wslot)

            def down(i):
                pe.wait_ge(s_lo, i * 6 + F.job)
                pe.wait_ge(s_alo, i * (2 * nb) + F.tiles[1])
                for o in range(KT):
                    for n in range(nb):
                        c = o * nb + n
                        c0, w, _ = F.blocks[n]
                        pe.wait_ge(s_res, i * (KT * nb) + (F.res - KT * nb + c - 1))
                        mm = 0
                        for f in range(2):
                            for wt, at_ in ((d_hi, a_hi), (d_hi, a_lo), (d_lo, a_hi)):
                                last = nc.tensor.matmul(PS[:, 6 + c % 2, 0:w], wt[:, f, o * P:(o + 1) * P],
                                                        at_[:, f, c0:c0 + w], start=(mm == 0), stop=(mm == 5))
                                mm += 1
                        last.then_inc(s_down, 1)

            def pair(i, first):
                j = i * 6 + F.job
                t = i * (2 * nb)
                tile(j, F.ws, 0, None if first else (s_fg, t + F.tiles[0] - nb), hready=first)
                if not first:
                    down(i)
                if ada_from is not None:
                    pe.wait_ge(s_res, i * (KT * nb) + F.res)
                    for m in range(4):
                        ada_step(pe, i * 4 + (ada_from + m), i * 32 + 16 * ((ada_from + m) // 2 + 1), m % 2, m > 0)
                    ada_sum(pe, i * 4 + (ada_from + 3), 1)
                    pe.wait_ge(s_mod, i * 4 + (ada_from + 4))
                tile(j + 1, 1 - F.ws, 3, None if first else (s_fp, t + F.tiles[0] - nb))
                tile(j + 2, F.ws, 0, (s_fg, t + F.tiles[0]))
                tile(j + 3, 1 - F.ws, 3, (s_fp, t + F.tiles[0]))
            pe.wait_ge(s_res, F.res)
            pair(0, True)
            with pe.Fori(1, PAIRS) as i:
                pair(i, False)
            down(PAIRS)
            if ada_from is not None:
                pe.wait_ge(s_res, F.res + PAIRS * KT * nb)
                for m in range(4):
                    ada_at(pe, ada_from + 4 * PAIRS + m, m > 0)
                ada_sum(pe, ada_from + 4 * PAIRS + 3, 1)

        def conv_free(act, jj):
            if jj:
                act.wait_ge(s_v, 7 + 3 * jj)

        def hi_job(act, j, dst, used=None, slot=None, count=None):
            slot = j % 2 if slot is None else slot
            act.wait_ge(s_stage[slot], 16 * (j // 2 + 1) if count is None else count)
            if used is not None:
                act.wait_ge(s_proj, used)
            nc.scalar.activation(dst, st3[slot], ACT.Copy).then_inc(s_hi, 1)

        def ada_copy(act, j, slot=None):
            slot = j % 2 if slot is None else slot
            act.wait_ge(s_amm, j + 1)
            if not (isinstance(j, int) and j < 2):
                act.wait_ge(s_asel, j - 1)
            nc.scalar.activation(ada_sb[:, slot, :], PS[:, 6 + slot, 0:P], ACT.Copy).then_inc(s_aev, 1)

        def norm_act(act, q):
            for n in range(NORM_NB[q]):
                c0, w, v = BLOCKS[n]
                at_ = (NORM_AT[q] + n) * KT
                for k in range(KT):
                    x_ready(act, q, n, k)
                    if at_ + k >= 2:
                        act.wait_ge(s_sqa, at_ + k - 1)
                    nc.scalar.activation(sq[:, k % 2, 0:w], X[:, k, c0:c0 + w], ACT.Square).then_inc(s_sq, 1)
                act.wait_ge(s_nmm, NORM_AT[q] + n + 1)
                if NORM_AT[q] + n:
                    act.wait_ge(s_rinv, NORM_AT[q] + n)
                nc.scalar.activation(root[:, 0:w], PS[:, 7, 0:w], ACT.Sqrt, bias=eps_t[:, 0:1],
                                     scale=1.0 / DM).then_inc(s_root, 1)
                for k in range(KT):
                    act.wait_ge(s_xn, at_ + k + 1)
                    nc.scalar.activation(h_hi[:, k, c0:c0 + w], xn[:, k % 2, 0:w], ACT.Identity,
                                         bias=shift_of(q, k, v)).then_inc(s_hhi, 1)

        def x_ready(eng, q, n, k):
            if q == 0:
                if k == 0 and n == 0:
                    eng.wait_ge(s_xcA, 10)
                    eng.wait_ge(s_xcV, 10)
            elif q == 1:
                eng.wait_ge(s_res, 3 * k + n + 1)
            elif q == 2:
                eng.wait_ge(s_res, RES_FFN0 - 3 * KT + 3 * k + n + 1)
            else:
                eng.wait_ge(s_res, RES_FFN0 + 2 * k + n + 1)

        def shift_of(q, k, v):
            m = (q // 2) * ADA + (SH1, SH2)[q % 2] + k
            return mod[:, m, v:v + 1]

        def fourier_act(act, g):
            act.wait_ge(s_ch, 2 * g + 1)
            if g:
                act.wait_ge(s_ld, 2 * g)
            nc.scalar.activation(TA[:, 0:4, :], PS[:, 6, :].rearrange("p (j c) -> p j c", j=4), ACT.Copy).then_inc(s_chA, 1)
            nc.scalar.activation(TA[:, 4, :], PS[:, 7, 0:P], ACT.Copy).then_inc(s_chA, 1)
            nc.scalar.activation(TT[0:2, :], PS[0:2, 7, P:2 * P], ACT.Copy).then_inc(s_chA, 1)
            act.wait_ge(s_ch, 2 * g + 2)
            nc.scalar.activation(TB[:, 0:4, :], PS[:, 6, :].rearrange("p (j c) -> p j c", j=4), ACT.Copy).then_inc(s_chA, 1)
            nc.scalar.activation(TB[:, 4, :], PS[:, 7, 0:P], ACT.Copy).then_inc(s_chA, 1)
            act.wait_ge(s_ld, 2 * g + 1)
            if g:
                act.wait_ge(s_fy, FY * g)
            nc.scalar.activation(QS[:, 0:512], PS[:, 7, :], ACT.Copy).then_inc(s_qs, 1)
            act.wait_ge(s_ld, 2 * g + 2)
            nc.scalar.activation(QS[:, 512:640], PS[:, 7, 0:P], ACT.Copy).then_inc(s_qs, 1)

        def mix_hi(act, proj):
            for n, (c0, w, _) in enumerate(BLOCKS):
                for k in range(KT):
                    if n == 0 and k == 0:
                        act.wait_ge(s_proj, proj)
                        act.wait_ge(s_fy, 4 * FY)
                        act.wait_ge(s_pevV, 24)
                    nc.scalar.activation(h_hi[:, k, c0:c0 + w], Y[:, k, c0:c0 + w], ACT.Copy).then_inc(s_mhi, 1)

        def ffn_act(act, F, ada_from=None):
            nb = F.nb
            d_hi_slots = [d_hi[:, s, :] for s in range(2)]

            def hi(i, n, wslot, used):
                jn = F.sp + 1 + n
                slot = jn % 2
                before = (F.job + 1 + n) // 2 + 1
                act.wait_ge(s_stage[slot], i * 48 + 16 * before)
                if used is not None:
                    act.wait_ge(*used)
                if wslot is None:
                    nc.scalar.activation(d_hi_slots[n - 3], stage[:, slot, :], ACT.Copy).then_inc(s_hi, 1)
                else:
                    nc.scalar.activation(w_hi[:, wslot, :, :], st3[slot], ACT.Copy).then_inc(s_hi, 1)

            def gate(i, half):
                if not (isinstance(i, int) and i * 2 + F.fc0 + half == 0):
                    act.wait_ge(s_fc, i * 2 + (F.fc0 + half))
                for n in range(nb):
                    c0, w, _ = F.blocks[n]
                    act.wait_ge(s_proj, i * (4 * nb) + (F.proj + 2 * nb * half + n + 1))
                    g0 = c0 + 1 if n < 2 else c0 + 2
                    nc.scalar.activation(fpad[:, g0:g0 + w], PS[:, n, 0:w], ACT.Copy).then_inc(s_fg, 1)

            def silu(i, half):
                act.wait_ge(s_fc, i * 2 + (F.fc0 + half + 1))
                nc.scalar.activation(fcv[:, 0:F.cw], fcv[:, 0:F.cw], ACT.Silu).then_inc(s_fs, 1)

            def a_half(i, half, first=False):
                if not first:
                    act.wait_ge(s_down, i * (KT * nb) + F.down)
                for n in range(nb):
                    c0, w, _ = F.blocks[n]
                    s0 = c0 if n < 2 else c0 + 1
                    act.wait_ge(s_fp, i * (2 * nb) + (F.tiles[0] + nb * half + n + 1))
                    nc.scalar.activation(a_hi[:, half, c0:c0 + w], fcv[:, s0:s0 + w], ACT.Copy).then_inc(s_ahi, 1)

            def pair(i, first):
                pb = F.proj
                hi(i, 0, 1 - F.ws, (s_proj, i * (4 * nb) + pb))
                if not first:
                    a_half(i - 1, 1, first=True)
                gate(i, 0)
                silu(i, 0)
                hi(i, 1, F.ws, (s_proj, i * (4 * nb) + (pb + nb)))
                if ada_from is not None:
                    for m in range(4):
                        ada_copy(act, i * 4 + (ada_from + m), (ada_from + m) % 2)
                a_half(i, 0, first=first)
                hi(i, 2, 1 - F.ws, (s_proj, i * (4 * nb) + (pb + 2 * nb)))
                hi(i, 3, None, None if first else (s_down, i * (KT * nb) + F.down))
                hi(i, 4, None, None)
                gate(i, 1)
                silu(i, 1)
                hi(i, 5, F.ws, (s_proj, i * (4 * nb) + (pb + 3 * nb)))
            act.wait_ge(s_hlo, (NORM_AT[2 * F.layer + 1] + nb) * KT)
            pair(0, True)
            with act.Fori(1, PAIRS) as i:
                pair(i, False)
            a_half(PAIRS - 1, 1, first=True)
            if ada_from is not None:
                for m in range(4):
                    ada_copy(act, ada_from + 4 * PAIRS + m)
        F0.fc0, F0.cw = 0, TOK + 1

        vn = [0]

        def chain(dve, ins):
            vn[0] += 1
            ins.then_inc(s_v, 1)
            dve.wait_ge(s_v, vn[0])

        def lo_job(dve, j, wslot):
            dve.wait_ge(s_hi, j + 1)
            nc.vector.tensor_tensor(w_lo[:, wslot, :, :], st3[j % 2], w_hi[:, wslot, :, :].bitcast(F32),
                                    ALU.subtract).then_inc(s_lo, 1)

        def ada_write(dve, j, slot=None, m=None):
            slot = j % 2 if slot is None else slot
            dve.wait_ge(s_asel, j + 1)
            if isinstance(j, int):
                dst, b = mod[:, j, :], cols[:, j:j + 1]
            else:
                dst, b = mod[:, bass.ds(j, 1), :], cols[:, bass.ds(j, 1)]
            if isinstance(j, int):
                nc.vector.tensor_scalar(dst, PS[:, 6 + slot, P:P + 2], b, None, ALU.add).then_inc(s_mod, 1)
            else:
                nc.vector.tensor_tensor(mod[:, bass.ds(j, 1), :].rearrange("p a v -> p (a v)"), PS[:, 6 + slot, P:P + 2],
                                        cols[:, bass.ds(j, 1)].broadcast_to((P, 2)), ALU.add).then_inc(s_mod, 1)

        def norm_vec(dve, q):
            sc = (q // 2) * ADA + (SC1, SC2)[q % 2]
            dve.wait_ge(s_mod, sc + KT)
            for v in range(2):
                chain(dve, nc.vector.scalar_tensor_tensor(gsc[:, q, v, :], mod[:, sc:sc + KT, v], 1.0,
                                                          cols[:, 96 + q * KT:96 + (q + 1) * KT], ALU.add, ALU.mult))
            for n in range(NORM_NB[q]):
                c0, w, v = BLOCKS[n]
                at_ = (NORM_AT[q] + n) * KT
                for k in range(KT):
                    dve.wait_ge(s_sq, at_ + k + 1)
                    if k == 0:
                        if NORM_AT[q] + n:
                            dve.wait_ge(s_nmm, NORM_AT[q] + n)
                        nc.vector.tensor_copy(ssum[:, 0:w], sq[:, 0, 0:w]).then_inc(s_sqa, 1)
                    else:
                        dve.wait_ge(s_sqa, at_ + k)
                        nc.vector.tensor_tensor(ssum[:, 0:w], ssum[:, 0:w], sq[:, k % 2, 0:w], ALU.add).then_inc(s_sqa, 1)
                dve.wait_ge(s_root, NORM_AT[q] + n + 1)
                nc.vector.reciprocal(rinv[:, 0:w], root[:, 0:w]).then_inc(s_rinv, 1)
                dve.wait_ge(s_rinv, NORM_AT[q] + n + 1)
                for k in range(KT + 1):
                    if k < KT:
                        if at_ + k >= 2:
                            dve.wait_ge(s_hlo, at_ + k - 1)
                        nc.vector.scalar_tensor_tensor(xn[:, k % 2, 0:w], X[:, k, c0:c0 + w], gsc[:, q, v, k:k + 1],
                                                       rinv[:, 0:w], ALU.mult, ALU.mult).then_inc(s_xn, 1)
                    if k:
                        kk = k - 1
                        dve.wait_ge(s_hhi, at_ + k)
                        nc.vector.scalar_tensor_tensor(h_lo[:, kk, c0:c0 + w], xn[:, kk % 2, 0:w], shift_of(q, kk, v),
                                                       h_hi[:, kk, c0:c0 + w].bitcast(F32), ALU.add, ALU.subtract).then_inc(s_hlo, 1)

        def fold(dve, u, e, o, half, last=False):
            nc.vector.tensor_copy(e[:, 0:half + 1:half], u[:, 0:half + 1:half])
            nc.vector.tensor_tensor(e[:, 1:half], u[:, 1:half], u[:, 2 * half - 1:half:-1], ALU.add)
            ins = nc.vector.tensor_tensor(o[:, 1:half], u[:, 1:half], u[:, 2 * half - 1:half:-1], ALU.subtract)
            if last:
                ins.then_inc(s_fold, 1)

        def conv3(dve, out, src, tap, width):
            chain(dve, nc.vector.tensor_scalar(out[:, 0:width], src[:, 0:width], tap(0), None, ALU.mult))
            chain(dve, nc.vector.scalar_tensor_tensor(out[:, 0:width], src[:, 1:1 + width], tap(1), out[:, 0:width],
                                                      ALU.mult, ALU.add))
            chain(dve, nc.vector.scalar_tensor_tensor(out[:, 0:width], src[:, 2:2 + width], tap(2), out[:, 0:width],
                                                      ALU.mult, ALU.add))

        def fourier_vec(dve, g):
            y = Y[:, 4 + g, :]
            dve.wait_ge(s_ld, 2 * g + 1)
            dve.wait_ge(s_qs, 2 * g + 1)
            nc.vector.tensor_tensor(y[:, 0:512], PS[:, 6, 0:512], QS[:, 0:512], ALU.subtract).then_inc(s_fy, 1)
            nc.vector.tensor_tensor(y[:, 1023:512:-1], PS[:, 6, 1:512], QS[:, 1:512], ALU.add).then_inc(s_fy, 1)
            dve.wait_ge(s_ld, 2 * g + 2)
            dve.wait_ge(s_qs, 2 * g + 2)
            nc.vector.tensor_tensor(y[:, 1024:1152], PS[:, 6, 0:P], QS[:, 512:640], ALU.subtract).then_inc(s_fy, 1)
            nc.vector.tensor_tensor(y[:, 1279:1152:-1], PS[:, 6, 1:P], QS[:, 513:640], ALU.add).then_inc(s_fy, 1)
            nc.vector.tensor_copy(y[:, 512:513], PS[:, 6, P:P + 1]).then_inc(s_fy, 1)
            nc.vector.tensor_copy(y[:, 1152:1153], PS[:, 6, P + 1:P + 2]).then_inc(s_fy, 1)

        def mix_lo(dve):
            for n, (c0, w, _) in enumerate(BLOCKS):
                for k in range(KT):
                    dve.wait_ge(s_mhi, n * KT + k + 1)
                    nc.vector.tensor_tensor(h_lo[:, k, c0:c0 + w], Y[:, k, c0:c0 + w],
                                            h_hi[:, k, c0:c0 + w].bitcast(F32), ALU.subtract).then_inc(s_mlo, 1)

        def add_residual(dve, bank, o, c0, w, gate_):
            nc.vector.scalar_tensor_tensor(X[:, o, c0:c0 + w], PS[:, bank, 0:w], gate_, X[:, o, c0:c0 + w],
                                           ALU.mult, ALU.add).then_inc(s_res, 1)

        def ffn_vec(dve, F, ada_from=None):
            nb = F.nb
            m0 = F.layer * ADA + G2
            taps = P + F.layer * 3 * FT

            def lo(i, n, wslot):
                slot = (F.sp + 1 + n) % 2
                dve.wait_ge(s_hi, i * 6 + (F.job + n + 2))
                if wslot is None:
                    nc.vector.tensor_tensor(d_lo[:, n - 3, :], stage[:, slot, :], d_hi[:, n - 3, :].bitcast(F32),
                                            ALU.subtract).then_inc(s_lo, 1)
                else:
                    nc.vector.tensor_tensor(w_lo[:, wslot, :, :], st3[slot], w_hi[:, wslot, :, :].bitcast(F32),
                                            ALU.subtract).then_inc(s_lo, 1)

            def conv(i, half):
                dve.wait_ge(s_fg, i * (2 * nb) + (F.tiles[0] + nb * (half + 1)))
                if not (isinstance(i, int) and i == half == F.tiles[1] == 0):
                    dve.wait_ge(s_alo, i * (2 * nb) + (F.tiles[1] + nb * half))
                f = i * 2 + half
                for t_ in range(3):
                    tap = cols[:, bass.ds(f + (taps + FT * t_), 1)]
                    src = fpad[:, t_:t_ + F.cw]
                    if t_ == 0:
                        ins = nc.vector.tensor_scalar(fcv[:, 0:F.cw], src, tap, None, ALU.mult)
                    else:
                        ins = nc.vector.scalar_tensor_tensor(fcv[:, 0:F.cw], src, tap, fcv[:, 0:F.cw], ALU.mult, ALU.add)
                    if t_ < 2:
                        ins.then_inc(s_v, 1)
                        dve.wait_ge(s_v, i * 4 + (F.v0 + 2 * half + t_ + 1))
                    else:
                        ins.then_inc(s_fc, 1)

            def product(i, half):
                dve.wait_ge(s_fs, i * 2 + (F.fc0 + half + 1))
                for n in range(nb):
                    c0, w, _ = F.blocks[n]
                    s0 = c0 if n < 2 else c0 + 1
                    dve.wait_ge(s_proj, i * (4 * nb) + (F.proj + nb * (2 * half + 1) + n + 1))
                    nc.vector.tensor_tensor(fcv[:, s0:s0 + w], fcv[:, s0:s0 + w], PS[:, 3 + n, 0:w],
                                            ALU.mult).then_inc(s_fp, 1)
                for n in range(nb):
                    c0, w, _ = F.blocks[n]
                    s0 = c0 if n < 2 else c0 + 1
                    dve.wait_ge(s_ahi, i * (2 * nb) + (F.tiles[0] + nb * half + n + 1))
                    nc.vector.tensor_tensor(a_lo[:, half, c0:c0 + w], fcv[:, s0:s0 + w],
                                            a_hi[:, half, c0:c0 + w].bitcast(F32), ALU.subtract).then_inc(s_alo, 1)

            def down(i):
                for o in range(KT):
                    for n, (c0, w, v) in enumerate(F.blocks):
                        c = o * nb + n
                        dve.wait_ge(s_down, i * (KT * nb) + (F.down - KT * nb + c + 1))
                        add_residual(dve, 6 + c % 2, o, c0, w, mod[:, m0 + o, v:v + 1])

            def pair(i, first):
                lo(i, 0, 1 - F.ws)
                if not first:
                    product(i - 1, 1)
                conv(i, 0)
                if not first:
                    down(i)
                lo(i, 1, F.ws)
                if ada_from is not None:
                    for m in range(4):
                        ada_write(dve, i * 4 + (ada_from + m), (ada_from + m) % 2)
                product(i, 0)
                lo(i, 2, 1 - F.ws)
                lo(i, 3, None)
                lo(i, 4, None)
                conv(i, 1)
                lo(i, 5, F.ws)
            for c_ in (0, 1025, TOK + 2):
                chain(dve, nc.vector.memset(fpad[:, c_:c_ + 1], 0.0))
            F.v0 = vn[0]
            pair(0, True)
            with dve.Fori(1, PAIRS) as i:
                pair(i, False)
            vn[0] += 4 * PAIRS
            product(PAIRS - 1, 1)
            down(PAIRS)
            if ada_from is not None:
                for m in range(4):
                    ada_write(dve, ada_from + 4 * PAIRS + m)

        C_QA, C_KA, C_VA, C_QM, C_KM, C_VM, C_OM, C_G = 0, 512, 640, 768, 1024, 1280, 1792, 2304
        odd_tiles = ([("g", 0), ("ka", 0), ("va", 0)] + [("qa", j) for j in range(4)] + [("km", j) for j in range(2)]
                     + [("vm", j) for j in range(4)] + [("qm", j) for j in range(2)] + [("om", j) for j in range(4)])
        odd_nb = [2 if t in ("qa", "qm", "om") else 3 for t, _ in odd_tiles]
        odd_cum = [0]
        for n_ in odd_nb:
            odd_cum.append(odd_cum[-1] + n_)
        NODD = len(odd_tiles)
        J_ODD = J_FFN0 + 6 * PAIRS + 1
        J_OUT1 = J_ODD + NODD - 1
        J_FFN1 = J_OUT1 + KT
        PR_ODD = 3 * J_FFN0 + 12 * PAIRS
        PR_OUT1 = PR_ODD + odd_cum[-1]
        PR_FFN1 = PR_OUT1 + 2 * KT
        PEV_ODD = 24
        RES_OUT1 = RES_FFN0 + 2 * KT
        RES_END = RES_OUT1 + PAIRS * KT * 2
        LAT = BLOCKS[:2]
        F1 = Ffn(1, J_FFN1, LAT, PR_FFN1, RES_OUT1, PAIRS * KT * 3, (6 * PAIRS, 6 * PAIRS), 0)
        F1.fc0, F1.cw = 2 * PAIRS, SEQ

        s_gz = sem("gate_weights_zeroed")
        s_gw = sem("gate_weights_loaded")
        s_ghl = sem("gate_weights_hi")
        s_gll = sem("gate_weights_lo")
        s_small = sem("small_columns_loaded")
        s_vt = sem("v_transposed")
        s_vc = sem("v_copied")
        s_rtab = sem("rope_tables_loaded")
        s_ones = sem("pads_written")
        s_rq = sem("rope_square")
        s_rs = sem("rope_sum")
        s_rr = sem("rope_root")
        s_rx = sem("rope_scaled")
        s_ro = sem("rope_rotated")
        s_rd = sem("rope_done")
        s_amk = sem("attention_masks_loaded")
        s_kctx = sem("context_keys_copied")
        s_sl = sem("block_operands_copied")
        s_S = sem("scores_ready")
        s_nm = sem("score_max_ready")
        s_ex = sem("probs_ready")
        s_pn = sem("probs_normalised")
        s_pt = sem("probs_transposed")
        s_pcA = sem("probs_copied_scalar")
        s_pcV = sem("probs_copied_vector")
        s_O = sem("attention_out_ready")
        s_yA = sem("attention_hi")
        s_yV = sem("attention_lo")
        s_att = sem("attention_chain")
        s_tick = sem("attention_scores_waited_for")
        s_rst = sem("row_tables_loaded")
        s_g1 = sem("log_gate_part")
        s_gexp = sem("gate_rows_exponentiated")
        s_gx = sem("gate_exponents_made")
        s_gt = sem("gate_rows_transposed")
        s_gc = sem("gate_columns_copied")
        s_mA = sem("mlstm_scores_ready")
        s_mB = sem("mlstm_exponents_made")
        s_mC = sem("mlstm_exponentiated")
        s_mD = sem("mlstm_weights_made")
        s_mE = sem("mlstm_out_ready")
        s_wv = sem("mlstm_values_weighted")
        s_mF = sem("mlstm_out_read")
        s_fT = sem("mlstm_out_transposed")
        s_fm = sem("mlstm_gated")
        s_fhi = sem("mlstm_mix_hi")
        s_flo = sem("mlstm_mix_lo")
        s_qh = [sem("query_half_loaded0"), sem("query_half_loaded1")]
        s_wo = [sem("out_rows_loaded0"), sem("out_rows_loaded1")]
        s_oT = sem("out_transposed")
        s_ocA = sem("out_copied_scalar")
        s_ocV = sem("out_copied_vector")
        s_act = sem("scalar_chain")
        an = [0]

        def achain(act, ins):
            an[0] += 1
            ins.then_inc(s_act, 1)
            act.wait_ge(s_act, an[0])

        def odd_view(kind, j):
            w = a["odd_w_in"][0]
            c = {"ka": C_KA, "va": C_VA, "qm": C_QM, "km": C_KM, "vm": C_VM, "om": C_OM}[kind] + j * P
            return w[:, c:c + P].rearrange("(k p) c -> p k c", p=P)

        def layer1_loads(sp):
            for n in range(1, NODD):
                j = J_ODD + n - 1
                kind, t = odd_tiles[n]
                sp.wait_ge(s_lo, j - 1)
                if kind == "qa":
                    wq = a["odd_w_in"][0][:, 0:512].rearrange("(k p) c -> p k c", p=P)
                    sp.dma_start(st3[j % 2][:, :, 0:64], wq[:, :, 64 * t:64 * t + 64]).then_inc(s_qh[j % 2], 16)
                    sp.dma_start(st3[j % 2][:, :, 64:128], wq[:, :, 256 + 64 * t:320 + 64 * t]).then_inc(s_stage[j % 2], 16)
                else:
                    sp.dma_start(st3[j % 2], odd_view(kind, t)).then_inc(s_stage[j % 2], 16)
                if n == 2:
                    sp.wait_ge(s_hlo, 9 * KT)
                    sp.dma_start(xs[:, :, 0:SEQ], X[:, :, 0:SEQ]).then_inc(s_spill, 16)
            sp.wait_ge(s_proj, PR_OUT1)
            sp.dma_start(rtab[:, :], a["rope_tables"]).then_inc(s_rtab, 16)
            sp.dma_start(amask[:, :, :], a["att_masks"]).then_inc(s_amk, 16)
            sp.wait_ge(s_yV, 8)
            sp.dma_start(R_rst[0:64, :], a["scan_resets"]).then_inc(s_rst, 16)
            sp.dma_start(sel[:, :, :], a["row_select"]).then_inc(s_rst, 16)
            sp.dma_start(mm_mask[:, :, :], a["mlstm_masks"]).then_inc(s_rst, 16)
            for o in range(KT):
                if o == 2:
                    sp.wait_ge(s_fT, 8)
                    sp.dma_start(X[:, :, 0:SEQ], xs[:, :, 0:SEQ]).then_inc(s_back, 16)
                j = J_OUT1 + o
                w = a["odd_w_out"][0][:, o * P:(o + 1) * P]
                sp.wait_ge(s_lo, j - 1)
                for h in range(2):
                    sp.dma_start(st3[j % 2][64 * h:64 * h + 64, 0:4, :],
                                 w[256 * h:256 * h + 256, :].rearrange("(t d) c -> d t c", t=4)).then_inc(s_wo[j % 2], 16)
                sp.dma_start(st3[j % 2][:, 4:8, :], w[512:1024, :].rearrange("(k p) c -> p k c", p=P)).then_inc(s_stage[j % 2], 16)
            ffn_loads(sp, F1)
            for t in range(8):
                sp.wait_ge(s_ocA, t + 1)
                sp.wait_ge(s_ocV, t + 1)
                sp.dma_start(a["out"][0, t * P:(t + 1) * P, :], out_tm[:, t, :]).then_inc(s_out, 16)
            sp.wait_ge(s_out, 8 * 16)

        def layer1_pool(gp):
            for n, (dst, src) in enumerate((
                    (sink[:, :], a["odd_sink"][0:1, :].broadcast_to((P, 8))),
                    (head_g[0:64, 0:1], a["odd_q_g"].rearrange("a d -> d a")), (head_g[64:128, 0:1], a["odd_q_g"].rearrange("a d -> d a")),
                    (head_g[0:64, 1:2], a["odd_k_g"].rearrange("a d -> d a")), (head_g[64:128, 1:2], a["odd_k_g"].rearrange("a d -> d a")))):
                gp.dma_start(dst, src).then_inc(s_small, 16)
            gp.memset(gate_b[:, :], 0.0).then_inc(s_gz, 1)
            gp.wait_ge(s_down, PAIRS * KT * 3)
            gp.wait_ge(s_res, RES_FFN0)
            gp.memset(gw[:, :, :], 0.0).then_inc(s_gz, 1)
            gp.wait_ge(s_gz, 2)
            for q, row in enumerate((0, 64, 32, 96)):
                gp.dma_start(gw[:, :, row:row + 4],
                             a["odd_w_in"][0][:, C_G + 4 * q:C_G + 4 * q + 4].rearrange("(k p) c -> p k c", p=P)).then_inc(s_gw, 16)
                gp.dma_start(gate_b[row:row + 4, :], a["odd_gate_b"][0, q:q + 1, :].rearrange("a h -> h a")).then_inc(s_gw, 16)
            gp.wait_ge(s_rd, 21)
            gp.tensor_copy(k_s[:, 384:640], kP[:, 1280:1536]).then_inc(s_kctx, 1)
            gp.wait_ge(s_vc, 3)
            gp.tensor_copy(v_s[:, 3:5, :], vAt[:, 10:12, :]).then_inc(s_kctx, 1)

            def block_copies(b, first):
                if not first:
                    gp.wait_ge(s_S, b * 8)
                gp.tensor_copy(q_s[:, :, :], qA[:, :, bass.ds(b * P, P)]).then_inc(s_sl, 1)
                gp.tensor_copy(k_s[:, 0:384], kP[:, bass.ds(b * P, 384)]).then_inc(s_sl, 1)
                if not first:
                    gp.wait_ge(s_O, b * 4)
                gp.tensor_copy(v_s[:, 0:3, :], vAt[:, bass.ds(b, 3), :]).then_inc(s_sl, 1)
            block_copies(0, True)
            with gp.Fori(1, 8) as b:
                block_copies(b, False)

        def layer1_pe(pe):
            norm_pe(pe, 2, 2 * ADA)
            pend = None
            for n, (kind, t) in enumerate(odd_tiles):
                if n == 0:
                    pe.wait_ge(s_gll, 1)
                else:
                    pe.wait_ge(s_lo, J_ODD + n)
                for b in range(odd_nb[n]):
                    if n < 2:
                        pe.wait_ge(*((s_fg, 6 * PAIRS) if n == 0 else (s_fp, 6 * PAIRS)))
                    else:
                        pe.wait_ge(s_pevA, PEV_ODD + odd_cum[n - 2] + min(b + 1, odd_nb[n - 2]))
                    if n == 0:
                        pe.wait_ge(s_hlo, (6 + b + 1) * KT)
                    block_mm(pe, BLOCKS[b], 3 * (n % 2) + b, (n + 1) % 2)
                if pend is not None:
                    v_transposes(pe, *pend)
                pend = (n, V_TILES.index(n)) if n in V_TILES else None
            rope_pe(pe)
            att_pe(pe, 0, True)
            with pe.Fori(1, 8) as i:
                att_pe(pe, i, False)
            mlstm_pe(pe)
            for o in range(KT):
                pe.wait_ge(s_lo, J_OUT1 + o + 1)
                for n in range(2):
                    if o < 2:
                        pe.wait_ge(s_fm, 8)
                        pe.wait_ge(s_mF, MF_END)
                    else:
                        pe.wait_ge(s_res, RES_FFN0 + 2 * (o - 2) + n + 1)
                    if o == 0 and n == 0:
                        pe.wait_ge(s_yV, 8)
                        pe.wait_ge(s_flo, 8)
                    block_mm(pe, LAT[n], 3 * (o % 2) + n, o % 2)
            norm_pe(pe, 3, 2 * ADA)
            ffn_pe(pe, F1, None)
            for t in range(8):
                for half in range(2):
                    g = 2 * t + half
                    if g == 0:
                        pe.wait_ge(s_res, RES_END)
                    if g < 6:
                        pe.wait_ge(s_fp, 6 * PAIRS + 4 * PAIRS)
                    else:
                        pe.wait_ge(s_ocA if g % 2 == 0 else s_ocV, (g - 6) // 2 + 1)
                    for k in range(4):
                        last = nc.tensor.transpose(PS[:, g % 6, k * P:(k + 1) * P], X[:, 4 * half + k, t * P:(t + 1) * P], ident[:, :])
                    last.then_inc(s_oT, 1)

        V_TILES = [n for n, (k, _) in enumerate(odd_tiles) if k in ("va", "vm")]
        V_GROUPS = ((0, 4), (4, 4), (8, 2))

        def v_transposes(pe, n, q):
            pe.wait_ge(s_pevA, PEV_ODD + odd_cum[n + 1])
            for g, (t0, cnt) in enumerate(V_GROUPS):
                u = 3 * q + g
                if u >= 2:
                    pe.wait_ge(s_vc, u - 1)
                else:
                    pe.wait_ge(s_root, 9)
                for t in range(cnt):
                    last = nc.tensor.transpose(PS[:, 6 + u % 2, t * P:(t + 1) * P], vtmp[:, (t0 + t) * P:(t0 + t + 1) * P], ident[:, :])
                last.then_inc(s_vt, 1)

        rope_units = []
        for t in range(4):
            for c0 in (0, 512):
                rope_units.append((qA[:, t, c0:c0 + 512], c0, 512, qA[:, t, c0:c0 + 512], True, 0))
        for c0 in (0, 512):
            rope_units.append((kA[:, c0:c0 + 512], c0, 512, kP[:, P + c0:P + c0 + 512], True, 1))
        rope_units.append((kA[:, 1024:1280], 0, 256, kP[:, 1280:1536], False, 1))

        def rope_pe(pe):
            pe.wait_ge(s_rtab, 16)
            for u, (_, _, w, _, rot, _) in enumerate(rope_units):
                if u == 0:
                    pe.wait_ge(s_vc, 15)
                    pe.wait_ge(s_pevA, PEV_ODD + odd_cum[-1])
                pe.wait_ge(s_rq, u + 1)
                if u:
                    pe.wait_ge(s_rr, u)
                nc.tensor.matmul(PS[:, 0, 0:w], BD, rt[0][:, 0:w], start=True, stop=True).then_inc(s_rs, 1)
                pe.wait_ge(s_rx, u + 1)
                if rot:
                    if u:
                        pe.wait_ge(s_rd, 2 * u)
                    nc.tensor.matmul(PS[:, 1, 0:w], ROT, rt[3][:, 0:w], start=True, stop=True).then_inc(s_ro, 1)

        def att_pe(pe, i, first):
            pe.wait_ge(s_sl, i * 3 + 3)
            if first:
                pe.wait_ge(s_rd, 21)
                pe.wait_ge(s_kctx, 2)

            def scores(u):
                kv, j = divmod(u, 4)
                if not (first and u < 2):
                    pe.wait_ge(s_nm, i * 8 + (u - 1))
                for c in range(2):
                    last = nc.tensor.matmul(PS[:, 2 * (u % 2) + c, 0:320], q_s[64 * kv:64 * kv + 64, j, :],
                                            k_s[64 * kv:64 * kv + 64, 320 * c:320 * c + 320], start=True, stop=True)
                last.then_inc(s_S, 1)

            scores(0)
            scores(1)
            for u in range(8):
                pe.wait_ge(s_pn, i * 8 + (u + 1))
                if not (first and u < 2):
                    pe.wait_ge(s_pcA, i * 8 + (u - 1))
                if not (first and u < 1):
                    pe.wait_ge(s_pcV, i * 8 + u)
                for t in range(5):
                    dst = PS[:, 4 + u % 2, t * P:(t + 1) * P] if t < 4 else PS[:, 6, (u % 2) * P:(u % 2 + 1) * P]
                    last = nc.tensor.transpose(dst, pr[:, u % 2, t * P:(t + 1) * P], ident[:, :])
                last.then_inc(s_pt, 1)
                if u + 2 < 8:
                    scores(u + 2)
                if u % 2:
                    g = u // 2
                    kv, j = divmod(u - 1, 4)
                    pe.wait_ge(s_pcA, i * 8 + (u + 1))
                    pe.wait_ge(s_pcV, i * 8 + (u + 1))
                    if g == 0 and not first:
                        pe.wait_ge(s_yV, i)
                    for t in range(5):
                        last = nc.tensor.matmul(PS[64 * kv:64 * kv + 64, 7, j * P:(j + 2) * P],
                                                v_s[:, t, 64 * kv:64 * kv + 64], pT[:, g % 2, t, :],
                                                start=(t == 0), stop=(t == 4))
                    last.then_inc(s_O, 1)

        m_units = []
        for st_ in range(10):
            m_units.append((0, 8 + st_ if st_ < 2 else st_ - 2, st_ >= 2))
            m_units.append((1, 9 - st_, st_ >= 2))
        m_out = [n for n, u in enumerate(m_units) if u[2]]
        MF_END = len(m_units)

        def mlstm_pe(pe):
            pe.wait_ge(s_gexp, 4)
            pe.wait_ge(s_yV, 8)
            srcs = [R_a, R_fl, R_del]
            for q in range(30):
                if q % 8 == 0 and q >= 16:
                    pe.wait_ge(s_gc, q // 8 - 1)
                kind, c = divmod(q, 10)
                last = nc.tensor.transpose(PS[:, (q // 8) % 2, (q % 8) * 64:(q % 8) * 64 + 64],
                                           srcs[kind][0:64, c * P:(c + 1) * P], ident[0:64, 0:64])
                if q % 8 == 7 or q == 29:
                    last.then_inc(s_gt, 1)
            pe.wait_ge(s_rst, 48)
            for dp in range(4):
                last = nc.tensor.matmul(PS[:, 2, dp * 10:dp * 10 + 10], sel[:, 8 + dp, :], m_rows[:, 2, :], start=True, stop=True)
            last.then_inc(s_gt, 1)
            for g in range(5):
                if g >= 3:
                    pe.wait_ge(s_gc, 5 + g - 2)
                for q in range(4 * g, 4 * g + 4):
                    t, c = divmod(q, 10)
                    last = nc.tensor.transpose(PS[:, 3 + g % 3, (q % 4) * P:(q % 4 + 1) * P], kM[:, t, c * P:(c + 1) * P], ident[:, :])
                last.then_inc(s_gt, 1)
            pe.wait_ge(s_gc, 10)
            order = []
            for n in range(len(m_units) + 1):
                if n < len(m_units) and m_units[n][2]:
                    order.append(("A", n))
                if n >= 1:
                    order.append(("E", n - 1))
            for what, n in order:
                d, c, _ = m_units[n]
                o = m_out.index(n) if n in m_out else None
                if what == "A":
                    if o:
                        pe.wait_ge(s_mD, 2 * o)
                    cs = slice(c * P, (c + 1) * P)
                    for h in range(4):
                        r0 = 64 * (h % 2)
                        nc.tensor.matmul(PS[:, h % 2, (h // 2) * P:(h // 2 + 1) * P], kM[r0:r0 + 64, h // 2, cs],
                                         qM[r0:r0 + 64, h // 2, cs], start=True, stop=True)
                    for p2 in range(2):
                        nc.tensor.matmul(PS[:, 0, 256 + p2 * P:256 + (p2 + 1) * P], sel[:, 8 + 2 * d + p2, :],
                                         R_rst[0:64, cs], start=True, stop=True)
                    for h in range(4):
                        last = nc.tensor.matmul(PS[:, 2, h * P:(h + 1) * P], sel[:, 4 * d + h, :], R_b[0:64, cs], start=True, stop=True)
                    last.then_inc(s_mA, 1)
                else:
                    nb0 = 3 + 2 * d
                    if n >= 2:
                        pe.wait_ge(s_mF, n - 1)
                    pe.wait_ge(s_wv, 4 * (n + 1))
                    if o is not None:
                        pe.wait_ge(s_mD, 2 * o + 2)
                        pe.wait_ge(s_mF, n - 1)
                        for h in range(4):
                            r0 = 64 * (h % 2)
                            dst = PS[:, nb0 + h % 2, (h // 2) * 129:(h // 2 + 1) * 129]
                            nc.tensor.matmul(dst, WT[:, d, h, :], vMt[:, c, h, :], start=True, stop=False)
                            nc.tensor.matmul(dst, qt[r0:r0 + 64, d, h // 2, :], C[r0:r0 + 64, 2 * d + h // 2, :], start=False, stop=True)
                    for h in range(4):
                        r0 = 64 * (h % 2)
                        last = nc.tensor.matmul(PS[r0:r0 + 64, nb0 + h // 2, 258:387], kMt[:, c, h * 64:h * 64 + 64],
                                                wv[:, d, h, :], start=True, stop=True)
                    last.then_inc(s_mE, 1)
            pe.wait_ge(s_mF, MF_END)
            for c in range(8):
                if c >= 2:
                    pe.wait_ge(s_fm, c - 1)
                for h in range(4):
                    last = nc.tensor.transpose(PS[:, c % 2, h * P:(h + 1) * P], hsum[:, c, h * P:(h + 1) * P], ident[:, :])
                last.then_inc(s_fT, 1)

        def layer1_act(act):
            norm_act(act, 2)
            act.wait_ge(s_gw, 8 * 16)
            act.wait_ge(s_proj, PR_ODD)
            nc.scalar.activation(w_hi[:, 1, :, :], gw[:, :, :], ACT.Copy).then_inc(s_ghl, 1)
            act.wait_ge(s_small, 5 * 16)
            for n, (kind, t) in enumerate(odd_tiles):
                if n + 1 < NODD:
                    if odd_tiles[n + 1][0] == "qa":
                        act.wait_ge(s_qh[(J_ODD + n) % 2], 16 * (odd_tiles[n + 1][1] // 2 + 1))
                    hi_job(act, J_ODD + n, w_hi[:, n % 2, :, :], PR_ODD + (odd_cum[n] if n else 0))
                for b in range(odd_nb[n]):
                    c0, w, _ = BLOCKS[b]
                    if n == 0 and b == 0:
                        act.wait_ge(s_spill, 32)
                        act.wait_ge(s_gll, 1)
                    if n in V_TILES and V_TILES.index(n) and b == 0:
                        act.wait_ge(s_vt, 3 * V_TILES.index(n))
                    act.wait_ge(s_proj, PR_ODD + odd_cum[n] + b + 1)
                    src = PS[:, 3 * (n % 2) + b, 0:w]
                    if kind == "g":
                        ins = nc.scalar.activation(G[:, c0:c0 + w], src, ACT.Identity, bias=gate_b[:, 0:1])
                    elif kind == "om":
                        ins = nc.scalar.activation(oM[:, t, c0:c0 + w], src, ACT.Sigmoid)
                    elif kind == "km":
                        ins = nc.scalar.activation(kM[:, t, c0:c0 + w], src, ACT.Copy, scale=0.125)
                    else:
                        dst = {"ka": kA[:, c0:c0 + w], "qa": qA[:, t, c0:c0 + w] if b < 2 else None, "va": vtmp[:, c0:c0 + w],
                               "vm": vtmp[:, c0:c0 + w], "qm": qM[:, t % 2, c0:c0 + w] if b < 2 else None}[kind]
                        ins = nc.scalar.activation(dst, src, ACT.Copy)
                    ins.then_inc(s_pevA, 1)
            for u, (src, _, w, _, rot, g) in enumerate(rope_units):
                if u == 0:
                    act.wait_ge(s_proj, PR_OUT1)
                    act.wait_ge(s_pevA, PEV_ODD + odd_cum[-1])
                else:
                    act.wait_ge(s_rs, u)
                nc.scalar.activation(rt[0][:, 0:w], src, ACT.Square).then_inc(s_rq, 1)
                act.wait_ge(s_rs, u + 1)
                if u:
                    act.wait_ge(s_rx, u)
                nc.scalar.activation(rt[1][:, 0:w], PS[:, 0, 0:w], ACT.Sqrt, bias=eps_t[:, 0:1], scale=1.0 / 64).then_inc(s_rr, 1)
            att_act(act, 0, True)
            with act.Fori(1, 8) as i:
                att_act(act, i, False)
            mlstm_act(act)
            for o in range(KT):
                if o == 0:
                    out_hi(act, 0)
                if o + 1 < KT:
                    out_hi(act, o + 1)
            hi_job(act, F1.job, w_hi[:, F1.ws, :, :], PR_OUT1 + 14)
            norm_act(act, 3)
            ffn_act(act, F1)
            for g in range(0, 16, 2):
                act.wait_ge(s_oT, g + 1)
                nc.scalar.activation(out_tm[:, g // 2, 0:512], PS[:, g % 6, :], ACT.Copy).then_inc(s_ocA, 1)

        def out_hi(act, o):
            j = J_OUT1 + o
            act.wait_ge(s_wo[j % 2], 32 * (sum(1 for x in range(o + 1) if (J_OUT1 + x) % 2 == j % 2)))
            hi_job(act, j, w_hi[:, o % 2, :, :], PR_OUT1 - odd_nb[-1] if o == 0 else PR_OUT1 + 2 * (o - 1))

        def att_act(act, i, first):
            def exps(u):
                act.wait_ge(s_nm, i * 8 + (u + 1))
                nc.scalar.activation(st8[:, u, 2:3], sink[:, u:u + 1], ACT.Exp, bias=st8[:, u, 1:2]).then_inc(s_ex, 1)
                nc.scalar.activation(pr[:, u % 2, :], pr[:, u % 2, :], ACT.Exp, bias=st8[:, u, 1:2],
                                     accum_out=st8[:, u, 3:4]).then_inc(s_ex, 1)
            if first:
                act.wait_ge(s_small, 5 * 16)
            exps(0)
            exps(1)
            for u in range(8):
                act.wait_ge(s_pt, i * 8 + (u + 1))
                g = u // 2
                if not (first and g < 2):
                    act.wait_ge(s_O, i * 4 + (g - 1))
                nc.scalar.activation(pT[:, g % 2, 0:4, (u % 2) * P:(u % 2 + 1) * P],
                                     PS[:, 4 + u % 2, :].rearrange("p (t q) -> p t q", t=4), ACT.Copy).then_inc(s_pcA, 1)
                if u + 2 < 8:
                    exps(u + 2)
            act.wait_ge(s_O, i * 4 + 4)
            nc.scalar.activation(h_hi[:, 0:4, bass.ds(i * P, P)], PS[:, 7, :].rearrange("p (j q) -> p j q", j=4),
                                 ACT.Copy).then_inc(s_yA, 1)

        def mlstm_act(act):
            act.wait_ge(s_yV, 8)
            achain(act, nc.scalar.activation(R_b[64:128, :], G[64:128, :], ACT.Abs))
            achain(act, nc.scalar.activation(R_b[64:128, :], R_b[64:128, :], ACT.Exp, scale=-1.0))
            nc.scalar.activation(R_b[64:128, :], R_b[64:128, :], ACT.Ln, bias=ones[64:128, 0:1]).then_inc(s_g1, 1)
            for n, (t, sc) in enumerate(((R_rst, 1.0), (R_fl, 1.0), (R_del, -1.0))):
                act.wait_ge(s_gx, n + 1)
                nc.scalar.activation(t[0:64, :], t[0:64, :], ACT.Exp, scale=sc).then_inc(s_gexp, 1)
            act.wait_ge(s_gx, 4)
            nc.scalar.activation(m_rows[:, 2, :], m_rows[:, 2, :], ACT.Exp).then_inc(s_gexp, 1)
            for g in range(10):
                act.wait_ge(s_gt, g + 1)
                if g < 4:
                    cnt = 8 if g < 3 else 6
                    src = PS[:, g % 2, 0:cnt * 64].rearrange("p (s d r) -> p s d r", s=cnt, d=2)[:, :, :, 0:4]
                    nc.scalar.activation(gcol[:, 8 * g:8 * g + cnt, :].rearrange("p s (d r) -> p s d r", d=2), src,
                                         ACT.Copy).then_inc(s_gc, 1)
                elif g == 4:
                    nc.scalar.activation(dec_bc[:, :, :], PS[:, 2, 0:40].rearrange("p (d c) -> p d c", d=4), ACT.Copy).then_inc(s_gc, 1)
                else:
                    for q in range(4):
                        t, c = divmod(4 * (g - 5) + q, 10)
                        ins = nc.scalar.activation(kMt[:, c, t * P:(t + 1) * P], PS[:, 3 + (g - 5) % 3, q * P:(q + 1) * P], ACT.Copy)
                    ins.then_inc(s_gc, 1)
            act.wait_ge(s_gc, 10)

            def values(n):
                d, c, _ = m_units[n]
                if n >= 2:
                    act.wait_ge(s_mE, n - 1)
                for h in range(4):
                    nc.scalar.activation(wv[:, d, h, :], vMt[:, c, h, :], ACT.Copy,
                                         scale=gcol[:, 10 + c, 4 * d + h:4 * d + h + 1]).then_inc(s_wv, 1)
            act.wait_ge(s_ones, 5)
            for n in range(len(m_units) + 1):
                if n < len(m_units):
                    d, c, out = m_units[n]
                    values(n)
                    if out:
                        o = m_out.index(n)
                        act.wait_ge(s_mB, 4 * (o + 1))
                        nc.scalar.activation(XE[:, d, :, :], XE[:, d, :, :], ACT.Exp).then_inc(s_mC, 1)
            for c in range(8):
                act.wait_ge(s_fm, c + 1)
                nc.scalar.activation(h_hi[:, 4:8, c * P:(c + 1) * P], gated(c), ACT.Copy).then_inc(s_fhi, 1)

        def gated(c):
            return XE[:, c % 2, :, :]

        def layer1_vec(dve):
            norm_vec(dve, 2)
            dve.wait_ge(s_ghl, 1)
            nc.vector.tensor_tensor(w_lo[:, 1, :, :], gw[:, :, :], w_hi[:, 1, :, :].bitcast(F32), ALU.subtract).then_inc(s_gll, 1)
            dve.wait_ge(s_spill, 32)
            nc.vector.memset(vMt[:, :, :, 128:129], 1.0).then_inc(s_ones, 1)
            nc.vector.memset(vAt[:, 0:1, :], 0.0).then_inc(s_ones, 1)
            nc.vector.memset(vAt[:, 9:10, :], 0.0).then_inc(s_ones, 1)
            for n in range(NODD):
                if n + 1 < NODD:
                    j = J_ODD + n
                    dve.wait_ge(s_hi, j + 1)
                    nc.vector.tensor_tensor(w_lo[:, n % 2, :, :], st3[j % 2], w_hi[:, n % 2, :, :].bitcast(F32),
                                            ALU.subtract).then_inc(s_lo, 1)
                if n - 1 in V_TILES:
                    q = V_TILES.index(n - 1)
                    for g, (t0, cnt) in enumerate(V_GROUPS):
                        dve.wait_ge(s_vt, 3 * q + g + 1)
                        src = PS[:, 6 + (3 * q + g) % 2, 0:cnt * P].rearrange("p (t c) -> p t c", t=cnt)
                        if q == 0:
                            r0 = (1, 5, 10)[g]
                            dst = vAt[:, r0:r0 + cnt, :]
                        else:
                            dst = vMt[:, t0:t0 + cnt, q - 1, 0:P]
                        nc.vector.tensor_copy(dst, src).then_inc(s_vc, 1)
            dve.wait_ge(s_proj, PR_OUT1)
            nc.vector.memset(kP[:, 0:P], 0.0).then_inc(s_ones, 1)
            nc.vector.memset(kP[:, P + SEQ:2 * P + SEQ], 0.0).then_inc(s_ones, 1)
            dve.wait_ge(s_rtab, 16)
            for u, (src, c0, w, dst, rot, g) in enumerate(rope_units):
                if u:
                    dve.wait_ge(s_rd, 2 * u)
                dve.wait_ge(s_rr, u + 1)
                chain(dve, nc.vector.reciprocal(rt[2][:, 0:w], rt[1][:, 0:w]))
                xn_ = rt[3][:, 0:w] if rot else dst
                if rot:
                    nc.vector.scalar_tensor_tensor(xn_, src, head_g[:, g:g + 1], rt[2][:, 0:w], ALU.mult, ALU.mult).then_inc(s_rx, 1)
                    dve.wait_ge(s_rx, u + 1)
                    nc.vector.tensor_tensor(rt[4][:, 0:w], xn_, COS[:, c0:c0 + w], ALU.mult).then_inc(s_rd, 1)
                    dve.wait_ge(s_ro, u + 1)
                    chain(dve, nc.vector.tensor_tensor(rt[2][:, 0:w], PS[:, 1, 0:w], SIN[:, c0:c0 + w], ALU.mult))
                    dve.wait_ge(s_rd, 2 * u + 1)
                    if g == 0:
                        chain(dve, nc.vector.tensor_tensor(rt[4][:, 0:w], rt[4][:, 0:w], rt[2][:, 0:w], ALU.add))
                        nc.vector.tensor_scalar(dst, rt[4][:, 0:w], 0.125, None, ALU.mult).then_inc(s_rd, 1)
                    else:
                        nc.vector.tensor_tensor(dst, rt[4][:, 0:w], rt[2][:, 0:w], ALU.add).then_inc(s_rd, 1)
                else:
                    nc.vector.scalar_tensor_tensor(dst, src, head_g[:, g:g + 1], rt[2][:, 0:w], ALU.mult, ALU.mult).then_inc(s_rx, 1)
                    dve.wait_ge(s_rx, u + 1)
                    nc.vector.tensor_copy(st8[:, 0, 0:1], eps_t[:, :]).then_inc(s_rd, 1)
            dve.wait_ge(s_amk, 16)
            att_vec(dve, 0, 0, True)
            with dve.Fori(1, 7) as i:
                att_vec(dve, i, 1, False)
            att_vec(dve, 7, 2, False)
            mlstm_vec(dve)
            for o in range(KT):
                if o == 0:
                    lo_job(dve, J_OUT1, 0)
                if o + 1 < KT:
                    lo_job(dve, J_OUT1 + o + 1, (o + 1) % 2)
                else:
                    lo_job(dve, F1.job, F1.ws)
                for n, (c0, w, v) in enumerate(LAT):
                    if o == 0 and n == 0:
                        dve.wait_ge(s_back, 32)
                    dve.wait_ge(s_proj, PR_OUT1 + 2 * o + n + 1)
                    add_residual(dve, 3 * (o % 2) + n, o, c0, w, mod[:, ADA + G1 + o, 0:1])
            norm_vec(dve, 3)
            ffn_vec(dve, F1)
            for g in range(1, 16, 2):
                dve.wait_ge(s_oT, g + 1)
                nc.vector.tensor_copy(out_tm[:, g // 2, 512:1024], PS[:, g % 6, :]).then_inc(s_ocV, 1)

        def att_vec(dve, i, var, first):
            def top(u):
                dve.wait_ge(s_S, i * 8 + (u + 1))
                if not (first and u < 2):
                    dve.wait_ge(s_pt, i * 8 + (u - 1))
                nc.vector.tensor_copy(tick[:, u:u + 1], eps_t[:, 0:1]).then_inc(s_tick, 1)
                dve.wait_ge(s_amk, 16)
                nc.vector.tensor_tensor_reduce(out=pr[:, u % 2, :].rearrange("p (c k) -> p c k", c=2),
                                               in0=PS[:, 2 * (u % 2):2 * (u % 2) + 2, 0:320],
                                               in1=amask[:, var, :].rearrange("p (c k) -> p c k", c=2),
                                               scale=1.0, scalar=-3.0e38, op0=ALU.add, op1=ALU.max,
                                               accum_out=st8[:, u, 0:1]).then_inc(s_att, 1)
                dve.wait_ge(s_att, i * 24 + att_n(u, 0))
                nc.vector.tensor_scalar(st8[:, u, 1:2], st8[:, u, 0:1], sink[:, u:u + 1], -1.0, ALU.max, ALU.mult).then_inc(s_nm, 1)

            def att_n(u, what):
                return {0: (1, 2, 5, 8, 11, 14, 17, 20), 1: (3, 6, 9, 12, 15, 18, 21, 23), 2: (4, 7, 10, 13, 16, 19, 22, 24)}[what][u]
            top(0)
            top(1)
            for u in range(8):
                dve.wait_ge(s_ex, i * 16 + (2 * u + 2))
                nc.vector.tensor_tensor(st8[:, u, 4:5], st8[:, u, 3:4], st8[:, u, 2:3], ALU.add).then_inc(s_att, 1)
                dve.wait_ge(s_att, i * 24 + att_n(u, 1))
                nc.vector.reciprocal(st8[:, u, 5:6], st8[:, u, 4:5]).then_inc(s_att, 1)
                dve.wait_ge(s_att, i * 24 + att_n(u, 2))
                nc.vector.tensor_scalar(pr[:, u % 2, :], pr[:, u % 2, :], st8[:, u, 5:6], None, ALU.mult).then_inc(s_pn, 1)
                dve.wait_ge(s_pt, i * 8 + (u + 1))
                g = u // 2
                if not (first and g < 2):
                    dve.wait_ge(s_O, i * 4 + (g - 1))
                nc.vector.tensor_copy(pT[:, g % 2, 4, (u % 2) * P:(u % 2 + 1) * P], PS[:, 6, (u % 2) * P:(u % 2 + 1) * P]).then_inc(s_pcV, 1)
                if u + 2 < 8:
                    top(u + 2)
            dve.wait_ge(s_yA, i + 1)
            nc.vector.tensor_tensor(h_lo[:, 0:4, bass.ds(i * P, P)], PS[:, 7, :].rearrange("p (j q) -> p j q", j=4),
                                    h_hi[:, 0:4, bass.ds(i * P, P)].bitcast(F32), ALU.subtract).then_inc(s_yV, 1)

        def mlstm_vec(dve):
            v = nc.vector
            fw, bw, rows_ = slice(0, 32), slice(32, 64), slice(0, 64)
            dve.wait_ge(s_rst, 48)
            dve.wait_ge(s_g1, 1)
            chain(dve, v.scalar_tensor_tensor(R_fl[0:64, :], G[64:128, :], 0.0, R_b[64:128, :], ALU.min, ALU.subtract))
            chain(dve, v.tensor_tensor_scan(R_b[fw, :], R_rst[fw, :], R_fl[fw, :], 0.0, ALU.mult, ALU.add))
            chain(dve, v.tensor_tensor_scan(R_b[bw, ::-1], R_rst[bw, ::-1], R_fl[bw, ::-1], 0.0, ALU.mult, ALU.add))
            chain(dve, v.memset(R_del[0:64, :], 0.0))
            for dst, src in ((R_del[fw, 128:1024:128], R_b[fw, 127:1023:128]), (R_del[fw, 1152:1153], R_b[fw, 1151:1152]),
                             (R_del[fw, 0:1], R_b[fw, 1279:1280]), (R_del[bw, 127:1023:128], R_b[bw, 128:1024:128]),
                             (R_del[bw, 1023:1024], R_b[bw, 1024:1025]), (R_del[bw, 1151:1152], R_b[bw, 1152:1153])):
                chain(dve, v.tensor_copy(dst, src))
            chain(dve, v.tensor_tensor(R_a[rows_, :], G[rows_, :], R_b[rows_, :], ALU.subtract))
            chain(dve, v.tensor_tensor_scan(R_m[fw, 1024:1280], R_del[fw, 1024:1280], R_a[fw, 1024:1280], 0.0, ALU.add, ALU.max))
            chain(dve, v.tensor_tensor_scan(R_m[fw, 0:1024], R_del[fw, 0:1024], R_a[fw, 0:1024], R_m[fw, 1279:1280], ALU.add, ALU.max))
            chain(dve, v.tensor_tensor_scan(R_m[bw, 1279:1023:-1], R_del[bw, 1279:1023:-1], R_a[bw, 1279:1023:-1], 0.0, ALU.add, ALU.max))
            chain(dve, v.tensor_tensor_scan(R_m[bw, 1023::-1], R_del[bw, 1023::-1], R_a[bw, 1023::-1], R_m[bw, 1024:1025], ALU.add, ALU.max))
            chain(dve, v.memset(m_rows[:, :, :], 0.0))
            for dst, x, y in ((m_rows[fw, 0, 1:8], R_m[fw, 127:1023:128], R_b[fw, 127:1023:128]),
                              (m_rows[fw, 0, 0:1], R_m[fw, 1279:1280], R_b[fw, 1279:1280]),
                              (m_rows[fw, 0, 9:10], R_m[fw, 1151:1152], R_b[fw, 1151:1152]),
                              (m_rows[bw, 0, 0:7], R_m[bw, 128:1024:128], R_b[bw, 128:1024:128]),
                              (m_rows[bw, 0, 7:9], R_m[bw, 1024:1153:128], R_b[bw, 1024:1153:128])):
                chain(dve, v.tensor_tensor(dst, x, y, ALU.add))
            chain(dve, v.tensor_copy(m_rows[fw, 1, :], R_m[fw, 127:1280:128]))
            chain(dve, v.tensor_copy(m_rows[bw, 1, :], R_m[bw, 0:1280:128]))
            ch = lambda t: t[0:64, :].rearrange("p (c t) -> p c t", t=P)
            bc = lambda n: m_rows[:, n, :].rearrange("p (c o) -> p c o", o=1).broadcast_to((64, 10, P))
            v.tensor_tensor(ch(R_rst), bc(0), ch(R_m), ALU.subtract).then_inc(s_gx, 1)
            v.tensor_tensor(ch(R_fl), ch(R_a), bc(1), ALU.subtract).then_inc(s_gx, 1)
            v.tensor_tensor(R_del[0:64, :], R_b[0:64, :], R_m[0:64, :], ALU.add).then_inc(s_gx, 1)
            v.tensor_tensor(m_rows[:, 2, :], m_rows[:, 0, :], m_rows[:, 1, :], ALU.subtract).then_inc(s_gx, 1)
            dve.wait_ge(s_gx, 4)
            chain(dve, v.tensor_scalar(R_b[0:64, :], R_m[0:64, :], -1.0, None, ALU.mult))
            dve.wait_ge(s_gc, 10)
            for n in range(len(m_units) + 1):
                if n < len(m_units) and m_units[n][2]:
                    d, c, _ = m_units[n]
                    o = m_out.index(n)
                    dve.wait_ge(s_mA, o + 1)
                    if o >= 2:
                        dve.wait_ge(s_mE, n - 1)
                        dve.wait_ge(s_mD, 2 * o - 2)
                    for h in range(4):
                        v.scalar_tensor_tensor(XE[:, d, h, :], PS[:, 2, h * P:(h + 1) * P], gcol[:, c, 4 * d + h:4 * d + h + 1],
                                               mm_mask[:, d, :], ALU.add, ALU.add).then_inc(s_mB, 1)
                    v.tensor_tensor(qt[:, d, :, :], qM[:, :, c * P:(c + 1) * P],
                                    PS[:, 0, 256:512].rearrange("p (a b) -> p a b", a=2), ALU.mult)
                    dve.wait_ge(s_mC, o + 1)
                    for e in range(2):
                        v.tensor_tensor(WT[:, d, e::2, :], XE[:, d, e::2, :],
                                        PS[:, e, 0:256].rearrange("p (a b) -> p a b", a=2), ALU.mult).then_inc(s_mD, 1)
                if n >= 1:
                    mlstm_read(dve, n - 1)
            for c in range(8):
                dve.wait_ge(s_fT, c + 1)
                if c >= 2:
                    dve.wait_ge(s_flo, c - 1)
                v.tensor_tensor(gated(c), PS[:, c % 2, :].rearrange("p (h t) -> p h t", h=4), oM[:, :, c * P:(c + 1) * P],
                                ALU.mult).then_inc(s_fm, 1)
                dve.wait_ge(s_fhi, c + 1)
                v.tensor_tensor(h_lo[:, 4:8, c * P:(c + 1) * P], gated(c), h_hi[:, 4:8, c * P:(c + 1) * P].bitcast(F32),
                                ALU.subtract).then_inc(s_flo, 1)

        def mlstm_read(dve, n):
            v = nc.vector
            d, c, out = m_units[n]
            nb0 = 3 + 2 * d
            dve.wait_ge(s_mE, n + 1)
            if out:
                for e in range(2):
                    dn = PS[:, nb0 + e, 128:258:129]
                    chain(dve, v.tensor_tensor(den[:, d, e::2, 0], dn, gcol[:, 20 + c, 4 * d + e:4 * d + 4:2], ALU.max))
                    chain(dve, v.scalar_tensor_tensor(den[:, d, e::2, 0], dn, -1.0, den[:, d, e::2, 0], ALU.mult, ALU.max))
                chain(dve, v.reciprocal(den[:, d, :, 1], den[:, d, :, 0]))
                first = (c < 4) == (d == 0)
                for h in range(4):
                    src = PS[:, nb0 + h % 2, (h // 2) * 129:(h // 2) * 129 + P]
                    dst = hsum[:, c, h * P:(h + 1) * P]
                    if first:
                        ins = v.tensor_scalar(dst, src, den[:, d, h, 1:2], None, ALU.mult)
                    else:
                        ins = v.scalar_tensor_tensor(dst, src, den[:, d, h, 1:2], dst, ALU.mult, ALU.add)
                chain(dve, ins)
            for p2 in range(2):
                src = PS[:, nb0 + p2, 258:387]
                if n < 2:
                    ins = v.tensor_copy(C[:, 2 * d + p2, :], src)
                else:
                    ins = v.scalar_tensor_tensor(C[:, 2 * d + p2, :], C[:, 2 * d + p2, :], dec_bc[:, 2 * d + p2, c:c + 1], src, ALU.mult, ALU.add)
            ins.then_inc(s_mF, 1)

        @block.sync
        def _(sp):
            fc = a["ffn_conv"].rearrange("l w (m p) -> (l w m) p", p=P)
            for dst, src in (
                (rows[0:96, 0, :], a["ada_b"].rearrange("l (m p) -> (l m) p", p=P)),
                (rows[96:128, 0, :], a["norm_g"].rearrange("l s (k p) -> (l s k) p", p=P)),
                (rows[:, 1, :], fc[0:P, :]),
                (rows[0:4, 2, :], fc[P:P + 4, :]),
                (rows[4:16, 2, :], a["even_conv"][0].rearrange("w (m p) -> (w m) p", p=P)),
                (rows[16:24, 2, :], a["c"].rearrange("b (k p) -> (b k) p", p=P)),
                (rows[24:32, 2, :], a["c_ctx"].rearrange("(k p) -> k p", p=P)),
            ):
                sp.dma_start(dst, src).then_inc(s_rows, 16)
            for t in range(NT):
                src = a["x"][0, t * P:(t + 1) * P, :] if t < 8 else a["ctx"][0, (t - 8) * P:(t - 7) * P, :]
                sp.dma_start(x_in[:, t, :], src).then_inc(s_in[t], 16)
            for j in range(NEV):
                load_job(sp, j, cols_of(a["even_w_in"][0], even_tiles[j]))
                if j == 1:
                    sp.wait_ge(s_hlo, 3 * KT)
                    sp.dma_start(xs, X[:, :, :]).then_inc(s_spill, 16)
                    sp.wait_ge(s_spill, 16)
                    sp.dma_start(xf[:, 0:n_tab], a["dft_tables"]).then_inc(s_tab, 16)
                    sp.dma_start(TAIL[0:2, :], a["dft_tails"]).then_inc(s_tab, 16)
            for o in range(KT):
                load_job(sp, J_OUT0 + o, cols_of(a["even_w_out"][0], o))
                if o == 1:
                    sp.wait_ge(s_fy, 4 * FY)
                    sp.wait_ge(s_pevV, 24)
                    sp.dma_start(X[:, :, :], xs).then_inc(s_back, 16)
            ffn_loads(sp, F0)
            layer1_loads(sp)

        @block.gpsimd
        def _(gp):
            done = 0

            def step(ins):
                nonlocal done
                done += 1
                ins.then_inc(s_const, 1)
                gp.wait_ge(s_const, done)
            step(gp.memset(ident[:, :], 0.0))
            step(gp.memset(ones[:, :], 1.0))
            step(gp.memset(eps_t[:, :], EPS))
            step(gp.memset(cT[:, :, :], 0.0))
            step(gp.memset(pick[:, :], 0.0))
            step(gp.affine_select(out=ident[:, :], in_=ident[:, :], compare_op=ALU.not_equal, fill=1.0,
                                  base=0, pattern=[[-1, P]], channel_multiplier=1))
            for q in range(4):
                step(gp.affine_select(out=pick[:, :], in_=pick[:, :], compare_op=ALU.not_equal, fill=1.0,
                                      base=-32 * q, pattern=[[-1, 2]], channel_multiplier=1))
            for j in range(2 * ADA):
                if j >= 2:
                    gp.wait_ge(s_amm, j - 1)
                gp.dma_start(ada_st[:, j % 2, :, :], cols_of(a["ada_w"][j // ADA], j % ADA)).then_inc(s_al[j % 2], 16)
            layer1_pool(gp)

        @block.tensor
        def _(pe):
            pe.wait_ge(s_const, CONST)
            pe.wait_ge(s_rows, 7 * 16)
            for r, n in enumerate((P, P, 32)):
                last = nc.tensor.transpose(PS[:, 7, r * P:r * P + n], rows[0:n, r, :], ident[0:n, 0:n])
            last.then_inc(s_rowT, 1)
            for t in range(NT):
                pe.wait_ge(s_in[t], 16)
                for half in range(2):
                    g = 2 * t + half
                    if g >= 6:
                        pe.wait_ge(s_xcA if g % 2 == 0 else s_xcV, (g - 6) // 2 + 1)
                    for k in range(4):
                        last = nc.tensor.transpose(PS[:, g % 6, k * P:(k + 1) * P],
                                                   x_in[:, t, (4 * half + k) * P:(4 * half + k + 1) * P], ident[:, :])
                    last.then_inc(s_xT, 1)
            pe.wait_ge(s_ct, 1)
            pe.wait_ge(s_cols, 1)
            for m in range(16):
                ada_at(pe, m, m > 0)
            ada_sum(pe, 15, 1)
            norm_pe(pe, 0, 16)
            for j in range(NEV):
                pe.wait_ge(s_lo, j + 1)
                for n in range(3):
                    if j < 2 and n == 0:
                        pe.wait_ge(s_xcA, 10)
                        pe.wait_ge(s_xcV, 10)
                    if 2 <= j < 6:
                        pe.wait_ge(s_pevA, 3 * (j - 2) + n + 1)
                    elif j >= 6:
                        jj, kind = divmod(j - 6, 3)
                        if kind == 0:
                            pe.wait_ge(s_pevA, 12 + 3 * jj + n + 1)
                        else:
                            pe.wait_ge(s_pevV, 6 * jj + 3 * (kind - 1) + n + 1)
                    if j == 0:
                        pe.wait_ge(s_hlo, KT * (n + 1))
                    block_mm(pe, BLOCKS[n], 3 * (j % 2) + n, j % 2)
                    if j >= 5:
                        m = 16 + 3 * (j - 5) + n
                        if m < ADA:
                            if m == 16:
                                pe.wait_ge(s_fy, 4 * FY)
                            ada_at(pe, m, m > 16)
                        elif m == ADA:
                            ada_sum(pe, ADA - 1, 1)
                if 1 <= j <= 4:
                    fourier_pe(pe, j - 1)
            for o in range(KT):
                pe.wait_ge(s_lo, J_OUT0 + o + 1)
                for n in range(3):
                    if o < 2:
                        if n == 0:
                            pe.wait_ge(s_pevV, 24)
                    else:
                        pe.wait_ge(s_res, 3 * (o - 2) + n + 1)
                    if o == 0:
                        pe.wait_ge(s_mlo, KT * (n + 1))
                    block_mm(pe, BLOCKS[n], 3 * (o % 2) + n, o % 2)
            norm_pe(pe, 1, ADA)
            ffn_pe(pe, F0, 3 * KT, ADA)
            layer1_pe(pe)

        @block.scalar
        def _(act):
            act.wait_ge(s_rowT, 1)
            nc.scalar.activation(cols[:, :], PS[:, 7, 0:288], ACT.Copy).then_inc(s_cols, 1)
            act.wait_ge(s_cols, 1)
            act.wait_ge(s_const, CONST)
            nc.scalar.activation(cT[:, :, 0:2].rearrange("p k v -> p v k"),
                                 cols[:, 272:288].rearrange("p (v k) -> p v k", v=2), ACT.Silu).then_inc(s_ct, 1)
            for g in range(0, 2 * NT, 2):
                act.wait_ge(s_xT, g + 1)
                nc.scalar.activation(X[:, 0:4, (g // 2) * P:(g // 2 + 1) * P],
                                     PS[:, g % 6, :].rearrange("p (k t) -> p k t", k=4), ACT.Copy).then_inc(s_xcA, 1)
            for m in range(16):
                ada_copy(act, m)
            norm_act(act, 0)
            hi_job(act, 0, w_hi[:, 0, :, :])
            for j in range(NEV):
                if j + 1 < NEV + KT:
                    hi_job(act, j + 1, w_hi[:, (j + 1) % 2, :, :], 3 * j if j else None)
                for n, (c0, w, _) in enumerate(BLOCKS):
                    bank = 3 * (j % 2) + n
                    if j < 4:
                        if j == 0 and n == 0:
                            act.wait_ge(s_spill, 16)
                        if j and n == 0:
                            act.wait_ge(s_fold, j)
                        act.wait_ge(s_proj, 3 * j + n + 1)
                        nc.scalar.activation(U[:, c0:c0 + w], PS[:, bank, 0:w], ACT.Copy).then_inc(s_pevA, 1)
                    elif (j - 4) % 3 == 0:
                        if n == 0:
                            conv_free(act, (j - 4) // 3)
                        act.wait_ge(s_proj, 3 * j + n + 1)
                        g0 = c0 + 1 if n < 2 else c0 + 2
                        nc.scalar.activation(gpad[:, g0:g0 + w], PS[:, bank, 0:w], ACT.Copy).then_inc(s_pevA, 1)
                    if j >= 5 and 16 + 3 * (j - 5) + n < ADA:
                        ada_copy(act, 16 + 3 * (j - 5) + n)
                if 1 <= j <= 4:
                    fourier_act(act, j - 1)
            mix_hi(act, 3 * NEV)
            for o in range(1, KT):
                hi_job(act, J_OUT0 + o, w_hi[:, o % 2, :, :], 3 * (J_OUT0 + o - 1))
            hi_job(act, F0.job, w_hi[:, F0.ws, :, :], 3 * (J_OUT0 + 7))
            norm_act(act, 1)
            ffn_act(act, F0, ADA)
            layer1_act(act)

        @block.vector
        def _(dve):
            for g in range(1, 2 * NT, 2):
                dve.wait_ge(s_xT, g + 1)
                nc.vector.tensor_copy(X[:, 4:8, (g // 2) * P:(g // 2 + 1) * P],
                                      PS[:, g % 6, :].rearrange("p (k t) -> p k t", k=4)).then_inc(s_xcV, 1)
            dve.wait_ge(s_cols, 1)
            for m in range(16):
                ada_write(dve, m)
            norm_vec(dve, 0)
            lo_job(dve, 0, 0)
            for t_, cs in ((gpad, (0, 1025, TOK + 2)),):
                for c_ in cs:
                    chain(dve, nc.vector.memset(t_[:, c_:c_ + 1], 0.0))
            dve.wait_ge(s_spill, 16)
            chain(dve, nc.vector.memset(FO[:, 0:1], 0.0))
            chain(dve, nc.vector.memset(FO[:, 512:513], 0.0))
            for j in range(NEV):
                lo_job(dve, j + 1, (j + 1) % 2)
                jj, kind = divmod(j - 4, 3)
                if j < 4:
                    dve.wait_ge(s_pevA, 3 * (j + 1))
                    if j:
                        dve.wait_ge(s_ch, 2 * j)
                    fold(dve, U[:, 0:1024], FE[:, 0:513], FO[:, 0:512], 512)
                    fold(dve, U[:, 1024:1280], FE[:, 516:645], FO[:, 512:640], 128, last=True)
                for n, (c0, w, _) in enumerate(BLOCKS):
                    bank = 3 * (j % 2) + n
                    s0 = c0 if n < 2 else c0 + 1
                    if j >= 4 and kind == 1:
                        dve.wait_ge(s_pevA, 12 + 3 * jj + n + 1)
                        dve.wait_ge(s_proj, 3 * j + n + 1)
                        nc.vector.tensor_tensor(gpad[:, s0 + 1:s0 + 1 + w], gpad[:, s0 + 1:s0 + 1 + w],
                                                PS[:, bank, 0:w], ALU.mult).then_inc(s_pevV, 1)
                    elif j >= 4 and kind == 2:
                        dve.wait_ge(s_proj, 3 * j + n + 1)
                        nc.vector.tensor_tensor(Y[:, jj, c0:c0 + w], conv_e[:, s0:s0 + w],
                                                PS[:, bank, 0:w], ALU.mult).then_inc(s_pevV, 1)
                    if j >= 5 and 16 + 3 * (j - 5) + n < ADA:
                        ada_write(dve, 16 + 3 * (j - 5) + n)
                if j >= 4 and kind == 1:
                    dve.wait_ge(s_pevV, 6 * jj + 3)
                    dve.wait_ge(s_ch, 8)
                    conv3(dve, conv_e, gpad, lambda w_: cols[:, 260 + 4 * w_ + jj:261 + 4 * w_ + jj], TOK + 1)
                if 1 <= j <= 4:
                    fourier_vec(dve, j - 1)
            mix_lo(dve)
            for o in range(KT):
                if o + 1 < KT:
                    lo_job(dve, J_OUT0 + o + 1, (o + 1) % 2)
                else:
                    lo_job(dve, F0.job, F0.ws)
                for n, (c0, w, v) in enumerate(BLOCKS):
                    if o == 0 and n == 0:
                        dve.wait_ge(s_back, 16)
                    dve.wait_ge(s_proj, 3 * (J_OUT0 + o) + n + 1)
                    add_residual(dve, 3 * (o % 2) + n, o, c0, w, mod[:, G1 + o, v:v + 1])
            norm_vec(dve, 1)
            ffn_vec(dve, F0, ADA)
            layer1_vec(dve)


def dft_tables():
    def cs(rows, cols_, length, scale):
        x = 2 * np.pi * ((rows[:, None] * cols_[None, :]) % length) / length
        return np.cos(x) * scale, np.sin(x) * scale
    t, k = np.arange(P), np.arange(512)
    channel = list(cs(t, t, P, P ** -0.5))
    latent = [cs(t + P * j, k, SEQ, SEQ ** -0.5) for j in range(4)]
    alt = np.where(t % 2 == 0, 1.0, -1.0)
    parts = channel + [c for c, _ in latent] + [s for _, s in latent]
    parts += list(cs(t, t, CTX, CTX ** -0.5)) + [np.stack([alt / 32, alt / 16], 1)]
    tails = np.zeros((2, 642), np.float32)
    tails[0, 0:512] = np.where(k % 2 == 0, 1, -1) / 32
    tails[1, 512:640] = alt / 16
    tails[0, 640], tails[1, 641] = 1 / 32, 1 / 16
    return np.concatenate(parts, 1).astype(np.float32), tails


def rope_tables():
    f32 = np.float32
    row, col = np.repeat(np.arange(SEQ // 64, dtype=f32), 64), np.tile(np.arange(64, dtype=f32), SEQ // 64)
    inv = (f32(10000.0) ** (-np.arange(0, 32, 2, dtype=f32) / f32(32))).astype(f32)
    rope = np.zeros((P, 2304), f32)
    for p in range(P):
        d = p % 64
        angle = ((row if d < 32 else col) * inv[d % 16]).astype(f32)
        rope[p, 0:1024], rope[p, 1024:2048] = np.cos(angle), np.sin(angle)
        if (d % 32) < 16:
            rope[p + 16, 2048 + p] = -1
        else:
            rope[p - 16, 2048 + p] = 1
        rope[(p // 64) * 64:(p // 64) * 64 + 64, 2176 + p] = 1
    return rope


def mask_tables():
    f32, neg = np.float32, np.float32(-1e30)
    q, k = np.arange(P)[:, None], np.arange(384)[None, :]
    att = np.zeros((P, 3, 640), f32)
    att[:, :, 0:384] = np.where(np.abs(k - (q + P)) <= P, 0, neg)[:, None, :]
    att[:, 0, 0:P] = neg
    att[:, 2, 2 * P:3 * P] = neg
    resets = np.ones((64, TOK), f32)
    resets[0:32, 0::P] = 0
    resets[32:64, P - 1::P] = 0
    sel = np.zeros((64, 12, P), f32)
    for d in range(2):
        for h in range(4):
            sel[32 * d + h, 4 * d + h, :] = 1
        for pair in range(2):
            sel[32 * d + 2 * pair, 8 + 2 * d + pair, 0:64] = 1
            sel[32 * d + 2 * pair + 1, 8 + 2 * d + pair, 64:128] = 1
    s, t = np.arange(P)[:, None], np.arange(P)[None, :]
    causal = np.stack([np.where(s <= t, 0, neg), np.where(s >= t, 0, neg)], 1).astype(f32)
    return att, resets, sel, causal


INPUTS = ["x", "c", "ctx", "c_ctx", "ada_w", "ada_b", "norm_g", "even_w_in", "even_conv", "even_w_out", "odd_w_in",
          "odd_gate_b", "odd_q_g", "odd_k_g", "odd_sink", "odd_w_out", "ffn_w_up", "ffn_conv", "ffn_w_down"]


def kernel(**inputs):
    import concourse.bacc as bacc
    from concourse.bass_utils import run_bass_kernel_spmd

    laid = {name: np.ascontiguousarray(inputs[name]) for name in INPUTS}
    laid["dft_tables"], laid["dft_tails"] = dft_tables()
    laid["rope_tables"] = rope_tables()
    laid["att_masks"], laid["scan_resets"], laid["row_select"], laid["mlstm_masks"] = mask_tables()
    nc = bacc.Bacc("TRN2", target_bir_lowering=False, num_devices=1)
    arrays, args = {}, {}
    for name, value in laid.items():
        arrays[f"in_{name}_dram"] = value
        args[name] = nc.dram_tensor(f"in_{name}_dram", value.shape, mybir.dt.from_np(value.dtype),
                                    kind="ExternalInput").ap()
    args["out"] = nc.dram_tensor("out_0_dram", (1, SEQ, DM), F32, kind="ExternalOutput").ap()
    program(nc, args)
    result = run_bass_kernel_spmd(nc, [arrays], core_ids=[0])
    return result.results[0]["out_0_dram"]
```

```python
import math
from contextlib import ExitStack

import numpy as np
import concourse.bass as bass
from concourse import mybir

F32 = mybir.dt.float32
F32R = mybir.dt.float32r
ALU = mybir.AluOpType
ACT = mybir.ActivationFunctionType
AX = mybir.AxisListType

P = 128
DM, KT = 1024, 8
SEQ, CTX = 1024, 256
TOK = SEQ + CTX
NT = TOK // P
BLOCKS = [(0, 512, 0), (512, 512, 0), (1024, 256, 1)]
DFF, FT = 2816, 22
EPS = 1e-6
ADA_X = 8
ADA = 48
SH1, SC1, G1, SH2, SC2, G2 = (8 * i for i in range(6))


def program(nc, a):
    es = ExitStack()
    with es:
        def sb(name, shape, dt=F32, stack=None):
            return (stack or es).enter_context(nc.sbuf_tensor(name, shape, dt))

        def sem(name):
            return es.enter_context(nc.semaphore(name))

        cols = sb("cols", [P, 288])
        ident = sb("ident", [P, P])
        ones = sb("ones", [P, P])
        eps_t = sb("eps_t", [P, 1])
        cT = sb("cT", [P, KT, 32])
        pick = sb("pick", [P, 2])
        mod = sb("mod", [P, 2 * ADA, 2])
        gsc = sb("gsc", [P, 4, 2, KT])
        ada_sb = sb("ada_sb", [P, 2, P])
        gcol = sb("gcol", [P, 30, 8])
        dec_bc = sb("dec_bc", [P, 4, 10])
        m_rows = sb("m_rows", [64, 3, 10])
        sink = sb("sink", [P, 8])
        head_g = sb("head_g", [P, 2])
        gate_b = sb("gate_b", [P, 1])
        st8 = sb("st8", [P, 8, 6])
        tick = sb("tick", [P, 8])
        den = sb("den", [P, 2, 4, 2])
        w_hi = sb("w_hi", [P, 2, KT, P], F32R)
        w_lo = sb("w_lo", [P, 2, KT, P], F32R)
        stage = sb("stage", [P, 2, KT * P])
        xbase = ExitStack()
        X = sb("X", [P, KT, TOK], F32, xbase)
        with ExitStack() as s2:
            xnB = sb("xnB", [P, 3, 512], F32, s2)
            diagB = sb("diagB", [P, 4, P], F32, s2)
        ada_st = sb("ada_st", [P, 2, KT, P], F32, xbase)

        with ExitStack() as s0:
            x_in = sb("x_in", [P, NT, DM], F32, s0)
            rows = sb("rows", [P, 3, P], F32, s0)
            ada_x = sb("ada_x", [P, ADA_X, KT, P], F32, s0)
        s1 = ExitStack()
        h_hi = sb("h_hi", [P, KT, TOK], F32R, s1)
        h_lo = sb("h_lo", [P, KT, TOK], F32R, s1)
        with ExitStack() as s2:
            xnA = sb("xnA", [P, 3, 512], F32, s2)
            diagA = sb("diagA", [P, 4, P], F32, s2)
            sb("fill_n", [P, 9216 - 2048], F32, s2)
            sq = sb("sq", [P, 2, 512], F32, s2)
            ssum = sb("ssum", [P, TOK], F32, s2)
            rms = sb("rms", [P, 2, NT], F32, s2)
        with ExitStack() as s2:
            Y = sb("Y", [P, KT, TOK], F32, s2)
            gpad = sb("gpad", [P, TOK + 3], F32, s2)
        with ExitStack() as s2:
            d_hi = sb("d_hi", [P, 2, DM], F32R, s2)
            d_lo = sb("d_lo", [P, 2, DM], F32R, s2)
            a_hi = sb("a_hi", [P, 2, TOK], F32R, s2)
            a_lo = sb("a_lo", [P, 2, TOK], F32R, s2)
            fpad = sb("fpad", [P, TOK + 3], F32, s2)
            fcv = sb("fcv", [P, TOK + 1], F32, s2)
        s1.close()
        with ExitStack() as s2:
            out_tm = sb("out_tm", [P, 8, DM], F32, s2)
        xbase.close()
        so = ExitStack()
        with so:
            qA = sb("qA", [P, 4, SEQ], F32, so)
            kM = sb("kM", [P, 2, TOK], F32, so)
            vMt = sb("vMt", [P, NT, 4, 129], F32, so)
            rq = sb("rq", [P, 3, 64], F32, so)
            rq_s = sb("rq_s", [P, 2, 8], F32, so)
            nsink = sb("nsink", [P, 8], F32, so)
            sb("fill0", [P, 12288 - 4096 - 2560 - 5160 - 216], F32, so)
            with ExitStack() as s2:
                sb("fill1", [P, 2 * KT * TOK], F32, s2)
                with ExitStack() as s3:
                    gw = sb("gw", [P, KT, P], F32, s3)
                qM = sb("qM", [P, 2, SEQ], F32, s2)
                oM = sb("oM", [P, 4, SEQ], F32, s2)
                with ExitStack() as s3:
                    kA = sb("kA", [P, TOK], F32, s3)
                    vAt = sb("vAt", [P, 12, P], F32, s3)
                    G = sb("G", [P, TOK], F32, s3)
                    vtmp = sb("vtmp", [P, TOK], F32, s3)
                    kbd = sb("kbd", [P, P], F32, s3)
                    kt = sb("kt", [P, 512], F32, s3)
                with ExitStack() as s3:
                    k_s = sb("k_s", [P, 640], F32, s3)
                    v_s = sb("v_s", [P, 5, P], F32, s3)
                    sb("fill2", [P, 1536 + 1280], F32, s3)
                    q_s = sb("q_s", [P, 8, P], F32, s3)
                with ExitStack() as s3:
                    C = sb("C", [P, 4, 129], F32, s3)
                    sel = sb("sel", [64, 12, P], F32, s3)
                    mm_mask = sb("mm_mask", [P, 2, P], F32, s3)
                    sb("fill3", [P, 2816 - 516 - 1536 - 256], F32, s3)
                    XE = sb("XE", [P, 2, 4, P], F32, s3)
                    WT = sb("WT", [P, 2, 4, P], F32, s3)
                    qt = sb("qt", [P, 2, 2, P], F32, s3)
                    wv = sb("wv", [P, 2, 4, 129], F32, s3)
            sb("fill4", [P, 4 * TOK], F32, so)
            with ExitStack() as s2:
                with ExitStack() as s3:
                    rtab = sb("rtab", [P, 2304], F32, s3)
                with ExitStack() as s3:
                    pr = sb("pr", [P, 3, 640], F32, s3)
                sb("fill_p", [P, 2304], F32, s2)
                kP = sb("kP", [P, 1536], F32, s2)
                rotg = sb("rotg", [P, P], F32, s2)
                sb("fill_q", [P, 1280 - P], F32, s2)
                sb("fill5", [P, 4 * TOK], F32, s2)
                with ExitStack() as s3:
                    rt = [sb(f"rt{n}", [P, 512], F32, s3) for n in range(5)]
                with ExitStack() as s3:
                    pT = sb("pT", [P, 2, 5, 256], F32, s3)
                    amask = sb("amask", [P, 3, 640], F32, s3)
            with ExitStack() as s2:
                R_rst = sb("R_rst", [P, TOK], F32, s2)
                R_fl = sb("R_fl", [P, TOK], F32, s2)
                R_b = sb("R_b", [P, TOK], F32, s2)
                R_del = sb("R_del", [P, TOK], F32, s2)
                sb("fill6", [P, 4 * TOK], F32, s2)
                R_a = sb("R_a", [P, TOK], F32, s2)
                R_m = sb("R_m", [P, TOK], F32, s2)
                kMt = sb("kMt", [P, NT, 256], F32, s2)
        hsum = qA[:, :, :].rearrange("p a b -> p (a b)").rearrange("p (c v) -> p c v", c=8)
        COS, SIN = rtab[:, 0:1024], rtab[:, 1024:2048]
        ROT, BD = rtab[:, 2048:2176], rtab[:, 2176:2304]
        PS = es.enter_context(nc.psum_tensor("PS", [P, 8, 512], F32))

        xf = X[:, :, :].rearrange("p k t -> p (k t)")
        at = 0

        def cut(n):
            nonlocal at
            at += n
            return xf[:, at - n:at]
        CC, CS = cut(P), cut(P)
        CL = cut(4 * 512).rearrange("p (j k) -> p j k", j=4)
        SL = cut(4 * 512).rearrange("p (j k) -> p j k", j=4)
        CX, SX, ALT = cut(P), cut(P), cut(2)
        n_tab = at
        U, FE, FO = cut(TOK), cut(648), cut(640)
        conv_e = xf[:, at - 1288:at]
        TA = cut(5 * P).rearrange("p (j c) -> p j c", j=5)
        TB = cut(5 * P).rearrange("p (j c) -> p j c", j=5)
        TT, QS = cut(P), cut(640)
        TAIL = cut(642)
        xs = nc.dram_tensor("x_spill", [P, KT, TOK], F32).ap()

        s_in = [sem(f"x_loaded{t}") for t in range(NT)]
        s_rows = sem("rows_loaded")
        s_const = sem("constants_written")
        s_rowT = sem("rows_transposed")
        s_cols = sem("cols_copied")
        s_ct = sem("silu_c_written")
        s_xT = sem("x_transposed")
        s_xcA = sem("x_copied_scalar")
        s_xcV = sem("x_copied_vector")
        s_stage = [sem("stage_loaded0"), sem("stage_loaded1")]
        s_hi = sem("weights_hi")
        s_lo = sem("weights_lo")
        s_al = [sem("ada_loaded0"), sem("ada_loaded1")]
        s_ax = [sem(f"ada_early{m}") for m in range(ADA_X)]
        s_amm = sem("ada_partials")
        s_aev = sem("ada_partials_copied")
        s_asel = sem("ada_summed")
        s_mod = sem("mod_written")
        s_sq = sem("norm_squares")
        s_sqa = sem("norm_square_added")
        s_col = sem("norm_sums_by_token")
        s_root = sem("norm_root")
        s_rinv = sem("norm_root_inverted")
        s_diag = sem("norm_diagonal")
        s_bc = sem("norm_inverse_broadcast")
        s_xn = sem("norm_scaled")
        s_hhi = sem("h_hi_written")
        s_hlo = sem("h_lo_written")
        s_spill = sem("x_spilled")
        s_back = sem("x_reloaded")
        s_tab = sem("dft_tables_loaded")
        s_proj = sem("proj_psum_ready")
        s_pevA = sem("proj_psum_read_scalar")
        s_pevV = sem("proj_psum_read_vector")
        s_fold = sem("fourier_folded")
        s_ch = sem("channel_dft_ready")
        s_chA = sem("channel_dft_copied")
        s_ld = sem("seq_dft_ready")
        s_qs = sem("seq_dft_sine_copied")
        s_fy = sem("fourier_written")
        s_mhi = sem("mix_hi")
        s_mlo = sem("mix_lo")
        s_res = sem("residual_added")
        s_v = sem("vector_chain")
        s_out = sem("out_stored")
        s_fg = sem("ffn_gate_copied")
        s_fc = sem("ffn_conv_done")
        s_fs = sem("ffn_silu_done")
        s_fp = sem("ffn_product")
        s_ahi = sem("ffn_act_hi")
        s_alo = sem("ffn_act_lo")
        s_down = sem("down_psum_ready")

        def cols_of(w, c):
            return w[:, c * P:(c + 1) * P].rearrange("(k p) c -> p k c", p=P)

        even_tiles = [12, 13, 14, 15]
        for j in range(4):
            even_tiles += [4 + j, 8 + j, j]
        NEV = len(even_tiles)
        J_OUT0, J_FFN0 = NEV, NEV + KT
        PAIRS = FT // 2
        FY = 6
        st3 = [stage[:, s, :].rearrange("p (k c) -> p k c", k=KT) for s in range(2)]
        RES_OUT0 = 3 * KT
        RES_FFN0 = RES_OUT0 + PAIRS * KT * 3

        class Ffn:
            def __init__(s, layer, job, blocks, proj, res, down, tiles, ws):
                s.layer, s.job, s.blocks, s.nb = layer, job, blocks, len(blocks)
                s.proj, s.res, s.down = proj, res, down
                s.tiles = tiles
                s.ws = ws
                s.sp = job % 2
        F0 = Ffn(0, J_FFN0, BLOCKS, 3 * J_FFN0, RES_OUT0, 0, (0, 0), J_FFN0 % 2)


        block = es.enter_context(nc.Block())

        def load_job(sp, j, src):
            if j >= 2:
                sp.wait_ge(s_lo, j - 1)
            sp.dma_start(st3[j % 2], src).then_inc(s_stage[j % 2], 16)

        def ffn_loads(sp, F):
            up, down = a["ffn_w_up"][F.layer], a["ffn_w_down"][F.layer]

            def up_view(c):
                return up[:, bass.ds(c, P)].rearrange("(k p) c -> p k c", p=P)

            def one(j, n, dst, view):
                sp.wait_ge(s_lo, j - 1)
                slot = (F.sp + n) % 2
                sp.dma_start(dst[slot], view).then_inc(s_stage[slot], 16)
            one(F.job, 0, st3, up_view(0))
            st2 = [stage[:, s, :] for s in range(2)]
            with sp.Fori(0, PAIRS) as i:
                j = i * 6 + (F.job + 1)
                one(j, 1, st3, up_view(i * 256 + DFF))
                one(j + 1, 2, st3, up_view(i * 256 + P))
                one(j + 2, 3, st3, up_view(i * 256 + (DFF + P)))
                one(j + 3, 4, st2, down[bass.ds(i * 256, P), :])
                one(j + 4, 5, st2, down[bass.ds(i * 256 + P, P), :])
                one(j + 5, 6, st3, up_view(i * 256 + 256))

        CONST = 10

        def block_mm(pe, blk, bank, wslot, ready=None, hook=None):
            c0, w, _ = blk
            for k in range(KT):
                if k == 6 and hook is not None:
                    hook()
                if ready is not None:
                    pe.wait_ge(s_hlo, ready + k + 1)
                for q, (wt, ht) in enumerate(((w_hi, h_hi), (w_hi, h_lo), (w_lo, h_hi))):
                    last = nc.tensor.matmul(PS[:, bank, 0:w], wt[:, wslot, k, :], ht[:, k, c0:c0 + w],
                                            start=(k == 0 and q == 0), stop=(k == KT - 1 and q == 2))
            last.then_inc(s_proj, 1)

        def ada_step(pe, j, loaded, slot, sum_last=True):
            early = isinstance(j, int) and 2 <= j < 2 + ADA_X
            src = ada_x[:, j - 2] if early else ada_st[:, slot]
            if early:
                pe.wait_ge(s_ax[j - 2], 16)
            else:
                pe.wait_ge(s_al[slot], loaded)
            if not (isinstance(j, int) and j < 2):
                pe.wait_ge(s_mod, j - 1)
            for k in range(KT):
                q = k % 4
                last = nc.tensor.matmul(PS[32 * q:32 * q + 32, 6 + slot, 0:P], cT[:, k, :], src[:, k, :],
                                        start=(k < 4), stop=(k >= 4), tile_position=(0, 32 * q))
            last.then_inc(s_amm, 1)
            if sum_last:
                ada_sum(pe, j - 1, 1 - slot)

        def ada_at(pe, j, sum_last=True):
            ada_step(pe, j, 16 * (j // 2 + 1 - (ADA_X // 2 if j >= 2 + ADA_X else 0)), j % 2, sum_last)

        def ada_sum(pe, j, slot):
            pe.wait_ge(s_aev, j + 1)
            nc.tensor.matmul(PS[:, 6 + slot, P:P + 2], ada_sb[:, slot, :], pick[:, :],
                             start=True, stop=True).then_inc(s_asel, 1)

        def sq_seq(q):
            nb = NORM_NB[q]
            if q % 2:
                return [(k, n) for k in range(KT) for n in range(nb)]
            return [(k, n) for n in range(nb) for k in range(KT)]

        def sq_at(q, k, n):
            return NORM_AT[q] * KT + sq_seq(q).index((k, n))

        def norm_cols(pe, q, n):
            c0, w, _ = BLOCKS[n]
            pe.wait_ge(s_sqa, sq_at(q, KT - 1, n) + 1)
            if q == 0:
                pe.wait_ge(s_xcA, NT)
                pe.wait_ge(s_xcV, NT)
            elif n:
                pe.wait_ge(s_root, NORM_AT[q] + n)
            for t in range(w // P):
                last = nc.tensor.matmul(PS[:, cols_bank(q, n), 4 * n + t:4 * n + t + 1], ssum[:, c0 + t * P:c0 + (t + 1) * P], ones[:, 0:1],
                                        start=True, stop=True)
            last.then_inc(s_col, 1)

        def cols_bank(q, n):
            return 6 if q else n

        def norm_bank(n):
            return 6 if n == 1 else 7

        def norm_bcast(pe, q, n):
            w = BLOCKS[n][1]
            if n == 1:
                pe.wait_ge(s_root, NORM_AT[q] + NORM_NB[q])
            if n == 2:
                pe.wait_ge(s_xn, (NORM_AT[q] + 1) * KT)
            pe.wait_ge(s_diag, NORM_AT[q] + n + 1)
            diag = diagA if q < 2 else diagB
            nc.tensor.matmul(PS[:, norm_bank(n), 0:w], ones[:, :],
                             diag[:, 0:w // P, :].rearrange("p t c -> p (t c)"), start=True, stop=True).then_inc(s_bc, 1)

        def first_pair(pe, q, weights, slots, free):
            nb = NORM_NB[q]
            for n in range(nb):
                for t in range(2):
                    if n == 0:
                        pe.wait_ge(*weights[t])
                    if free is not None:
                        pe.wait_ge(*free[t])
                    block_mm(pe, BLOCKS[n], 3 * t + n, slots[t], (NORM_AT[q] + n) * KT if t == 0 else None,
                             (lambda: norm_bcast(pe, q, n + 1)) if t == 0 and n + 1 < nb else None)
        NORM_NB = (3, 3, 3, 2)
        NORM_AT = (0, 3, 6, 9)

        def fourier_pe(pe, g):
            if g == 0:
                pe.wait_ge(s_tab, 32)
                pe.wait_ge(s_xn, 3 * KT)
            pe.wait_ge(s_fold, g + 1)
            if g >= 1:
                pe.wait_ge(s_fy, FY * g)
                pe.wait_ge(s_qs, 2 * g)
            for half, (src, tab) in enumerate(((FE, CC), (FO, CS))):
                if half:
                    pe.wait_ge(s_chA, 5 * g + 3)
                for j in range(5):
                    c0 = j * P if j < 4 else (516 if half == 0 else 512)
                    dst = PS[:, 6, j * P:(j + 1) * P] if j < 4 else PS[:, 7, 0:P]
                    last = nc.tensor.matmul(dst, src[:, c0:c0 + P], tab, start=True, stop=True)
                if half == 0:
                    last = nc.tensor.matmul(PS[0:2, 7, P:2 * P], FE[:, 512:645:132], CC, start=True, stop=True)
                last.then_inc(s_ch, 1)
            pe.wait_ge(s_chA, 5 * g + 5)
            for j in range(4):
                nc.tensor.matmul(PS[:, 6, :], TA[:, j, :], CL[:, j, :], start=(j == 0), stop=False)
            nc.tensor.matmul(PS[:, 6, :], TT[0:2, :], TAIL[0:2, 0:512], start=False, stop=True)
            for j in range(4):
                last = nc.tensor.matmul(PS[:, 7, :], TB[:, j, :], SL[:, j, :], start=(j == 0), stop=(j == 3))
            last.then_inc(s_ld, 1)
            pe.wait_ge(s_fy, FY * g + 2)
            pe.wait_ge(s_qs, 2 * g + 1)
            nc.tensor.matmul(PS[:, 6, 0:P], TA[:, 4, :], CX, start=True, stop=False)
            nc.tensor.matmul(PS[:, 6, 0:P], TT[0:2, :], TAIL[0:2, 512:640], start=False, stop=True)
            for j in range(4):
                nc.tensor.matmul(PS[:, 6, P:P + 1], TA[:, j, :], ALT[:, 0:1], start=(j == 0), stop=False)
            nc.tensor.matmul(PS[:, 6, P:P + 1], TT[0:2, :], TAIL[0:2, 640:641], start=False, stop=True)
            nc.tensor.matmul(PS[:, 6, P + 1:P + 2], TA[:, 4, :], ALT[:, 1:2], start=True, stop=False)
            nc.tensor.matmul(PS[:, 6, P + 1:P + 2], TT[0:2, :], TAIL[0:2, 641:642], start=False, stop=True)
            nc.tensor.matmul(PS[:, 7, 0:P], TB[:, 4, :], SX, start=True, stop=True).then_inc(s_ld, 1)

        DOWN_BANK = (6, 7, 2)

        def ffn_pe(pe, F, ada_from=None):
            nb = F.nb

            def tile(job, wslot, bank0, free, after=None, bank2=None):
                pe.wait_ge(s_lo, job + 1)
                for n in range(nb):
                    if free is not None:
                        pe.wait_ge(free[0], free[1] + (n + 1))
                    if n == 2 and bank2 is not None:
                        pe.wait_ge(s_res, bank2)
                    block_mm(pe, F.blocks[n], bank0 + n, wslot)
                    if after is not None:
                        after(n)

            def down(i, last=False):
                pe.wait_ge(s_lo, i * 6 + F.job)
                pe.wait_ge(s_alo, i * (2 * nb) + F.tiles[1])
                if ada_from is not None:
                    pe.wait_ge(s_mod, i * 4 + ada_from)
                for o in range(KT):
                    for n in range(nb):
                        c = o * nb + n
                        c0, w, _ = F.blocks[n]
                        if o == 0 and n == 2:
                            pe.wait_ge(s_fg, i * (2 * nb) + (F.tiles[0] + (0 if last else nb)))
                        pe.wait_ge(s_res, i * (KT * nb) + (F.res - KT * nb + c - nb + 1))
                        mm = 0
                        for f in range(2):
                            for wt, at_ in ((d_hi, a_hi), (d_hi, a_lo), (d_lo, a_hi)):
                                ins = nc.tensor.matmul(PS[:, DOWN_BANK[n], 0:w], wt[:, f, o * P:(o + 1) * P],
                                                       at_[:, f, c0:c0 + w], start=(mm == 0), stop=(mm == 5))
                                mm += 1
                        ins.then_inc(s_down, 1)

            def ada(i, m):
                if m == 0:
                    pe.wait_ge(s_res, i * (KT * nb) + F.res)
                ada_step(pe, i * 4 + (ada_from + m), i * 32 + 16 * ((ada_from + m) // 2 + 1 - ADA_X // 2), m % 2, m > 0)

            def pair(i, first):
                j = i * 6 + F.job
                t = i * (2 * nb)

                def last_sum(n):
                    if ada_from is not None and n == 0 and not first:
                        ada_sum(pe, i * 4 + (ada_from - 1), 1)

                def in_gate(n):
                    if ada_from is not None and n in (0, 2):
                        ada(i, n // 2)

                def in_value(n):
                    if ada_from is not None and n in (0, 2):
                        ada(i, 2 + n // 2)
                if first:
                    first_pair(pe, 2 * F.layer + 1, ((s_lo, j + 1), (s_lo, j + 2)), (F.ws, 1 - F.ws), None)
                else:
                    tile(j, F.ws, 0, (s_fg, t + F.tiles[0] - nb), after=last_sum)
                    tile(j + 1, 1 - F.ws, 3, (s_fp, t + F.tiles[0] - nb))
                    down(i)
                tile(j + 2, F.ws, 0, (s_fg, t + F.tiles[0]), after=in_gate, bank2=None if first else i * (KT * nb) + F.res)
                tile(j + 3, 1 - F.ws, 3, (s_fp, t + F.tiles[0]), after=in_value)
            pe.wait_ge(s_res, F.res)
            pair(0, True)
            with pe.Fori(1, PAIRS) as i:
                pair(i, False)
            if ada_from is not None:
                ada_sum(pe, 4 * PAIRS + ada_from - 1, 1)
            if F.layer == 1:
                down(PAIRS, last=True)
                return
            pe.wait_ge(s_lo, PAIRS * 6 + F.job)
            pe.wait_ge(s_alo, PAIRS * (2 * nb) + F.tiles[1])
            pe.wait_ge(s_mod, 2 * ADA)
            for c in range(KT * nb):
                n, o = divmod(c, KT)
                c0, w, _ = F.blocks[n]
                if c < 3:
                    pe.wait_ge(s_fg, PAIRS * (2 * nb) + F.tiles[0])
                else:
                    pe.wait_ge(s_res, (PAIRS - 1) * (KT * nb) + F.res + c - 2)
                for f in range(2):
                    for q, (wt, at_) in enumerate(((d_hi, a_hi), (d_hi, a_lo), (d_lo, a_hi))):
                        ins = nc.tensor.matmul(PS[:, c % 3, 0:w], wt[:, f, o * P:(o + 1) * P],
                                               at_[:, f, c0:c0 + w], start=(f == 0 and q == 0), stop=(f == 1 and q == 2))
                ins.then_inc(s_down, 1)
                if c == 10:
                    norm_cols(pe, 2, 0)
                elif c == 15:
                    norm_bcast(pe, 2, 0)
                elif c == 20:
                    norm_cols(pe, 2, 1)
            norm_cols(pe, 2, 2)


        def conv_free(act, jj):
            if jj:
                act.wait_ge(s_v, 7 + 3 * jj)

        def hi_job(act, j, dst, used=None, slot=None, count=None):
            slot = j % 2 if slot is None else slot
            act.wait_ge(s_stage[slot], 16 * (j // 2 + 1) if count is None else count)
            if used is not None:
                act.wait_ge(s_proj, used)
            nc.scalar.activation(dst, st3[slot], ACT.Copy).then_inc(s_hi, 1)

        def ada_copy(act, j, slot=None):
            slot = j % 2 if slot is None else slot
            act.wait_ge(s_amm, j + 1)
            if not (isinstance(j, int) and j < 2):
                act.wait_ge(s_asel, j - 1)
            nc.scalar.activation(ada_sb[:, slot, :], PS[:, 6 + slot, 0:P], ACT.Copy).then_inc(s_aev, 1)

        def sq_act(act, q, k, n):
            c0, w, _ = BLOCKS[n]
            at_ = sq_at(q, k, n)
            x_ready(act, q, n, k)
            if at_ >= 2:
                act.wait_ge(s_sqa, at_ - 1)
            nc.scalar.activation(sq[:, at_ % 2, 0:w], X[:, k, c0:c0 + w], ACT.Square).then_inc(s_sq, 1)

        def root_act(act, q, n):
            act.wait_ge(s_col, NORM_AT[q] + n + 1)
            cnt = BLOCKS[n][1] // P
            nc.scalar.activation(rms[:, 0, 4 * n:4 * n + cnt], PS[:, cols_bank(q, n), 4 * n:4 * n + cnt], ACT.Sqrt,
                                 bias=eps_t[:, 0:1], scale=1.0 / DM).then_inc(s_root, 1)

        def h_act(act, q, n, hooks={}):
            c0, w, v = BLOCKS[n]
            at_ = (NORM_AT[q] + n) * KT
            xn = xnA if q < 2 else xnB
            for k in range(KT):
                if k in hooks:
                    hooks[k]()
                act.wait_ge(s_xn, at_ + k + 1)
                nc.scalar.activation(h_hi[:, k, c0:c0 + w], xn[:, (at_ + k) % 3, 0:w], ACT.Identity,
                                     bias=shift_of(q, k, v)).then_inc(s_hhi, 1)

        def x_ready(eng, q, n, k):
            if q == 0:
                if k == 0:
                    eng.wait_ge(s_xcA, min(4 * n + 4, NT))
                    eng.wait_ge(s_xcV, min(4 * n + 4, NT))
            elif q == 1:
                eng.wait_ge(s_res, 3 * k + n + 1)
            elif q == 2:
                eng.wait_ge(s_res, RES_FFN0 - 3 * KT + KT * n + k + 1)
            else:
                eng.wait_ge(s_res, RES_FFN0 + 2 * k + n + 1)

        def shift_of(q, k, v):
            m = (q // 2) * ADA + (SH1, SH2)[q % 2] + k
            return mod[:, m, v:v + 1]

        def fourier_act(act, g):
            act.wait_ge(s_ch, 2 * g + 1)
            if g:
                act.wait_ge(s_ld, 2 * g)
            nc.scalar.activation(TA[:, 0:4, :], PS[:, 6, :].rearrange("p (j c) -> p j c", j=4), ACT.Copy).then_inc(s_chA, 1)
            nc.scalar.activation(TA[:, 4, :], PS[:, 7, 0:P], ACT.Copy).then_inc(s_chA, 1)
            nc.scalar.activation(TT[0:2, :], PS[0:2, 7, P:2 * P], ACT.Copy).then_inc(s_chA, 1)
            act.wait_ge(s_ch, 2 * g + 2)
            nc.scalar.activation(TB[:, 0:4, :], PS[:, 6, :].rearrange("p (j c) -> p j c", j=4), ACT.Copy).then_inc(s_chA, 1)
            nc.scalar.activation(TB[:, 4, :], PS[:, 7, 0:P], ACT.Copy).then_inc(s_chA, 1)
            act.wait_ge(s_ld, 2 * g + 1)
            if g:
                act.wait_ge(s_fy, FY * g)
            nc.scalar.activation(QS[:, 0:512], PS[:, 7, :], ACT.Copy).then_inc(s_qs, 1)
            act.wait_ge(s_ld, 2 * g + 2)
            nc.scalar.activation(QS[:, 512:640], PS[:, 7, 0:P], ACT.Copy).then_inc(s_qs, 1)

        def mix_hi(act, proj):
            for n, (c0, w, _) in enumerate(BLOCKS):
                for k in range(KT):
                    if n == 0 and k == 0:
                        act.wait_ge(s_proj, proj)
                        act.wait_ge(s_fy, 4 * FY)
                        act.wait_ge(s_pevV, 24)
                    nc.scalar.activation(h_hi[:, k, c0:c0 + w], Y[:, k, c0:c0 + w], ACT.Copy).then_inc(s_mhi, 1)

        def ffn_act(act, F, ada_from=None):
            nb = F.nb
            d_hi_slots = [d_hi[:, s, :] for s in range(2)]

            def hi(i, n, wslot, used):
                jn = F.sp + 1 + n
                slot = jn % 2
                before = (F.job + 1 + n) // 2 + 1
                act.wait_ge(s_stage[slot], i * 48 + 16 * before)
                if used is not None:
                    act.wait_ge(*used)
                if wslot is None:
                    nc.scalar.activation(d_hi_slots[n - 3], stage[:, slot, :], ACT.Copy).then_inc(s_hi, 1)
                else:
                    nc.scalar.activation(w_hi[:, wslot, :, :], st3[slot], ACT.Copy).then_inc(s_hi, 1)

            def gate(i, half, after=None):
                if not (isinstance(i, int) and i * 2 + F.fc0 + half == 0):
                    act.wait_ge(s_fc, i * 2 + (F.fc0 + half))
                for n in range(nb):
                    c0, w, _ = F.blocks[n]
                    if isinstance(i, int) and i == half == 0:
                        act.wait_ge(s_proj, F.proj + 2 * n + 1)
                    else:
                        act.wait_ge(s_proj, i * (4 * nb) + (F.proj + 2 * nb * half + n + 1))
                    g0 = c0 + 1 if n < 2 else c0 + 2
                    nc.scalar.activation(fpad[:, g0:g0 + w], PS[:, n, 0:w], ACT.Copy).then_inc(s_fg, 1)
                    if after is not None:
                        after(n)

            def silu(i, half):
                act.wait_ge(s_fc, i * 2 + (F.fc0 + half + 1))
                nc.scalar.activation(fcv[:, 0:F.cw], fcv[:, 0:F.cw], ACT.Silu).then_inc(s_fs, 1)

            def a_half(i, half):
                if half == 0 and not isinstance(i, int):
                    act.wait_ge(s_down, i * (KT * nb) + F.down)
                for n in range(nb):
                    c0, w, _ = F.blocks[n]
                    s0 = c0 if n < 2 else c0 + 1
                    act.wait_ge(s_fp, i * (2 * nb) + (F.tiles[0] + nb * half + n + 1))
                    nc.scalar.activation(a_hi[:, half, c0:c0 + w], fcv[:, s0:s0 + w], ACT.Copy).then_inc(s_ahi, 1)

            def pair(i, first):
                pb = F.proj

                def ada(m):
                    if ada_from is not None:
                        ada_copy(act, i * 4 + (ada_from + m), (ada_from + m) % 2)

                def in_gate(n):
                    if n in (0, 2):
                        ada(n // 2)
                if not first:
                    hi(i, 0, 1 - F.ws, (s_proj, i * (4 * nb) + pb))
                gate(i, 0)
                hi(i, 1, F.ws, (s_proj, pb + 2 * nb - 1) if first else (s_proj, i * (4 * nb) + (pb + nb)))
                silu(i, 0)
                hi(i, 2, 1 - F.ws, (s_proj, i * (4 * nb) + (pb + 2 * nb)))
                a_half(i, 0)
                hi(i, 3, None, None if first else (s_down, i * (KT * nb) + F.down))
                hi(i, 4, None, None)
                gate(i, 1, in_gate)
                hi(i, 5, F.ws, (s_proj, i * (4 * nb) + (pb + 3 * nb)))
                ada(2)
                silu(i, 1)
                ada(3)
                a_half(i, 1)
            act.wait_ge(s_hlo, (NORM_AT[2 * F.layer + 1] + nb) * KT)
            pair(0, True)
            with act.Fori(1, PAIRS) as i:
                pair(i, False)
            if F.layer == 1:
                return
            for n in range(2):
                hi_job(act, J_ODD + n, w_hi[:, (n + 1) % 2, :, :], PR_ODD)
            for c in range(KT * nb):
                sq_act(act, 2, c % KT, c // KT)
                if c == 11:
                    root_act(act, 2, 0)
                elif c == 22:
                    root_act(act, 2, 1)
            root_act(act, 2, 2)
        F0.fc0, F0.cw = 0, TOK + 1

        vn = [0]

        def chain(dve, ins):
            vn[0] += 1
            ins.then_inc(s_v, 1)
            dve.wait_ge(s_v, vn[0])

        def lo_job(dve, j, wslot):
            dve.wait_ge(s_hi, j + 1)
            nc.vector.tensor_tensor(w_lo[:, wslot, :, :], st3[j % 2], w_hi[:, wslot, :, :].bitcast(F32),
                                    ALU.subtract).then_inc(s_lo, 1)

        def ada_write(dve, j, slot=None, m=None):
            slot = j % 2 if slot is None else slot
            dve.wait_ge(s_asel, j + 1)
            if isinstance(j, int):
                dst, b = mod[:, j, :], cols[:, j:j + 1]
            else:
                dst, b = mod[:, bass.ds(j, 1), :], cols[:, bass.ds(j, 1)]
            if isinstance(j, int):
                nc.vector.tensor_scalar(dst, PS[:, 6 + slot, P:P + 2], b, None, ALU.add).then_inc(s_mod, 1)
            else:
                nc.vector.tensor_tensor(mod[:, bass.ds(j, 1), :].rearrange("p a v -> p (a v)"), PS[:, 6 + slot, P:P + 2],
                                        cols[:, bass.ds(j, 1)].broadcast_to((P, 2)), ALU.add).then_inc(s_mod, 1)

        def gains_vec(dve, q):
            sc = (q // 2) * ADA + (SC1, SC2)[q % 2]
            dve.wait_ge(s_mod, sc + KT)
            for v in range(2):
                chain(dve, nc.vector.scalar_tensor_tensor(gsc[:, q, v, :], mod[:, sc:sc + KT, v], 1.0,
                                                          cols[:, 96 + q * KT:96 + (q + 1) * KT], ALU.add, ALU.mult))

        def sum_vec(dve, q, k, n):
            c0, w, _ = BLOCKS[n]
            at_ = sq_at(q, k, n)
            dve.wait_ge(s_sq, at_ + 1)
            if k == 0:
                if q:
                    dve.wait_ge(s_col, NORM_AT[q])
                nc.vector.tensor_copy(ssum[:, c0:c0 + w], sq[:, at_ % 2, 0:w]).then_inc(s_sqa, 1)
            else:
                dve.wait_ge(s_sqa, sq_at(q, k - 1, n) + 1)
                nc.vector.tensor_tensor(ssum[:, c0:c0 + w], ssum[:, c0:c0 + w], sq[:, at_ % 2, 0:w], ALU.add).then_inc(s_sqa, 1)

        def diag_vec(dve, q, n):
            at_, cnt = NORM_AT[q] + n, BLOCKS[n][1] // P
            dve.wait_ge(s_root, at_ + 1)
            nc.vector.reciprocal(rms[:, 1, 4 * n:4 * n + cnt], rms[:, 0, 4 * n:4 * n + cnt]).then_inc(s_rinv, 1)
            dve.wait_ge(s_rinv, at_ + 1)
            if at_:
                dve.wait_ge(s_bc, at_)
            diag = diagA if q < 2 else diagB
            nc.vector.tensor_tensor(diag[:, 0:cnt, :],
                                    ident[:, :].rearrange("p (o c) -> p o c", o=1).broadcast_to((P, cnt, P)),
                                    rms[:, 1, 4 * n:4 * n + cnt].rearrange("p (t o) -> p t o", o=1).broadcast_to((P, cnt, P)),
                                    ALU.mult).then_inc(s_diag, 1)

        def h_vec(dve, q, n, hooks={}):
            c0, w, v = BLOCKS[n]
            at_ = (NORM_AT[q] + n) * KT
            xn = xnA if q < 2 else xnB
            dve.wait_ge(s_bc, NORM_AT[q] + n + 1)
            for k in range(KT + 2):
                if k in hooks:
                    hooks[k]()
                if k < KT:
                    if at_ + k >= 3:
                        dve.wait_ge(s_hlo, at_ + k - 2)
                    nc.vector.scalar_tensor_tensor(xn[:, (at_ + k) % 3, 0:w], X[:, k, c0:c0 + w], gsc[:, q, v, k:k + 1],
                                                   PS[:, norm_bank(n), 0:w], ALU.mult, ALU.mult).then_inc(s_xn, 1)
                if k == 5 and n + 1 < NORM_NB[q]:
                    diag_vec(dve, q, n + 1)
                if k >= 2:
                    kk = k - 2
                    dve.wait_ge(s_hhi, at_ + kk + 1)
                    nc.vector.scalar_tensor_tensor(h_lo[:, kk, c0:c0 + w], xn[:, (at_ + kk) % 3, 0:w], shift_of(q, kk, v),
                                                   h_hi[:, kk, c0:c0 + w].bitcast(F32), ALU.add, ALU.subtract).then_inc(s_hlo, 1)

        def fold(dve, u, e, o, half, last=False):
            nc.vector.tensor_copy(e[:, 0:half + 1:half], u[:, 0:half + 1:half])
            nc.vector.tensor_tensor(e[:, 1:half], u[:, 1:half], u[:, 2 * half - 1:half:-1], ALU.add)
            ins = nc.vector.tensor_tensor(o[:, 1:half], u[:, 1:half], u[:, 2 * half - 1:half:-1], ALU.subtract)
            if last:
                ins.then_inc(s_fold, 1)

        def conv3(dve, out, src, tap, width):
            chain(dve, nc.vector.tensor_scalar(out[:, 0:width], src[:, 0:width], tap(0), None, ALU.mult))
            chain(dve, nc.vector.scalar_tensor_tensor(out[:, 0:width], src[:, 1:1 + width], tap(1), out[:, 0:width],
                                                      ALU.mult, ALU.add))
            chain(dve, nc.vector.scalar_tensor_tensor(out[:, 0:width], src[:, 2:2 + width], tap(2), out[:, 0:width],
                                                      ALU.mult, ALU.add))

        def fourier_vec(dve, g):
            y = Y[:, 4 + g, :]
            dve.wait_ge(s_ld, 2 * g + 1)
            dve.wait_ge(s_qs, 2 * g + 1)
            nc.vector.tensor_tensor(y[:, 0:512], PS[:, 6, 0:512], QS[:, 0:512], ALU.subtract).then_inc(s_fy, 1)
            nc.vector.tensor_tensor(y[:, 1023:512:-1], PS[:, 6, 1:512], QS[:, 1:512], ALU.add).then_inc(s_fy, 1)
            dve.wait_ge(s_ld, 2 * g + 2)
            dve.wait_ge(s_qs, 2 * g + 2)
            nc.vector.tensor_tensor(y[:, 1024:1152], PS[:, 6, 0:P], QS[:, 512:640], ALU.subtract).then_inc(s_fy, 1)
            nc.vector.tensor_tensor(y[:, 1279:1152:-1], PS[:, 6, 1:P], QS[:, 513:640], ALU.add).then_inc(s_fy, 1)
            nc.vector.tensor_copy(y[:, 512:513], PS[:, 6, P:P + 1]).then_inc(s_fy, 1)
            nc.vector.tensor_copy(y[:, 1152:1153], PS[:, 6, P + 1:P + 2]).then_inc(s_fy, 1)

        def mix_lo(dve):
            for n, (c0, w, _) in enumerate(BLOCKS):
                for k in range(KT):
                    dve.wait_ge(s_mhi, n * KT + k + 1)
                    nc.vector.tensor_tensor(h_lo[:, k, c0:c0 + w], Y[:, k, c0:c0 + w],
                                            h_hi[:, k, c0:c0 + w].bitcast(F32), ALU.subtract).then_inc(s_mlo, 1)

        def add_residual(dve, bank, o, c0, w, gate_):
            nc.vector.scalar_tensor_tensor(X[:, o, c0:c0 + w], PS[:, bank, 0:w], gate_, X[:, o, c0:c0 + w],
                                           ALU.mult, ALU.add).then_inc(s_res, 1)

        def ffn_vec(dve, F, ada_from=None):
            nb = F.nb
            m0 = F.layer * ADA + G2
            taps = P + F.layer * 3 * FT

            def lo(i, n, wslot):
                slot = (F.sp + 1 + n) % 2
                dve.wait_ge(s_hi, i * 6 + (F.job + n + 2))
                if wslot is None:
                    nc.vector.tensor_tensor(d_lo[:, n - 3, :], stage[:, slot, :], d_hi[:, n - 3, :].bitcast(F32),
                                            ALU.subtract).then_inc(s_lo, 1)
                else:
                    nc.vector.tensor_tensor(w_lo[:, wslot, :, :], st3[slot], w_hi[:, wslot, :, :].bitcast(F32),
                                            ALU.subtract).then_inc(s_lo, 1)

            def conv(i, half):
                dve.wait_ge(s_fg, i * (2 * nb) + (F.tiles[0] + nb * (half + 1)))
                if not (isinstance(i, int) and i == half == F.tiles[1] == 0):
                    dve.wait_ge(s_alo, i * (2 * nb) + (F.tiles[1] + nb * half))
                f = i * 2 + half
                for t_ in range(3):
                    tap = cols[:, bass.ds(f + (taps + FT * t_), 1)]
                    src = fpad[:, t_:t_ + F.cw]
                    if t_ == 0:
                        ins = nc.vector.tensor_scalar(fcv[:, 0:F.cw], src, tap, None, ALU.mult)
                    else:
                        ins = nc.vector.scalar_tensor_tensor(fcv[:, 0:F.cw], src, tap, fcv[:, 0:F.cw], ALU.mult, ALU.add)
                    if t_ < 2:
                        ins.then_inc(s_v, 1)
                        dve.wait_ge(s_v, i * 4 + (F.v0 + 2 * half + t_ + 1))
                    else:
                        ins.then_inc(s_fc, 1)

            def product(i, half):
                dve.wait_ge(s_fs, i * 2 + (F.fc0 + half + 1))
                for n in range(nb):
                    c0, w, _ = F.blocks[n]
                    s0 = c0 if n < 2 else c0 + 1
                    if isinstance(i, int) and i == half == 0:
                        dve.wait_ge(s_proj, F.proj + 2 * n + 2)
                    else:
                        dve.wait_ge(s_proj, i * (4 * nb) + (F.proj + nb * (2 * half + 1) + n + 1))
                    nc.vector.tensor_tensor(fcv[:, s0:s0 + w], fcv[:, s0:s0 + w], PS[:, 3 + n, 0:w],
                                            ALU.mult).then_inc(s_fp, 1)

            def product_lo(i, half):
                for n in range(nb):
                    c0, w, _ = F.blocks[n]
                    s0 = c0 if n < 2 else c0 + 1
                    dve.wait_ge(s_ahi, i * (2 * nb) + (F.tiles[0] + nb * half + n + 1))
                    nc.vector.tensor_tensor(a_lo[:, half, c0:c0 + w], fcv[:, s0:s0 + w],
                                            a_hi[:, half, c0:c0 + w].bitcast(F32), ALU.subtract).then_inc(s_alo, 1)

            def down(i):
                for o in range(KT):
                    for n, (c0, w, v) in enumerate(F.blocks):
                        c = o * nb + n
                        dve.wait_ge(s_down, i * (KT * nb) + (F.down - KT * nb + c + 1))
                        add_residual(dve, DOWN_BANK[n], o, c0, w, mod[:, m0 + o, v:v + 1])

            def pair(i, first):
                def ada(m):
                    if ada_from is not None:
                        ada_write(dve, i * 4 + (ada_from + m), (ada_from + m) % 2)
                if not first:
                    lo(i, 0, 1 - F.ws)
                    ada(-1)
                conv(i, 0)
                lo(i, 1, F.ws)
                product(i, 0)
                lo(i, 2, 1 - F.ws)
                if not first:
                    down(i)
                product_lo(i, 0)
                lo(i, 3, None)
                lo(i, 4, None)
                ada(0)
                conv(i, 1)
                lo(i, 5, F.ws)
                ada(1)
                product(i, 1)
                ada(2)
                product_lo(i, 1)
            for c_ in (0, 1025, TOK + 2):
                chain(dve, nc.vector.memset(fpad[:, c_:c_ + 1], 0.0))
            F.v0 = vn[0]
            pair(0, True)
            with dve.Fori(1, PAIRS) as i:
                pair(i, False)
            vn[0] += 4 * PAIRS
            if ada_from is not None:
                ada_write(dve, ada_from + 4 * PAIRS - 1)
            if F.layer == 1:
                down(PAIRS)
                return
            gains_vec(dve, 2)
            for n in range(2):
                lo_job(dve, J_ODD + n, (n + 1) % 2)
            for c in range(KT * nb):
                n, o = divmod(c, KT)
                c0, w, v = F.blocks[n]
                dve.wait_ge(s_down, PAIRS * (KT * nb) - KT * nb + c + 1)
                add_residual(dve, c % 3, o, c0, w, mod[:, m0 + o, v:v + 1])
                if c:
                    sum_vec(dve, 2, (c - 1) % KT, (c - 1) // KT)
                if c == 12:
                    diag_vec(dve, 2, 0)
            sum_vec(dve, 2, KT - 1, nb - 1)


        C_QA, C_KA, C_VA, C_QM, C_KM, C_VM, C_OM, C_G = 0, 512, 640, 768, 1024, 1280, 1792, 2304
        odd_tiles = ([("ka", 0), ("va", 0), ("g", 0)] + [("qa", j) for j in range(4)] + [("km", j) for j in range(2)]
                     + [("vm", j) for j in range(4)] + [("qm", j) for j in range(2)] + [("om", j) for j in range(4)])
        odd_nb = [2 if t in ("qa", "qm", "om") else 3 for t, _ in odd_tiles]
        odd_cum = [0]
        for n_ in odd_nb:
            odd_cum.append(odd_cum[-1] + n_)
        NODD = len(odd_tiles)
        J_ODD = J_FFN0 + 6 * PAIRS + 1
        odd_job = [J_ODD + n if n < 2 else J_ODD + n - 1 for n in range(NODD)]
        odd_job[2] = None
        J_OUT1 = J_ODD + NODD - 1
        J_FFN1 = J_OUT1 + KT
        PR_ODD = 3 * J_FFN0 + 12 * PAIRS
        PR_OUT1 = PR_ODD + odd_cum[-1]
        PR_FFN1 = PR_OUT1 + 2 * KT
        PEV_ODD = 24
        RES_OUT1 = RES_FFN0 + 2 * KT
        RES_END = RES_OUT1 + PAIRS * KT * 2
        LAT = BLOCKS[:2]
        F1 = Ffn(1, J_FFN1, LAT, PR_FFN1, RES_OUT1, PAIRS * KT * 3, (6 * PAIRS, 6 * PAIRS), 0)
        F1.fc0, F1.cw = 2 * PAIRS, SEQ

        s_gz = sem("gate_weights_zeroed")
        s_gw = sem("gate_weights_loaded")
        s_ghl = sem("gate_weights_hi")
        s_gll = sem("gate_weights_lo")
        s_small = sem("small_columns_loaded")
        s_vt = sem("v_transposed")
        s_vc = sem("v_copied")
        s_rtab = sem("rope_tables_loaded")
        s_ones = sem("pads_written")
        s_amk = sem("attention_masks_loaded")
        s_kbd = sem("head_sum_table_loaded")
        s_kq = sem("key_square")
        s_ks = sem("key_sum")
        s_kr = sem("key_root")
        s_kn = sem("key_normalised")
        s_rg = sem("rope_gain_folded")
        s_rc = sem("rope_cosine_part")
        s_ro = sem("rope_rotated")
        s_rd = sem("rope_done")
        s_rq = sem("query_square")
        s_rs = sem("query_sums_by_token")
        s_rr = sem("query_root")
        s_ri = sem("query_scales_written")
        s_kctx = sem("context_keys_copied")
        s_sl = sem("block_operands_copied")
        s_slv = sem("block_values_copied")
        s_slr = sem("block_scales_copied")
        s_S = sem("scores_ready")
        s_nm = sem("score_max_ready")
        s_ex = sem("probs_ready")
        s_pn = sem("probs_normalised")
        s_pt = sem("probs_transposed")
        s_pcA = sem("probs_copied_scalar")
        s_pcV = sem("probs_copied_vector")
        s_O = sem("attention_out_ready")
        s_yA = sem("attention_hi")
        s_yV = sem("attention_lo")
        s_att = sem("attention_chain")
        s_tick = sem("attention_scores_waited_for")
        s_rst = sem("row_tables_loaded")
        s_g1 = sem("log_gate_part")
        s_gexp = sem("gate_rows_exponentiated")
        s_gx = sem("gate_exponents_made")
        s_gt = sem("gate_rows_transposed")
        s_gc = sem("gate_columns_copied")
        s_mA = sem("mlstm_scores_ready")
        s_mB = sem("mlstm_exponents_made")
        s_mC = sem("mlstm_exponentiated")
        s_mD = sem("mlstm_weights_made")
        s_mE = sem("mlstm_out_ready")
        s_wv = sem("mlstm_values_weighted")
        s_mF = sem("mlstm_out_read")
        s_fT = sem("mlstm_out_transposed")
        s_fm = sem("mlstm_gated")
        s_fhi = sem("mlstm_mix_hi")
        s_flo = sem("mlstm_mix_lo")
        s_qh = [sem("query_half_loaded0"), sem("query_half_loaded1")]
        s_wo = [sem("out_rows_loaded0"), sem("out_rows_loaded1")]
        s_oT = sem("out_transposed")
        s_ocA = sem("out_copied_scalar")
        s_ocV = sem("out_copied_vector")
        s_act = sem("scalar_chain")
        an = [0]

        def achain(act, ins):
            an[0] += 1
            ins.then_inc(s_act, 1)
            act.wait_ge(s_act, an[0])

        def odd_view(kind, j):
            w = a["odd_w_in"][0]
            c = {"ka": C_KA, "va": C_VA, "qm": C_QM, "km": C_KM, "vm": C_VM, "om": C_OM}[kind] + j * P
            return w[:, c:c + P].rearrange("(k p) c -> p k c", p=P)

        def layer1_loads(sp):
            for n in range(NODD):
                j = odd_job[n]
                if j is None:
                    sp.wait_ge(s_hlo, 9 * KT)
                    sp.dma_start(kbd[:, :], a["rope_tables"][:, 2176:2304]).then_inc(s_kbd, 16)
                    continue
                kind, t = odd_tiles[n]
                sp.wait_ge(s_lo, j - 1)
                if kind == "qa":
                    wq = a["odd_w_in"][0][:, 0:512].rearrange("(k p) c -> p k c", p=P)
                    sp.dma_start(st3[j % 2][:, :, 0:64], wq[:, :, 64 * t:64 * t + 64]).then_inc(s_qh[j % 2], 16)
                    sp.dma_start(st3[j % 2][:, :, 64:128], wq[:, :, 256 + 64 * t:320 + 64 * t]).then_inc(s_stage[j % 2], 16)
                else:
                    sp.dma_start(st3[j % 2], odd_view(kind, t)).then_inc(s_stage[j % 2], 16)
                if n == 1:
                    sp.wait_ge(s_res, RES_FFN0 - KT)
                    sp.dma_start(xs[:, :, 0:SEQ], X[:, :, 0:SEQ]).then_inc(s_spill, 16)
            sp.wait_ge(s_proj, PR_OUT1)
            sp.dma_start(rtab[:, :], a["rope_tables"]).then_inc(s_rtab, 16)
            sp.dma_start(amask[:, :, :], a["att_masks"]).then_inc(s_amk, 16)
            sp.wait_ge(s_yV, 8)
            sp.dma_start(R_rst[0:64, :], a["scan_resets"]).then_inc(s_rst, 16)
            sp.dma_start(sel[:, :, :], a["row_select"]).then_inc(s_rst, 16)
            sp.dma_start(mm_mask[:, :, :], a["mlstm_masks"]).then_inc(s_rst, 16)
            for o in range(KT):
                if o == 2:
                    sp.wait_ge(s_fT, 8)
                    sp.dma_start(X[:, :, 0:SEQ], xs[:, :, 0:SEQ]).then_inc(s_back, 16)
                j = J_OUT1 + o
                w = a["odd_w_out"][0][:, o * P:(o + 1) * P]
                sp.wait_ge(s_lo, j - 1)
                for h in range(2):
                    sp.dma_start(st3[j % 2][64 * h:64 * h + 64, 0:4, :],
                                 w[256 * h:256 * h + 256, :].rearrange("(t d) c -> d t c", t=4)).then_inc(s_wo[j % 2], 16)
                sp.dma_start(st3[j % 2][:, 4:8, :], w[512:1024, :].rearrange("(k p) c -> p k c", p=P)).then_inc(s_stage[j % 2], 16)
            ffn_loads(sp, F1)
            for t in range(8):
                sp.wait_ge(s_ocA, t + 1)
                sp.wait_ge(s_ocV, t + 1)
                sp.dma_start(a["out"][0, t * P:(t + 1) * P, :], out_tm[:, t, :]).then_inc(s_out, 16)
            sp.wait_ge(s_out, 8 * 16)

        def layer1_pool(gp):
            for n, (dst, src) in enumerate((
                    (sink[:, :], a["odd_sink"][0:1, :].broadcast_to((P, 8))),
                    (head_g[0:64, 0:1], a["odd_q_g"].rearrange("a d -> d a")), (head_g[64:128, 0:1], a["odd_q_g"].rearrange("a d -> d a")),
                    (head_g[0:64, 1:2], a["odd_k_g"].rearrange("a d -> d a")), (head_g[64:128, 1:2], a["odd_k_g"].rearrange("a d -> d a")))):
                gp.dma_start(dst, src).then_inc(s_small, 16)
            gp.memset(gate_b[:, :], 0.0).then_inc(s_gz, 1)
            gp.wait_ge(s_down, PAIRS * KT * 3)
            gp.wait_ge(s_res, RES_FFN0)
            gp.memset(gw[:, :, :], 0.0).then_inc(s_gz, 1)
            gp.wait_ge(s_gz, 2)
            for q, row in enumerate((0, 64, 32, 96)):
                gp.dma_start(gw[:, :, row:row + 4],
                             a["odd_w_in"][0][:, C_G + 4 * q:C_G + 4 * q + 4].rearrange("(k p) c -> p k c", p=P)).then_inc(s_gw, 16)
                gp.dma_start(gate_b[row:row + 4, :], a["odd_gate_b"][0, q:q + 1, :].rearrange("a h -> h a")).then_inc(s_gw, 16)
            gp.wait_ge(s_rtab, 16)
            gp.wait_ge(s_kn, 3)
            gp.wait_ge(s_pevA, PEV_ODD + odd_cum[-1])
            for u, (src, c0, _, _) in enumerate(rope_units):
                if u >= 2:
                    gp.wait_ge(s_rd, u - 1)
                gp.tensor_tensor(rt[u % 2][:, :], src, COS[:, c0:c0 + 512], ALU.mult).then_inc(s_rc, 1)
            gp.wait_ge(s_rd, 2)
            gp.tensor_copy(k_s[:, 384:640], kA[:, 1024:1280]).then_inc(s_kctx, 1)
            gp.wait_ge(s_kctx, 1)
            gp.wait_ge(s_vc, 3)
            gp.tensor_copy(v_s[:, 3:5, :], vAt[:, 10:12, :]).then_inc(s_kctx, 1)
            gp.memset(q_s[:, :, :], 0.0).then_inc(s_kctx, 1)
            gp.wait_ge(s_kctx, 3)
            gp.wait_ge(s_rd, 10)
            gp.wait_ge(s_ri, 2)

            def block_copies(b, first):
                if not first:
                    gp.wait_ge(s_S, b * 8)
                    gp.wait_ge(s_slv, b)
                for kv in range(2):
                    r = slice(64 * kv, 64 * kv + 64)
                    if kv:
                        gp.wait_ge(s_sl, b * 3 + 1)
                    gp.tensor_copy(q_s[r, 4 * kv:4 * kv + 4, :], qA[r, :, bass.ds(b * P, P)]).then_inc(s_sl, 1)
                gp.wait_ge(s_sl, b * 3 + 2)
                gp.tensor_copy(k_s[:, 0:384], kP[:, bass.ds(b * P, 384)]).then_inc(s_sl, 1)
                if not first:
                    gp.wait_ge(s_ex, b * 16)
                gp.tensor_copy(rq_s[:, :, :], rq[:, 0:2, bass.ds(b * 8, 8)]).then_inc(s_slr, 1)
                if not first:
                    gp.wait_ge(s_O, b * 4)
                gp.tensor_copy(v_s[:, 0:3, :], vAt[:, bass.ds(b, 3), :]).then_inc(s_slv, 1)
            block_copies(0, True)
            with gp.Fori(1, 8) as b:
                block_copies(b, False)

        def layer1_pe(pe):
            first_pair(pe, 2, ((s_lo, J_ODD + 1), (s_lo, J_ODD + 2)), (1, 0), ((s_res, RES_FFN0), (s_fp, 6 * PAIRS)))
            pend = (1, 0)
            for n in range(2, NODD):
                if odd_job[n] is None:
                    pe.wait_ge(s_gll, 1)
                else:
                    pe.wait_ge(s_lo, odd_job[n] + 1)
                for b in range(odd_nb[n]):
                    pe.wait_ge(s_pevA, PEV_ODD + odd_cum[n - 2] + min(b + 1, odd_nb[n - 2]))
                    block_mm(pe, BLOCKS[b], 3 * (n % 2) + b, (n + 1) % 2)
                if pend is not None:
                    if pend[1] == 1:
                        pe.wait_ge(s_kr, 3)
                    v_transposes(pe, *pend)
                if n in (3, 5, 7):
                    u, w = (n - 3) // 2, KN[(n - 3) // 2][1]
                    if u == 0:
                        pe.wait_ge(s_kbd, 16)
                        pe.wait_ge(s_vc, 3)
                    pe.wait_ge(s_kq, u + 1)
                    if u:
                        pe.wait_ge(s_kr, u)
                    nc.tensor.matmul(PS[:, 7, 0:w], kbd[:, :], kt[:, 0:w], start=True, stop=True).then_inc(s_ks, 1)
                pend = (n, V_TILES.index(n)) if n in V_TILES else None
            rope_pe(pe)
            att_pe(pe, 0, True)
            with pe.Fori(1, 8) as i:
                att_pe(pe, i, False)
            mlstm_pe(pe)
            for o in range(KT):
                pe.wait_ge(s_lo, J_OUT1 + o + 1)
                for n in range(2):
                    if o < 2:
                        pe.wait_ge(s_fm, 8)
                        pe.wait_ge(s_mF, MF_END)
                    else:
                        pe.wait_ge(s_res, RES_FFN0 + 2 * (o - 2) + n + 1)
                    if o == 0 and n == 0:
                        pe.wait_ge(s_yV, 8)
                        pe.wait_ge(s_flo, 8)
                    block_mm(pe, LAT[n], 3 * (o % 2) + n, o % 2)
            norm_cols(pe, 3, 0)
            norm_bcast(pe, 3, 0)
            norm_cols(pe, 3, 1)
            ffn_pe(pe, F1)
            for t in range(8):
                for half in range(2):
                    g = 2 * t + half
                    if g == 0:
                        pe.wait_ge(s_res, RES_END)
                    if g < 6:
                        pe.wait_ge(s_fp, 6 * PAIRS + 4 * PAIRS)
                    else:
                        pe.wait_ge(s_ocA if g % 2 == 0 else s_ocV, (g - 6) // 2 + 1)
                    for k in range(4):
                        last = nc.tensor.transpose(PS[:, g % 6, k * P:(k + 1) * P], X[:, 4 * half + k, t * P:(t + 1) * P], ident[:, :])
                    last.then_inc(s_oT, 1)

        V_TILES = [n for n, (k, _) in enumerate(odd_tiles) if k in ("va", "vm")]
        V_GROUPS = ((0, 4), (4, 4), (8, 2))

        def v_transposes(pe, n, q):
            pe.wait_ge(s_pevA, PEV_ODD + odd_cum[n + 1])
            for g, (t0, cnt) in enumerate(V_GROUPS):
                u = 3 * q + g
                if u >= 2:
                    pe.wait_ge(s_vc, u - 1)
                else:
                    pe.wait_ge(s_xn, 9 * KT)
                for t in range(cnt):
                    last = nc.tensor.transpose(PS[:, 6 + u % 2, t * P:(t + 1) * P], vtmp[:, (t0 + t) * P:(t0 + t + 1) * P], ident[:, :])
                last.then_inc(s_vt, 1)

        KN = ((0, 512), (512, 512), (1024, 256))

        rope_units = [(kA[:, c0:c0 + 512], c0, kP[:, P + c0:P + c0 + 512], None) for c0 in (0, 512)]
        for t in range(4):
            for c0 in (0, 512):
                rope_units.append((qA[:, t, c0:c0 + 512], c0, qA[:, t, c0:c0 + 512], t))

        def rope_pe(pe):
            pe.wait_ge(s_rtab, 16)
            pe.wait_ge(s_kn, 3)
            pe.wait_ge(s_pevA, PEV_ODD + odd_cum[-1])
            for u, (src, c0, _, t) in enumerate(rope_units):
                if u >= 2:
                    pe.wait_ge(s_rd, u - 1)
                elif u == 0:
                    pe.wait_ge(s_vc, 15)
                if t == 0:
                    pe.wait_ge(s_rg, 1)
                nc.tensor.matmul(PS[:, u % 2, :], ROT if t is None else rotg[:, :], src, start=True, stop=True).then_inc(s_ro, 1)
                if t is not None:
                    pe.wait_ge(s_rq, u - 1)
                    for c in range(4):
                        col = (c0 // P + c) * 8 + t
                        last = nc.tensor.matmul(PS[:, 2, col:col + 5:4], rt[3 + u % 2][:, c * P:(c + 1) * P], BD[:, 0:65:64],
                                                start=True, stop=True)
                    last.then_inc(s_rs, 1)

        def att_pe(pe, i, first):
            pe.wait_ge(s_sl, i * 3 + 3)
            if first:
                pe.wait_ge(s_kctx, 3)

            def scores(u):
                if not (first and u < 2):
                    pe.wait_ge(s_nm, i * 8 + (u - 1))
                elif u == 0:
                    pe.wait_ge(s_rr, 1)
                    pe.wait_ge(s_rd, 10)
                for c in range(2):
                    last = nc.tensor.matmul(PS[:, 2 * (u % 2) + c, 0:320], q_s[:, u, :],
                                            k_s[:, 320 * c:320 * c + 320], start=True, stop=True)
                last.then_inc(s_S, 1)

            def outputs(g):
                kv, j = divmod(2 * g, 4)
                pe.wait_ge(s_pcA, i * 8 + (2 * g + 2))
                pe.wait_ge(s_pcV, i * 8 + (2 * g + 2))
                if g == 0:
                    pe.wait_ge(s_slv, i + 1)
                    if not first:
                        pe.wait_ge(s_yV, i)
                for t in range(5):
                    last = nc.tensor.matmul(PS[64 * kv:64 * kv + 64, 7, j * P:(j + 2) * P],
                                            v_s[:, t, 64 * kv:64 * kv + 64], pT[:, g % 2, t, :],
                                            start=(t == 0), stop=(t == 4))
                last.then_inc(s_O, 1)

            scores(0)
            scores(1)
            for u in range(8):
                if u + 2 < 8:
                    scores(u + 2)
                pe.wait_ge(s_pn, i * 8 + (u + 1))
                if not (first and u < 2):
                    pe.wait_ge(s_pcA, i * 8 + (u - 1))
                if not (first and u < 1):
                    pe.wait_ge(s_pcV, i * 8 + u)
                for t in range(5):
                    dst = PS[:, 4 + u % 2, t * P:(t + 1) * P] if t < 4 else PS[:, 6, (u % 2) * P:(u % 2 + 1) * P]
                    last = nc.tensor.transpose(dst, pr[:, u % 3, t * P:(t + 1) * P], ident[:, :])
                last.then_inc(s_pt, 1)
                if u >= 2 and u % 2 == 0:
                    outputs(u // 2 - 1)
            outputs(3)

        m_units = []
        for st_ in range(10):
            m_units.append((0, 8 + st_ if st_ < 2 else st_ - 2, st_ >= 2))
            m_units.append((1, 9 - st_, st_ >= 2))
        m_out = [n for n, u in enumerate(m_units) if u[2]]
        MF_END = len(m_units)

        def mlstm_pe(pe):
            pe.wait_ge(s_gexp, 4)
            pe.wait_ge(s_yV, 8)
            srcs = [R_a, R_fl, R_del]
            for q in range(30):
                if q % 8 == 0 and q >= 16:
                    pe.wait_ge(s_gc, q // 8 - 1)
                kind, c = divmod(q, 10)
                last = nc.tensor.transpose(PS[:, (q // 8) % 2, (q % 8) * 64:(q % 8) * 64 + 64],
                                           srcs[kind][0:64, c * P:(c + 1) * P], ident[0:64, 0:64])
                if q % 8 == 7 or q == 29:
                    last.then_inc(s_gt, 1)
            pe.wait_ge(s_rst, 48)
            for dp in range(4):
                last = nc.tensor.matmul(PS[:, 2, dp * 10:dp * 10 + 10], sel[:, 8 + dp, :], m_rows[:, 2, :], start=True, stop=True)
            last.then_inc(s_gt, 1)
            for g in range(5):
                if g >= 3:
                    pe.wait_ge(s_gc, 5 + g - 2)
                for q in range(4 * g, 4 * g + 4):
                    t, c = divmod(q, 10)
                    last = nc.tensor.transpose(PS[:, 3 + g % 3, (q % 4) * P:(q % 4 + 1) * P], kM[:, t, c * P:(c + 1) * P], ident[:, :])
                last.then_inc(s_gt, 1)
            pe.wait_ge(s_gc, 10)
            order = []
            for n in range(len(m_units) + 1):
                if n < len(m_units) and m_units[n][2]:
                    order.append(("A", n))
                if n >= 1:
                    order.append(("E", n - 1))
            for what, n in order:
                d, c, _ = m_units[n]
                o = m_out.index(n) if n in m_out else None
                if what == "A":
                    if o:
                        pe.wait_ge(s_mD, 2 * o)
                    cs = slice(c * P, (c + 1) * P)
                    for h in range(4):
                        r0 = 64 * (h % 2)
                        nc.tensor.matmul(PS[:, h % 2, (h // 2) * P:(h // 2 + 1) * P], kM[r0:r0 + 64, h // 2, cs],
                                         qM[r0:r0 + 64, h // 2, cs], start=True, stop=True)
                    for p2 in range(2):
                        nc.tensor.matmul(PS[:, 0, 256 + p2 * P:256 + (p2 + 1) * P], sel[:, 8 + 2 * d + p2, :],
                                         R_rst[0:64, cs], start=True, stop=True)
                    for h in range(4):
                        last = nc.tensor.matmul(PS[:, 2, h * P:(h + 1) * P], sel[:, 4 * d + h, :], R_b[0:64, cs], start=True, stop=True)
                    last.then_inc(s_mA, 1)
                else:
                    nb0 = 3 + 2 * d
                    if n >= 2:
                        pe.wait_ge(s_mF, n - 1)
                    pe.wait_ge(s_wv, 4 * (n + 1))
                    if o is not None:
                        pe.wait_ge(s_mD, 2 * o + 2)
                        pe.wait_ge(s_mF, n - 1)
                        for h in range(4):
                            r0 = 64 * (h % 2)
                            dst = PS[:, nb0 + h % 2, (h // 2) * 129:(h // 2 + 1) * 129]
                            nc.tensor.matmul(dst, WT[:, d, h, :], vMt[:, c, h, :], start=True, stop=False)
                            nc.tensor.matmul(dst, qt[r0:r0 + 64, d, h // 2, :], C[r0:r0 + 64, 2 * d + h // 2, :], start=False, stop=True)
                    for h in range(4):
                        r0 = 64 * (h % 2)
                        last = nc.tensor.matmul(PS[r0:r0 + 64, nb0 + h // 2, 258:387], kMt[:, c, h * 64:h * 64 + 64],
                                                wv[:, d, h, :], start=True, stop=True)
                    last.then_inc(s_mE, 1)
            pe.wait_ge(s_mF, MF_END)
            for c in range(8):
                if c >= 2:
                    pe.wait_ge(s_fm, c - 1)
                for h in range(4):
                    last = nc.tensor.transpose(PS[:, c % 2, h * P:(h + 1) * P], hsum[:, c, h * P:(h + 1) * P], ident[:, :])
                last.then_inc(s_fT, 1)

        def layer1_act(act):
            for n in range(3):
                h_act(act, 2, n)
            act.wait_ge(s_small, 5 * 16)
            for n, (kind, t) in enumerate(odd_tiles):
                if 1 <= n and n + 1 < NODD:
                    used = PR_ODD + (5 if n == 1 else odd_cum[n])
                    if odd_job[n + 1] is None:
                        act.wait_ge(s_gw, 8 * 16)
                        act.wait_ge(s_proj, used)
                        nc.scalar.activation(w_hi[:, n % 2, :, :], gw[:, :, :], ACT.Copy).then_inc(s_ghl, 1)
                    else:
                        if odd_tiles[n + 1][0] == "qa":
                            act.wait_ge(s_qh[odd_job[n + 1] % 2], 16 * (odd_tiles[n + 1][1] // 2 + 1))
                        hi_job(act, odd_job[n + 1], w_hi[:, n % 2, :, :], used)
                for b in range(odd_nb[n]):
                    c0, w, _ = BLOCKS[b]
                    if b == 0 and n in (4, 6, 8):
                        u = (n - 4) // 2
                        w_ = KN[u][1]
                        act.wait_ge(s_ks, u + 1)
                        nc.scalar.activation(kt[:, 0:w_], PS[:, 7, 0:w_], ACT.Sqrt, bias=eps_t[:, 0:1], scale=1.0 / 64).then_inc(s_kr, 1)
                    if b == 0 and n in (3, 5, 7):
                        u = (n - 3) // 2
                        k0, w_ = KN[u]
                        if u:
                            act.wait_ge(s_kn, u)
                        else:
                            act.wait_ge(s_pevA, PEV_ODD + 3)
                            act.wait_ge(s_hlo, 9 * KT)
                        nc.scalar.activation(kt[:, 0:w_], kA[:, k0:k0 + w_], ACT.Square).then_inc(s_kq, 1)
                    if n == 3 and b == 0:
                        act.wait_ge(s_spill, 32)
                        act.wait_ge(s_hlo, 9 * KT)
                    if kind == "qm" and t == 0 and b == 0:
                        act.wait_ge(s_gll, 1)
                    if n in V_TILES and V_TILES.index(n) and b == 0:
                        act.wait_ge(s_vt, 3 * V_TILES.index(n))
                    act.wait_ge(s_proj, PR_ODD + (2 * b + n + 1 if n < 2 else odd_cum[n] + b + 1))
                    src = PS[:, 3 * (n % 2) + b, 0:w]
                    if kind == "g":
                        ins = nc.scalar.activation(G[:, c0:c0 + w], src, ACT.Identity, bias=gate_b[:, 0:1])
                    elif kind == "om":
                        ins = nc.scalar.activation(oM[:, t, c0:c0 + w], src, ACT.Sigmoid)
                    elif kind == "km":
                        ins = nc.scalar.activation(kM[:, t, c0:c0 + w], src, ACT.Copy, scale=0.125)
                    else:
                        dst = {"ka": kA[:, c0:c0 + w], "qa": qA[:, t, c0:c0 + w] if b < 2 else None, "va": vtmp[:, c0:c0 + w],
                               "vm": vtmp[:, c0:c0 + w], "qm": qM[:, t % 2, c0:c0 + w] if b < 2 else None}[kind]
                        ins = nc.scalar.activation(dst, src, ACT.Copy)
                    ins.then_inc(s_pevA, 1)
            act.wait_ge(s_proj, PR_OUT1)
            act.wait_ge(s_pevA, PEV_ODD + odd_cum[-1])
            for u, (src, _, _, t) in enumerate(rope_units[2:]):
                if u >= 2:
                    act.wait_ge(s_rs, u - 1)
                nc.scalar.activation(rt[3 + u % 2][:, :], src, ACT.Square).then_inc(s_rq, 1)
            act.wait_ge(s_rs, 8)
            nc.scalar.activation(rq[:, 2, :], PS[:, 2, 0:64], ACT.Sqrt, bias=eps_t[:, 0:1], scale=1.0 / 64).then_inc(s_rr, 1)
            att_act(act, 0, True)
            with act.Fori(1, 8) as i:
                att_act(act, i, False)
            att_hi(act, 8)
            mlstm_act(act)
            out_hi(act, 0)
            for o in range(KT):
                if o + 1 < KT:
                    out_hi(act, o + 1)
                else:
                    hi_job(act, F1.job, w_hi[:, F1.ws, :, :], PR_OUT1 + 14)
                for n in range(2):
                    sq_act(act, 3, o, n)
            root_act(act, 3, 0)
            root_act(act, 3, 1)
            h_act(act, 3, 0, {3: lambda: hi_job(act, F1.job + 1, w_hi[:, 1 - F1.ws, :, :], PR_FFN1)})
            h_act(act, 3, 1)
            ffn_act(act, F1)
            for g in range(0, 16, 2):
                act.wait_ge(s_oT, g + 1)
                nc.scalar.activation(out_tm[:, g // 2, 0:512], PS[:, g % 6, :], ACT.Copy).then_inc(s_ocA, 1)

        def out_hi(act, o):
            j = J_OUT1 + o
            act.wait_ge(s_wo[j % 2], 32 * (sum(1 for x in range(o + 1) if (J_OUT1 + x) % 2 == j % 2)))
            hi_job(act, j, w_hi[:, o % 2, :, :], PR_OUT1 - odd_nb[-1] if o == 0 else PR_OUT1 + 2 * (o - 1))

        def att_act(act, i, first):
            def exps(u):
                act.wait_ge(s_nm, i * 8 + (u + 1))
                nc.scalar.activation(st8[:, u, 2:3], sink[:, u:u + 1], ACT.Exp, bias=st8[:, u, 1:2]).then_inc(s_ex, 1)
                nc.scalar.activation(pr[:, u % 3, :], pr[:, u % 3, :], ACT.Exp, bias=st8[:, u, 1:2], scale=rq_s[:, 0, u:u + 1],
                                     accum_out=st8[:, u, 3:4]).then_inc(s_ex, 1)
            exps(0)
            exps(1)
            if not first:
                att_hi(act, i)
            for u in range(8):
                act.wait_ge(s_pt, i * 8 + (u + 1))
                g = u // 2
                if not (first and g < 2):
                    act.wait_ge(s_O, i * 4 + (g - 1))
                nc.scalar.activation(pT[:, g % 2, 0:4, (u % 2) * P:(u % 2 + 1) * P],
                                     PS[:, 4 + u % 2, :].rearrange("p (t q) -> p t q", t=4), ACT.Copy).then_inc(s_pcA, 1)
                if u + 2 < 8:
                    exps(u + 2)

        def att_hi(act, i):
            act.wait_ge(s_O, i * 4)
            nc.scalar.activation(h_hi[:, 0:4, bass.ds(i * P - P, P)], PS[:, 7, :].rearrange("p (j q) -> p j q", j=4),
                                 ACT.Copy).then_inc(s_yA, 1)

        def mlstm_act(act):
            act.wait_ge(s_yV, 8)
            achain(act, nc.scalar.activation(R_b[64:128, :], G[64:128, :], ACT.Abs))
            achain(act, nc.scalar.activation(R_b[64:128, :], R_b[64:128, :], ACT.Exp, scale=-1.0))
            nc.scalar.activation(R_b[64:128, :], R_b[64:128, :], ACT.Ln, bias=ones[64:128, 0:1]).then_inc(s_g1, 1)
            for n, (t, sc) in enumerate(((R_rst, 1.0), (R_fl, 1.0), (R_del, -1.0))):
                act.wait_ge(s_gx, n + 1)
                nc.scalar.activation(t[0:64, :], t[0:64, :], ACT.Exp, scale=sc).then_inc(s_gexp, 1)
            act.wait_ge(s_gx, 4)
            nc.scalar.activation(m_rows[:, 2, :], m_rows[:, 2, :], ACT.Exp).then_inc(s_gexp, 1)
            for g in range(10):
                act.wait_ge(s_gt, g + 1)
                if g < 4:
                    cnt = 8 if g < 3 else 6
                    src = PS[:, g % 2, 0:cnt * 64].rearrange("p (s d r) -> p s d r", s=cnt, d=2)[:, :, :, 0:4]
                    nc.scalar.activation(gcol[:, 8 * g:8 * g + cnt, :].rearrange("p s (d r) -> p s d r", d=2), src,
                                         ACT.Copy).then_inc(s_gc, 1)
                elif g == 4:
                    nc.scalar.activation(dec_bc[:, :, :], PS[:, 2, 0:40].rearrange("p (d c) -> p d c", d=4), ACT.Copy).then_inc(s_gc, 1)
                else:
                    for q in range(4):
                        t, c = divmod(4 * (g - 5) + q, 10)
                        ins = nc.scalar.activation(kMt[:, c, t * P:(t + 1) * P], PS[:, 3 + (g - 5) % 3, q * P:(q + 1) * P], ACT.Copy)
                    ins.then_inc(s_gc, 1)
            act.wait_ge(s_gc, 10)

            def values(n):
                d, c, _ = m_units[n]
                if n >= 2:
                    act.wait_ge(s_mE, n - 1)
                for h in range(4):
                    nc.scalar.activation(wv[:, d, h, :], vMt[:, c, h, :], ACT.Copy,
                                         scale=gcol[:, 10 + c, 4 * d + h:4 * d + h + 1]).then_inc(s_wv, 1)
            act.wait_ge(s_ones, 5)
            for n in range(len(m_units) + 1):
                if n < len(m_units):
                    d, c, out = m_units[n]
                    values(n)
                    if out:
                        o = m_out.index(n)
                        act.wait_ge(s_mB, 4 * (o + 1))
                        nc.scalar.activation(XE[:, d, :, :], XE[:, d, :, :], ACT.Exp).then_inc(s_mC, 1)
            for c in range(8):
                act.wait_ge(s_fm, c + 1)
                nc.scalar.activation(h_hi[:, 4:8, c * P:(c + 1) * P], gated(c), ACT.Copy).then_inc(s_fhi, 1)

        def gated(c):
            return XE[:, c % 2, :, :]

        def layer1_vec(dve):
            for n in range(3):
                h_vec(dve, 2, n)
            dve.wait_ge(s_spill, 32)
            dve.wait_ge(s_hlo, 9 * KT)
            nc.vector.memset(vMt[:, :, :, 128:129], 1.0).then_inc(s_ones, 1)
            nc.vector.memset(vAt[:, 0:1, :], 0.0).then_inc(s_ones, 1)
            nc.vector.memset(vAt[:, 9:10, :], 0.0).then_inc(s_ones, 1)
            for n in range(1, NODD):
                if n + 1 < NODD and odd_job[n + 1] is None:
                    dve.wait_ge(s_ghl, 1)
                    nc.vector.tensor_tensor(w_lo[:, n % 2, :, :], gw[:, :, :], w_hi[:, n % 2, :, :].bitcast(F32),
                                            ALU.subtract).then_inc(s_gll, 1)
                elif n + 1 < NODD:
                    lo_job(dve, odd_job[n + 1], n % 2)
                if n in (4, 6, 8):
                    u = (n - 4) // 2
                    k0, w_ = KN[u]
                    dve.wait_ge(s_kr, u + 1)
                    chain(dve, nc.vector.reciprocal(kt[:, 0:w_], kt[:, 0:w_]))
                    nc.vector.scalar_tensor_tensor(kA[:, k0:k0 + w_], kA[:, k0:k0 + w_], head_g[:, 1:2], kt[:, 0:w_],
                                                   ALU.mult, ALU.mult).then_inc(s_kn, 1)
                if n - 1 in V_TILES:
                    q = V_TILES.index(n - 1)
                    for g, (t0, cnt) in enumerate(V_GROUPS):
                        dve.wait_ge(s_vt, 3 * q + g + 1)
                        src = PS[:, 6 + (3 * q + g) % 2, 0:cnt * P].rearrange("p (t c) -> p t c", t=cnt)
                        if q == 0:
                            r0 = (1, 5, 10)[g]
                            dst = vAt[:, r0:r0 + cnt, :]
                        else:
                            dst = vMt[:, t0:t0 + cnt, q - 1, 0:P]
                        nc.vector.tensor_copy(dst, src).then_inc(s_vc, 1)
            dve.wait_ge(s_proj, PR_OUT1)
            nc.vector.memset(kP[:, 0:P], 0.0).then_inc(s_ones, 1)
            nc.vector.memset(kP[:, P + SEQ:2 * P + SEQ], 0.0).then_inc(s_ones, 1)
            dve.wait_ge(s_rtab, 16)
            dve.wait_ge(s_small, 5 * 16)
            nc.vector.tensor_scalar(rotg[:, :], ROT, head_g[:, 0:1], None, ALU.mult).then_inc(s_rg, 1)
            chain(dve, nc.vector.tensor_scalar(nsink[:, :], sink[:, :], -1.0, None, ALU.mult))
            for u, (_, c0, dst, t) in enumerate(rope_units):
                if u:
                    dve.wait_ge(s_rd, u)
                dve.wait_ge(s_ro, u + 1)
                chain(dve, nc.vector.tensor_tensor(rt[2][:, :], PS[:, u % 2, :], SIN[:, c0:c0 + 512], ALU.mult))
                dve.wait_ge(s_rc, u + 1)
                if t is None:
                    nc.vector.tensor_tensor(dst, rt[u % 2][:, :], rt[2][:, :], ALU.add).then_inc(s_rd, 1)
                else:
                    dve.wait_ge(s_rq, u - 1)
                    nc.vector.scalar_tensor_tensor(dst, rt[u % 2][:, :], head_g[:, 0:1], rt[2][:, :], ALU.mult, ALU.add).then_inc(s_rd, 1)
            dve.wait_ge(s_rr, 1)
            chain(dve, nc.vector.reciprocal(rq[:, 1, :], rq[:, 2, :]))
            nc.vector.tensor_scalar(rq[:, 0, :], rq[:, 1, :], 0.125, None, ALU.mult).then_inc(s_ri, 1)
            dve.wait_ge(s_ri, 1)
            nc.vector.tensor_scalar(rq[:, 1, :], rq[:, 0, :], -1.0, None, ALU.mult).then_inc(s_ri, 1)
            dve.wait_ge(s_amk, 16)
            att_vec(dve, 0, 0, True)
            with dve.Fori(1, 7) as i:
                att_vec(dve, i, 1, False)
            att_vec(dve, 7, 2, False)
            att_lo(dve, 8)
            mlstm_vec(dve)
            for o in range(KT):
                if o == 0:
                    lo_job(dve, J_OUT1, 0)
                if o + 1 < KT:
                    lo_job(dve, J_OUT1 + o + 1, (o + 1) % 2)
                else:
                    lo_job(dve, F1.job, F1.ws)
                for n, (c0, w, v) in enumerate(LAT):
                    if o == 0 and n == 0:
                        dve.wait_ge(s_back, 32)
                    dve.wait_ge(s_proj, PR_OUT1 + 2 * o + n + 1)
                    add_residual(dve, 3 * (o % 2) + n, o, c0, w, mod[:, ADA + G1 + o, 0:1])
                    if (o, n) != (0, 0):
                        sum_vec(dve, 3, *((o, 0) if n else (o - 1, 1)))
            sum_vec(dve, 3, KT - 1, 1)
            gains_vec(dve, 3)
            diag_vec(dve, 3, 0)
            h_vec(dve, 3, 0, {6: lambda: lo_job(dve, F1.job + 1, 1 - F1.ws)})
            h_vec(dve, 3, 1)
            ffn_vec(dve, F1)
            for g in range(1, 16, 2):
                dve.wait_ge(s_oT, g + 1)
                nc.vector.tensor_copy(out_tm[:, g // 2, 512:1024], PS[:, g % 6, :]).then_inc(s_ocV, 1)

        def att_vec(dve, i, var, first):
            def top(u):
                dve.wait_ge(s_S, i * 8 + (u + 1))
                if u == 0:
                    dve.wait_ge(s_slr, i + 1)
                if u >= 3:
                    dve.wait_ge(s_pt, i * 8 + (u - 2))
                elif not first:
                    dve.wait_ge(s_pt, i * 8)
                nc.vector.tensor_copy(tick[:, u:u + 1], eps_t[:, 0:1]).then_inc(s_tick, 1)
                dve.wait_ge(s_amk, 16)
                nc.vector.tensor_tensor_reduce(out=pr[:, u % 3, :].rearrange("p (c k) -> p c k", c=2),
                                               in0=PS[:, 2 * (u % 2):2 * (u % 2) + 2, 0:320],
                                               in1=amask[:, var, :].rearrange("p (c k) -> p c k", c=2),
                                               scale=1.0, scalar=-3.0e38, op0=ALU.add, op1=ALU.max,
                                               accum_out=st8[:, u, 0:1]).then_inc(s_att, 1)
                dve.wait_ge(s_att, i * 24 + att_n(u, 0))
                nc.vector.tensor_scalar(st8[:, u, 1:2], st8[:, u, 0:1], rq_s[:, 1, u:u + 1], nsink[:, u:u + 1],
                                        ALU.mult, ALU.min).then_inc(s_nm, 1)

            def att_n(u, what):
                return {0: (1, 2, 5, 8, 11, 14, 17, 20), 1: (3, 6, 9, 12, 15, 18, 21, 23), 2: (4, 7, 10, 13, 16, 19, 22, 24)}[what][u]
            top(0)
            top(1)
            if not first:
                att_lo(dve, i)
            for u in range(8):
                dve.wait_ge(s_ex, i * 16 + (2 * u + 2))
                nc.vector.tensor_tensor(st8[:, u, 4:5], st8[:, u, 3:4], st8[:, u, 2:3], ALU.add).then_inc(s_att, 1)
                dve.wait_ge(s_att, i * 24 + att_n(u, 1))
                nc.vector.reciprocal(st8[:, u, 5:6], st8[:, u, 4:5]).then_inc(s_att, 1)
                dve.wait_ge(s_att, i * 24 + att_n(u, 2))
                nc.vector.tensor_scalar(pr[:, u % 3, :], pr[:, u % 3, :], st8[:, u, 5:6], None, ALU.mult).then_inc(s_pn, 1)
                if u + 2 < 8:
                    top(u + 2)
                dve.wait_ge(s_pt, i * 8 + (u + 1))
                g = u // 2
                if not (first and g < 2):
                    dve.wait_ge(s_O, i * 4 + (g - 1))
                nc.vector.tensor_copy(pT[:, g % 2, 4, (u % 2) * P:(u % 2 + 1) * P], PS[:, 6, (u % 2) * P:(u % 2 + 1) * P]).then_inc(s_pcV, 1)

        def att_lo(dve, i):
            dve.wait_ge(s_yA, i)
            nc.vector.tensor_tensor(h_lo[:, 0:4, bass.ds(i * P - P, P)], PS[:, 7, :].rearrange("p (j q) -> p j q", j=4),
                                    h_hi[:, 0:4, bass.ds(i * P - P, P)].bitcast(F32), ALU.subtract).then_inc(s_yV, 1)

        def mlstm_vec(dve):
            v = nc.vector
            fw, bw, rows_ = slice(0, 32), slice(32, 64), slice(0, 64)
            dve.wait_ge(s_rst, 48)
            dve.wait_ge(s_g1, 1)
            chain(dve, v.scalar_tensor_tensor(R_fl[0:64, :], G[64:128, :], 0.0, R_b[64:128, :], ALU.min, ALU.subtract))
            chain(dve, v.tensor_tensor_scan(R_b[fw, :], R_rst[fw, :], R_fl[fw, :], 0.0, ALU.mult, ALU.add))
            chain(dve, v.tensor_tensor_scan(R_b[bw, ::-1], R_rst[bw, ::-1], R_fl[bw, ::-1], 0.0, ALU.mult, ALU.add))
            chain(dve, v.memset(R_del[0:64, :], 0.0))
            for dst, src in ((R_del[fw, 128:1024:128], R_b[fw, 127:1023:128]), (R_del[fw, 1152:1153], R_b[fw, 1151:1152]),
                             (R_del[fw, 0:1], R_b[fw, 1279:1280]), (R_del[bw, 127:1023:128], R_b[bw, 128:1024:128]),
                             (R_del[bw, 1023:1024], R_b[bw, 1024:1025]), (R_del[bw, 1151:1152], R_b[bw, 1152:1153])):
                chain(dve, v.tensor_copy(dst, src))
            chain(dve, v.tensor_tensor(R_a[rows_, :], G[rows_, :], R_b[rows_, :], ALU.subtract))
            chain(dve, v.tensor_tensor_scan(R_m[fw, 1024:1280], R_del[fw, 1024:1280], R_a[fw, 1024:1280], 0.0, ALU.add, ALU.max))
            chain(dve, v.tensor_tensor_scan(R_m[fw, 0:1024], R_del[fw, 0:1024], R_a[fw, 0:1024], R_m[fw, 1279:1280], ALU.add, ALU.max))
            chain(dve, v.tensor_tensor_scan(R_m[bw, 1279:1023:-1], R_del[bw, 1279:1023:-1], R_a[bw, 1279:1023:-1], 0.0, ALU.add, ALU.max))
            chain(dve, v.tensor_tensor_scan(R_m[bw, 1023::-1], R_del[bw, 1023::-1], R_a[bw, 1023::-1], R_m[bw, 1024:1025], ALU.add, ALU.max))
            chain(dve, v.memset(m_rows[:, :, :], 0.0))
            for dst, x, y in ((m_rows[fw, 0, 1:8], R_m[fw, 127:1023:128], R_b[fw, 127:1023:128]),
                              (m_rows[fw, 0, 0:1], R_m[fw, 1279:1280], R_b[fw, 1279:1280]),
                              (m_rows[fw, 0, 9:10], R_m[fw, 1151:1152], R_b[fw, 1151:1152]),
                              (m_rows[bw, 0, 0:7], R_m[bw, 128:1024:128], R_b[bw, 128:1024:128]),
                              (m_rows[bw, 0, 7:9], R_m[bw, 1024:1153:128], R_b[bw, 1024:1153:128])):
                chain(dve, v.tensor_tensor(dst, x, y, ALU.add))
            chain(dve, v.tensor_copy(m_rows[fw, 1, :], R_m[fw, 127:1280:128]))
            chain(dve, v.tensor_copy(m_rows[bw, 1, :], R_m[bw, 0:1280:128]))
            ch = lambda t: t[0:64, :].rearrange("p (c t) -> p c t", t=P)
            bc = lambda n: m_rows[:, n, :].rearrange("p (c o) -> p c o", o=1).broadcast_to((64, 10, P))
            v.tensor_tensor(ch(R_rst), bc(0), ch(R_m), ALU.subtract).then_inc(s_gx, 1)
            v.tensor_tensor(ch(R_fl), ch(R_a), bc(1), ALU.subtract).then_inc(s_gx, 1)
            v.tensor_tensor(R_del[0:64, :], R_b[0:64, :], R_m[0:64, :], ALU.add).then_inc(s_gx, 1)
            v.tensor_tensor(m_rows[:, 2, :], m_rows[:, 0, :], m_rows[:, 1, :], ALU.subtract).then_inc(s_gx, 1)
            dve.wait_ge(s_gx, 4)
            chain(dve, v.tensor_scalar(R_b[0:64, :], R_m[0:64, :], -1.0, None, ALU.mult))
            dve.wait_ge(s_gc, 10)
            for n in range(len(m_units) + 1):
                if n < len(m_units) and m_units[n][2]:
                    d, c, _ = m_units[n]
                    o = m_out.index(n)
                    dve.wait_ge(s_mA, o + 1)
                    if o >= 2:
                        dve.wait_ge(s_mE, n - 1)
                        dve.wait_ge(s_mD, 2 * o - 2)
                    for h in range(4):
                        v.scalar_tensor_tensor(XE[:, d, h, :], PS[:, 2, h * P:(h + 1) * P], gcol[:, c, 4 * d + h:4 * d + h + 1],
                                               mm_mask[:, d, :], ALU.add, ALU.add).then_inc(s_mB, 1)
                    v.tensor_tensor(qt[:, d, :, :], qM[:, :, c * P:(c + 1) * P],
                                    PS[:, 0, 256:512].rearrange("p (a b) -> p a b", a=2), ALU.mult)
                    dve.wait_ge(s_mC, o + 1)
                    for e in range(2):
                        v.tensor_tensor(WT[:, d, e::2, :], XE[:, d, e::2, :],
                                        PS[:, e, 0:256].rearrange("p (a b) -> p a b", a=2), ALU.mult).then_inc(s_mD, 1)
                if n >= 1:
                    mlstm_read(dve, n - 1)
            for c in range(8):
                dve.wait_ge(s_fT, c + 1)
                if c >= 2:
                    dve.wait_ge(s_flo, c - 1)
                v.tensor_tensor(gated(c), PS[:, c % 2, :].rearrange("p (h t) -> p h t", h=4), oM[:, :, c * P:(c + 1) * P],
                                ALU.mult).then_inc(s_fm, 1)
                dve.wait_ge(s_fhi, c + 1)
                v.tensor_tensor(h_lo[:, 4:8, c * P:(c + 1) * P], gated(c), h_hi[:, 4:8, c * P:(c + 1) * P].bitcast(F32),
                                ALU.subtract).then_inc(s_flo, 1)

        def mlstm_read(dve, n):
            v = nc.vector
            d, c, out = m_units[n]
            nb0 = 3 + 2 * d
            dve.wait_ge(s_mE, n + 1)
            if out:
                for e in range(2):
                    dn = PS[:, nb0 + e, 128:258:129]
                    chain(dve, v.tensor_tensor(den[:, d, e::2, 0], dn, gcol[:, 20 + c, 4 * d + e:4 * d + 4:2], ALU.max))
                    chain(dve, v.scalar_tensor_tensor(den[:, d, e::2, 0], dn, -1.0, den[:, d, e::2, 0], ALU.mult, ALU.max))
                chain(dve, v.reciprocal(den[:, d, :, 1], den[:, d, :, 0]))
                first = (c < 4) == (d == 0)
                for h in range(4):
                    src = PS[:, nb0 + h % 2, (h // 2) * 129:(h // 2) * 129 + P]
                    dst = hsum[:, c, h * P:(h + 1) * P]
                    if first:
                        ins = v.tensor_scalar(dst, src, den[:, d, h, 1:2], None, ALU.mult)
                    else:
                        ins = v.scalar_tensor_tensor(dst, src, den[:, d, h, 1:2], dst, ALU.mult, ALU.add)
                chain(dve, ins)
            for p2 in range(2):
                src = PS[:, nb0 + p2, 258:387]
                if n < 2:
                    ins = v.tensor_copy(C[:, 2 * d + p2, :], src)
                else:
                    ins = v.scalar_tensor_tensor(C[:, 2 * d + p2, :], C[:, 2 * d + p2, :], dec_bc[:, 2 * d + p2, c:c + 1], src, ALU.mult, ALU.add)
            ins.then_inc(s_mF, 1)

        @block.sync
        def _(sp):
            fc = a["ffn_conv"].rearrange("l w (m p) -> (l w m) p", p=P)
            for dst, src in (
                (rows[0:96, 0, :], a["ada_b"].rearrange("l (m p) -> (l m) p", p=P)),
                (rows[96:128, 0, :], a["norm_g"].rearrange("l s (k p) -> (l s k) p", p=P)),
                (rows[:, 1, :], fc[0:P, :]),
                (rows[0:4, 2, :], fc[P:P + 4, :]),
                (rows[4:16, 2, :], a["even_conv"][0].rearrange("w (m p) -> (w m) p", p=P)),
                (rows[16:24, 2, :], a["c"].rearrange("b (k p) -> (b k) p", p=P)),
                (rows[24:32, 2, :], a["c_ctx"].rearrange("(k p) -> k p", p=P)),
            ):
                sp.dma_start(dst, src).then_inc(s_rows, 16)
            for t in range(NT):
                src = a["x"][0, t * P:(t + 1) * P, :] if t < 8 else a["ctx"][0, (t - 8) * P:(t - 7) * P, :]
                sp.dma_start(x_in[:, t, :], src).then_inc(s_in[t], 16)
            for j in range(NEV):
                load_job(sp, j, cols_of(a["even_w_in"][0], even_tiles[j]))
                if j == 1:
                    sp.wait_ge(s_xcA, NT)
                    sp.wait_ge(s_xcV, NT)
                    sp.wait_ge(s_amm, 14)
                    sp.dma_start(xs, X[:, :, :]).then_inc(s_spill, 16)
                    sp.wait_ge(s_spill, 16)
                    sp.wait_ge(s_hlo, 3 * KT)
                    sp.dma_start(xf[:, 0:n_tab], a["dft_tables"]).then_inc(s_tab, 16)
                    sp.dma_start(TAIL[0:2, :], a["dft_tails"]).then_inc(s_tab, 16)
            for o in range(KT):
                load_job(sp, J_OUT0 + o, cols_of(a["even_w_out"][0], o))
                if o == 1:
                    sp.wait_ge(s_fy, 4 * FY)
                    sp.wait_ge(s_pevV, 24)
                    sp.dma_start(X[:, :, :], xs).then_inc(s_back, 16)
            ffn_loads(sp, F0)
            layer1_loads(sp)

        @block.gpsimd
        def _(gp):
            done = 0

            def step(ins):
                nonlocal done
                done += 1
                ins.then_inc(s_const, 1)
                gp.wait_ge(s_const, done)
            step(gp.memset(ident[:, :], 0.0))
            step(gp.memset(ones[:, :], 1.0))
            step(gp.memset(eps_t[:, :], EPS))
            step(gp.memset(cT[:, :, :], 0.0))
            step(gp.memset(pick[:, :], 0.0))
            step(gp.affine_select(out=ident[:, :], in_=ident[:, :], compare_op=ALU.not_equal, fill=1.0,
                                  base=0, pattern=[[-1, P]], channel_multiplier=1))
            for q in range(4):
                step(gp.affine_select(out=pick[:, :], in_=pick[:, :], compare_op=ALU.not_equal, fill=1.0,
                                      base=-32 * q, pattern=[[-1, 2]], channel_multiplier=1))
            for j in range(2 * ADA):
                src = cols_of(a["ada_w"][j // ADA], j % ADA)
                if 2 <= j < 2 + ADA_X:
                    gp.dma_start(ada_x[:, j - 2, :, :], src).then_inc(s_ax[j - 2], 16)
                    continue
                if j >= 2 + ADA_X:
                    gp.wait_ge(s_amm, j - 1 if j >= 4 + ADA_X else j - ADA_X - 1)
                gp.dma_start(ada_st[:, j % 2, :, :], src).then_inc(s_al[j % 2], 16)
            layer1_pool(gp)

        @block.tensor
        def _(pe):
            pe.wait_ge(s_const, CONST)
            pe.wait_ge(s_rows, 7 * 16)
            for r, n in enumerate((P, P, 32)):
                last = nc.tensor.transpose(PS[:, 7, r * P:r * P + n], rows[0:n, r, :], ident[0:n, 0:n])
            last.then_inc(s_rowT, 1)
            for t in range(NT):
                pe.wait_ge(s_in[t], 16)
                for half in range(2):
                    g = 2 * t + half
                    if g >= 6:
                        pe.wait_ge(s_xcA if g % 2 == 0 else s_xcV, (g - 6) // 2 + 1)
                    for k in range(4):
                        last = nc.tensor.transpose(PS[:, g % 6, k * P:(k + 1) * P],
                                                   x_in[:, t, (4 * half + k) * P:(4 * half + k + 1) * P], ident[:, :])
                    last.then_inc(s_xT, 1)
            pe.wait_ge(s_ct, 1)
            pe.wait_ge(s_cols, 1)
            for m in range(16):
                ada_at(pe, m, m > 0)
                if m in (6, 10, 14):
                    norm_cols(pe, 0, (m - 6) // 4)
            ada_sum(pe, 15, 1)
            pe.wait_ge(s_mod, 16)
            norm_bcast(pe, 0, 0)
            first_pair(pe, 0, ((s_lo, 1), (s_lo, 2)), (0, 1), ((s_xcA, NT), (s_xcV, NT)))
            fourier_pe(pe, 0)
            for j in range(2, NEV):
                pe.wait_ge(s_lo, j + 1)
                for n in range(3):
                    if 2 <= j < 6:
                        pe.wait_ge(s_pevA, 3 * (j - 2) + n + 1)
                    elif j >= 6:
                        jj, kind = divmod(j - 6, 3)
                        if kind == 0:
                            pe.wait_ge(s_pevA, 12 + 3 * jj + n + 1)
                        else:
                            pe.wait_ge(s_pevV, 6 * jj + 3 * (kind - 1) + n + 1)
                    block_mm(pe, BLOCKS[n], 3 * (j % 2) + n, j % 2)
                    if j >= 5:
                        m = 16 + 3 * (j - 5) + n
                        if m < ADA:
                            if m == 16:
                                pe.wait_ge(s_fy, 4 * FY)
                            ada_at(pe, m, m > 16)
                        elif m == ADA:
                            ada_sum(pe, ADA - 1, 1)
                if 2 <= j <= 4:
                    fourier_pe(pe, j - 1)
            for o in range(KT):
                pe.wait_ge(s_lo, J_OUT0 + o + 1)
                for n in range(3):
                    if o < 2:
                        if n == 0:
                            pe.wait_ge(s_pevV, 24)
                    else:
                        pe.wait_ge(s_res, 3 * (o - 2) + n + 1)
                    if o == 0:
                        pe.wait_ge(s_mlo, KT * (n + 1))
                    block_mm(pe, BLOCKS[n], 3 * (o % 2) + n, o % 2)
                    if n == 0 and 1 <= o <= 4:
                        ada_at(pe, ADA + o - 1, o > 1)
                    elif n == 0 and o == 5:
                        ada_sum(pe, ADA + 3, 1)
                    elif (o, n) == (7, 1):
                        pe.wait_ge(s_mod, ADA + 4)
                        norm_cols(pe, 1, 0)
            norm_bcast(pe, 1, 0)
            norm_cols(pe, 1, 1)
            norm_cols(pe, 1, 2)
            ffn_pe(pe, F0, ADA + 4)
            layer1_pe(pe)

        @block.scalar
        def _(act):
            act.wait_ge(s_rowT, 1)
            nc.scalar.activation(cols[:, :], PS[:, 7, 0:288], ACT.Copy).then_inc(s_cols, 1)
            act.wait_ge(s_cols, 1)
            act.wait_ge(s_const, CONST)
            nc.scalar.activation(cT[:, :, 0:2].rearrange("p k v -> p v k"),
                                 cols[:, 272:288].rearrange("p (v k) -> p v k", v=2), ACT.Silu).then_inc(s_ct, 1)
            for g in range(0, 2 * NT, 2):
                act.wait_ge(s_xT, g + 1)
                nc.scalar.activation(X[:, 0:4, (g // 2) * P:(g // 2 + 1) * P],
                                     PS[:, g % 6, :].rearrange("p (k t) -> p k t", k=4), ACT.Copy).then_inc(s_xcA, 1)
            for m in range(16):
                ada_copy(act, m)
                if 2 <= m < 14:
                    for q in (2 * m - 4, 2 * m - 3):
                        sq_act(act, 0, q % KT, q // KT)
                if m in (7, 11, 15):
                    root_act(act, 0, (m - 7) // 4)
            hi_job(act, 0, w_hi[:, 0, :, :])
            hi_job(act, 1, w_hi[:, 1, :, :])
            for n in range(3):
                h_act(act, 0, n)
            for j in range(NEV):
                if j:
                    hi_job(act, j + 1, w_hi[:, (j + 1) % 2, :, :], 5 if j == 1 else 3 * j)
                for n, (c0, w, _) in enumerate(BLOCKS):
                    bank = 3 * (j % 2) + n
                    if j < 4:
                        if j == 0 and n == 0:
                            act.wait_ge(s_spill, 16)
                            act.wait_ge(s_hlo, 3 * KT)
                        if j and n == 0:
                            act.wait_ge(s_fold, j)
                        act.wait_ge(s_proj, 2 * n + j + 1 if j < 2 else 3 * j + n + 1)
                        nc.scalar.activation(U[:, c0:c0 + w], PS[:, bank, 0:w], ACT.Copy).then_inc(s_pevA, 1)
                    elif (j - 4) % 3 == 0:
                        if n == 0:
                            conv_free(act, (j - 4) // 3)
                        act.wait_ge(s_proj, 3 * j + n + 1)
                        g0 = c0 + 1 if n < 2 else c0 + 2
                        nc.scalar.activation(gpad[:, g0:g0 + w], PS[:, bank, 0:w], ACT.Copy).then_inc(s_pevA, 1)
                    if j >= 5 and 16 + 3 * (j - 5) + n < ADA:
                        ada_copy(act, 16 + 3 * (j - 5) + n)
                if 1 <= j <= 4:
                    fourier_act(act, j - 1)
            mix_hi(act, 3 * NEV)
            for o in range(1, KT):
                hi_job(act, J_OUT0 + o, w_hi[:, o % 2, :, :], 3 * (J_OUT0 + o - 1))
                for n in range(3):
                    sq_act(act, 1, o - 1, n)
                if 1 <= o <= 4:
                    ada_copy(act, ADA + o - 1)
            hi_job(act, F0.job, w_hi[:, F0.ws, :, :], 3 * (J_OUT0 + 7))
            sq_act(act, 1, KT - 1, 0)
            sq_act(act, 1, KT - 1, 1)
            root_act(act, 1, 0)
            sq_act(act, 1, KT - 1, 2)
            root_act(act, 1, 1)
            root_act(act, 1, 2)
            h_act(act, 1, 0, {3: lambda: hi_job(act, F0.job + 1, w_hi[:, 1 - F0.ws, :, :], F0.proj)})
            h_act(act, 1, 1)
            h_act(act, 1, 2)
            ffn_act(act, F0, ADA + 4)
            layer1_act(act)

        @block.vector
        def _(dve):
            for g in range(1, 2 * NT, 2):
                dve.wait_ge(s_xT, g + 1)
                nc.vector.tensor_copy(X[:, 4:8, (g // 2) * P:(g // 2 + 1) * P],
                                      PS[:, g % 6, :].rearrange("p (k t) -> p k t", k=4)).then_inc(s_xcV, 1)
            dve.wait_ge(s_cols, 1)
            for m in range(16):
                ada_write(dve, m)
                if 2 <= m < 14:
                    for q in (2 * m - 4, 2 * m - 3):
                        sum_vec(dve, 0, q % KT, q // KT)
                if m == 9:
                    diag_vec(dve, 0, 0)
            gains_vec(dve, 0)
            lo_job(dve, 0, 0)
            lo_job(dve, 1, 1)
            for n in range(3):
                h_vec(dve, 0, n)
            for t_, cs in ((gpad, (0, 1025, TOK + 2)),):
                for c_ in cs:
                    chain(dve, nc.vector.memset(t_[:, c_:c_ + 1], 0.0))
            dve.wait_ge(s_spill, 16)
            dve.wait_ge(s_hlo, 3 * KT)
            chain(dve, nc.vector.memset(FO[:, 0:1], 0.0))
            chain(dve, nc.vector.memset(FO[:, 512:513], 0.0))
            for j in range(NEV):
                if j:
                    lo_job(dve, j + 1, (j + 1) % 2)
                jj, kind = divmod(j - 4, 3)
                if j < 4:
                    dve.wait_ge(s_pevA, 3 * (j + 1))
                    if j:
                        dve.wait_ge(s_ch, 2 * j)
                    fold(dve, U[:, 0:1024], FE[:, 0:513], FO[:, 0:512], 512)
                    fold(dve, U[:, 1024:1280], FE[:, 516:645], FO[:, 512:640], 128, last=True)
                for n, (c0, w, _) in enumerate(BLOCKS):
                    bank = 3 * (j % 2) + n
                    s0 = c0 if n < 2 else c0 + 1
                    if j >= 4 and kind == 1:
                        dve.wait_ge(s_pevA, 12 + 3 * jj + n + 1)
                        dve.wait_ge(s_proj, 3 * j + n + 1)
                        nc.vector.tensor_tensor(gpad[:, s0 + 1:s0 + 1 + w], gpad[:, s0 + 1:s0 + 1 + w],
                                                PS[:, bank, 0:w], ALU.mult).then_inc(s_pevV, 1)
                    elif j >= 4 and kind == 2:
                        dve.wait_ge(s_proj, 3 * j + n + 1)
                        nc.vector.tensor_tensor(Y[:, jj, c0:c0 + w], conv_e[:, s0:s0 + w],
                                                PS[:, bank, 0:w], ALU.mult).then_inc(s_pevV, 1)
                    if j >= 5 and 16 + 3 * (j - 5) + n < ADA:
                        ada_write(dve, 16 + 3 * (j - 5) + n)
                if j >= 4 and kind == 1:
                    dve.wait_ge(s_pevV, 6 * jj + 3)
                    dve.wait_ge(s_ch, 8)
                    conv3(dve, conv_e, gpad, lambda w_: cols[:, 260 + 4 * w_ + jj:261 + 4 * w_ + jj], TOK + 1)
                if 1 <= j <= 4:
                    fourier_vec(dve, j - 1)
            mix_lo(dve)
            for o in range(KT):
                if o + 1 < KT:
                    lo_job(dve, J_OUT0 + o + 1, (o + 1) % 2)
                else:
                    lo_job(dve, F0.job, F0.ws)
                for n, (c0, w, v) in enumerate(BLOCKS):
                    if o == 0 and n == 0:
                        dve.wait_ge(s_back, 16)
                    dve.wait_ge(s_proj, 3 * (J_OUT0 + o) + n + 1)
                    add_residual(dve, 3 * (o % 2) + n, o, c0, w, mod[:, G1 + o, v:v + 1])
                    if (o, n) != (0, 0):
                        sum_vec(dve, 1, *((o, n - 1) if n else (o - 1, 2)))
                    if n == 0 and 2 <= o <= 5:
                        ada_write(dve, ADA + o - 2)
                    if (o, n) == (7, 1):
                        gains_vec(dve, 1)
                    if (o, n) == (7, 2):
                        diag_vec(dve, 1, 0)
            sum_vec(dve, 1, KT - 1, 2)
            h_vec(dve, 1, 0, {6: lambda: lo_job(dve, F0.job + 1, 1 - F0.ws)})
            h_vec(dve, 1, 1)
            h_vec(dve, 1, 2)
            ffn_vec(dve, F0, ADA + 4)
            layer1_vec(dve)


def dft_tables():
    def cs(rows, cols_, length, scale):
        x = 2 * np.pi * ((rows[:, None] * cols_[None, :]) % length) / length
        return np.cos(x) * scale, np.sin(x) * scale
    t, k = np.arange(P), np.arange(512)
    channel = list(cs(t, t, P, P ** -0.5))
    latent = [cs(t + P * j, k, SEQ, SEQ ** -0.5) for j in range(4)]
    alt = np.where(t % 2 == 0, 1.0, -1.0)
    parts = channel + [c for c, _ in latent] + [s for _, s in latent]
    parts += list(cs(t, t, CTX, CTX ** -0.5)) + [np.stack([alt / 32, alt / 16], 1)]
    tails = np.zeros((2, 642), np.float32)
    tails[0, 0:512] = np.where(k % 2 == 0, 1, -1) / 32
    tails[1, 512:640] = alt / 16
    tails[0, 640], tails[1, 641] = 1 / 32, 1 / 16
    return np.concatenate(parts, 1).astype(np.float32), tails


def rope_tables():
    f32 = np.float32
    row, col = np.repeat(np.arange(SEQ // 64, dtype=f32), 64), np.tile(np.arange(64, dtype=f32), SEQ // 64)
    inv = (f32(10000.0) ** (-np.arange(0, 32, 2, dtype=f32) / f32(32))).astype(f32)
    rope = np.zeros((P, 2304), f32)
    for p in range(P):
        d = p % 64
        angle = ((row if d < 32 else col) * inv[d % 16]).astype(f32)
        rope[p, 0:1024], rope[p, 1024:2048] = np.cos(angle), np.sin(angle)
        if (d % 32) < 16:
            rope[p + 16, 2048 + p] = -1
        else:
            rope[p - 16, 2048 + p] = 1
        rope[(p // 64) * 64:(p // 64) * 64 + 64, 2176 + p] = 1
    return rope


def mask_tables():
    f32, neg = np.float32, np.float32(-1e30)
    q, k = np.arange(P)[:, None], np.arange(384)[None, :]
    att = np.zeros((P, 3, 640), f32)
    att[:, :, 0:384] = np.where(np.abs(k - (q + P)) <= P, 0, neg)[:, None, :]
    att[:, 0, 0:P] = neg
    att[:, 2, 2 * P:3 * P] = neg
    resets = np.ones((64, TOK), f32)
    resets[0:32, 0::P] = 0
    resets[32:64, P - 1::P] = 0
    sel = np.zeros((64, 12, P), f32)
    for d in range(2):
        for h in range(4):
            sel[32 * d + h, 4 * d + h, :] = 1
        for pair in range(2):
            sel[32 * d + 2 * pair, 8 + 2 * d + pair, 0:64] = 1
            sel[32 * d + 2 * pair + 1, 8 + 2 * d + pair, 64:128] = 1
    s, t = np.arange(P)[:, None], np.arange(P)[None, :]
    causal = np.stack([np.where(s <= t, 0, neg), np.where(s >= t, 0, neg)], 1).astype(f32)
    return att, resets, sel, causal


INPUTS = ["x", "c", "ctx", "c_ctx", "ada_w", "ada_b", "norm_g", "even_w_in", "even_conv", "even_w_out", "odd_w_in",
          "odd_gate_b", "odd_q_g", "odd_k_g", "odd_sink", "odd_w_out", "ffn_w_up", "ffn_conv", "ffn_w_down"]


def kernel(**inputs):
    import concourse.bacc as bacc
    from concourse.bass_utils import run_bass_kernel_spmd

    laid = {name: np.ascontiguousarray(inputs[name]) for name in INPUTS}
    laid["dft_tables"], laid["dft_tails"] = dft_tables()
    laid["rope_tables"] = rope_tables()
    laid["att_masks"], laid["scan_resets"], laid["row_select"], laid["mlstm_masks"] = mask_tables()
    nc = bacc.Bacc("TRN2", target_bir_lowering=False, num_devices=1)
    arrays, args = {}, {}
    for name, value in laid.items():
        arrays[f"in_{name}_dram"] = value
        args[name] = nc.dram_tensor(f"in_{name}_dram", value.shape, mybir.dt.from_np(value.dtype),
                                    kind="ExternalInput").ap()
    args["out"] = nc.dram_tensor("out_0_dram", (1, SEQ, DM), F32, kind="ExternalOutput").ap()
    program(nc, args)
    result = run_bass_kernel_spmd(nc, [arrays], core_ids=[0])
    return result.results[0]["out_0_dram"]
```

```python
from contextlib import ExitStack

import numpy as np
import concourse.bass as bass
from concourse import mybir

F32 = mybir.dt.float32
F32R = mybir.dt.float32r
ALU = mybir.AluOpType
ACT = mybir.ActivationFunctionType

P = 128
DM, KT = 1024, 8
SEQ, CTX = 1024, 256
TOK = SEQ + CTX
NT = TOK // P
BLOCKS = [(0, 512, 0), (512, 512, 0), (1024, 256, 1)]
DFF, FT = 2816, 22
EPS = 1e-6
ADA_X = 8
ADA = 48
SH1, SC1, G1, SH2, SC2, G2 = (8 * i for i in range(6))


def program(nc, a):
    es = ExitStack()
    with es:
        def sb(name, shape, dt=F32, stack=None):
            return (stack or es).enter_context(nc.sbuf_tensor(name, shape, dt))

        def sem(name):
            return es.enter_context(nc.semaphore(name))

        cols = sb("cols", [P, 288])
        ident = sb("ident", [P, P])
        ones = sb("ones", [P, P])
        eps_t = sb("eps_t", [P, 1])
        cT = sb("cT", [P, KT, 32])
        pick = sb("pick", [P, 2])
        mod = sb("mod", [P, 2 * ADA, 2])
        gsc = sb("gsc", [P, 4, 2, KT])
        ada_sb = sb("ada_sb", [P, 2, P])
        gcol = sb("gcol", [P, 30, 8])
        dec_bc = sb("dec_bc", [P, 4, 10])
        m_rows = sb("m_rows", [64, 3, 10])
        sink = sb("sink", [P, 8])
        head_g = sb("head_g", [P, 2])
        gate_b = sb("gate_b", [P, 1])
        st8 = sb("st8", [P, 8, 6])
        tick = sb("tick", [P, 8])
        den = sb("den", [P, 2, 4, 2])
        w_hi = sb("w_hi", [P, 2, KT, P], F32R)
        w_lo = sb("w_lo", [P, 2, KT, P], F32R)
        stage = sb("stage", [P, 2, KT * P])
        xbase = ExitStack()
        X = sb("X", [P, KT, TOK], F32, xbase)
        with ExitStack() as s2:
            xnB = sb("xnB", [P, 3, 512], F32, s2)
            diagB = sb("diagB", [P, 4, P], F32, s2)
        ada_st = sb("ada_st", [P, 2, KT, P], F32, xbase)

        with ExitStack() as s0:
            x_in = sb("x_in", [P, NT, DM], F32, s0)
            rows = sb("rows", [P, 3, P], F32, s0)
            ada_x = sb("ada_x", [P, ADA_X, KT, P], F32, s0)
        s1 = ExitStack()
        h_hi = sb("h_hi", [P, KT, TOK], F32R, s1)
        h_lo = sb("h_lo", [P, KT, TOK], F32R, s1)
        with ExitStack() as s2:
            xnA = sb("xnA", [P, 3, 512], F32, s2)
            diagA = sb("diagA", [P, 4, P], F32, s2)
            ada4 = sb("ada4", [P, 4, 4 * P], F32, s2)
            sb("fill_n", [P, 9216 - 4096], F32, s2)
            sq = sb("sq", [P, 2, 512], F32, s2)
            ssum = sb("ssum", [P, TOK], F32, s2)
            rms = sb("rms", [P, 2, NT], F32, s2)
        with ExitStack() as s2:
            Y = sb("Y", [P, KT, TOK], F32, s2)
            gpad = sb("gpad", [P, TOK + 3], F32, s2)
        with ExitStack() as s2:
            d_hi = sb("d_hi", [P, 2, DM], F32R, s2)
            d_lo = sb("d_lo", [P, 2, DM], F32R, s2)
            a_hi = sb("a_hi", [P, 2, TOK], F32R, s2)
            a_lo = sb("a_lo", [P, 2, TOK], F32R, s2)
            fpad = sb("fpad", [P, TOK + 3], F32, s2)
            fcv = sb("fcv", [P, TOK + 1], F32, s2)
        s1.close()
        with ExitStack() as s2:
            out_tm = sb("out_tm", [P, 8, DM], F32, s2)
        xbase.close()
        so = ExitStack()
        with so:
            qA = sb("qA", [P, 4, SEQ], F32, so)
            kM = sb("kM", [P, 2, TOK], F32, so)
            vMt = sb("vMt", [P, NT, 4, 129], F32, so)
            rq = sb("rq", [P, 3, 64], F32, so)
            rq_s = sb("rq_s", [P, 2, 8], F32, so)
            nsink = sb("nsink", [P, 8], F32, so)
            sb("fill0", [P, 12288 - 4096 - 2560 - 5160 - 216], F32, so)
            with ExitStack() as s2:
                sb("fill1", [P, 2 * KT * TOK], F32, s2)
                with ExitStack() as s3:
                    gw = sb("gw", [P, KT, P], F32, s3)
                qM = sb("qM", [P, 2, SEQ], F32, s2)
                oM = sb("oM", [P, 4, SEQ], F32, s2)
                with ExitStack() as s3:
                    kA = sb("kA", [P, TOK], F32, s3)
                    vAt = sb("vAt", [P, 12, P], F32, s3)
                    G = sb("G", [P, TOK], F32, s3)
                    vtmp = sb("vtmp", [P, TOK], F32, s3)
                    kbd = sb("kbd", [P, P], F32, s3)
                    kt = sb("kt", [P, 512], F32, s3)
                with ExitStack() as s3:
                    k_s = sb("k_s", [P, 640], F32, s3)
                    v_s = sb("v_s", [P, 5, P], F32, s3)
                    sb("fill2", [P, 1536 + 1280], F32, s3)
                    q_s = sb("q_s", [P, 8, P], F32, s3)
                with ExitStack() as s3:
                    C = sb("C", [P, 4, 129], F32, s3)
                    sel = sb("sel", [P, 12, P], F32, s3)
                    mm_mask = sb("mm_mask", [P, 2, P], F32, s3)
                    sb("fill3", [P, 2816 - 516 - 1536 - 256], F32, s3)
                    XE = sb("XE", [P, 2, 4, P], F32, s3)
                    WT = sb("WT", [P, 2, 4, P], F32, s3)
                    qt = sb("qt", [P, 2, 2, P], F32, s3)
                    wv = sb("wv", [P, 2, 4, 129], F32, s3)
            sb("fill4", [P, 4 * TOK], F32, so)
            with ExitStack() as s2:
                with ExitStack() as s3:
                    rtab = sb("rtab", [P, 2304], F32, s3)
                with ExitStack() as s3:
                    pr = sb("pr", [P, 3, 640], F32, s3)
                sb("fill_p", [P, 2304], F32, s2)
                kP = sb("kP", [P, 1536], F32, s2)
                with ExitStack() as s3:
                    rotg = sb("rotg", [P, P], F32, s3)
                lnr = sb("lnr", [P, TOK], F32, s2)
                sb("fill5", [P, 4 * TOK], F32, s2)
                with ExitStack() as s3:
                    rt = [sb(f"rt{n}", [P, 512], F32, s3) for n in range(5)]
                with ExitStack() as s3:
                    pT = sb("pT", [P, 2, 5, 256], F32, s3)
                    amask = sb("amask", [P, 3, 640], F32, s3)
            with ExitStack() as s2:
                R_rst = sb("R_rst", [P, TOK], F32, s2)
                R_fl = sb("R_fl", [P, TOK], F32, s2)
                R_b = sb("R_b", [P, TOK], F32, s2)
                R_del = sb("R_del", [P, TOK], F32, s2)
                sb("fill6", [P, 4 * TOK], F32, s2)
                R_a = sb("R_a", [P, TOK], F32, s2)
                R_m = sb("R_m", [P, TOK], F32, s2)
                kMt = sb("kMt", [P, NT, 256], F32, s2)
        hsum = qA[:, :, :].rearrange("p a b -> p (a b)").rearrange("p (c v) -> p c v", c=8)
        COS, SIN = rtab[:, 0:1024], rtab[:, 1024:2048]
        ROT, BD = rtab[:, 2048:2176], rtab[:, 2176:2304]
        PS = es.enter_context(nc.psum_tensor("PS", [P, 8, 512], F32))

        xf = X[:, :, :].rearrange("p k t -> p (k t)")
        at = 0

        def cut(n):
            nonlocal at
            at += n
            return xf[:, at - n:at]
        CC, CS = cut(P), cut(P)
        CL = cut(4 * 512).rearrange("p (j k) -> p j k", j=4)
        SL = cut(4 * 512).rearrange("p (j k) -> p j k", j=4)
        CX, SX, ALT = cut(P), cut(P), cut(2)
        n_tab = at
        U, FE, FO = cut(TOK), cut(648), cut(640)
        conv_e = xf[:, at - 1288:at]
        TA = cut(5 * P).rearrange("p (j c) -> p j c", j=5)
        TB = cut(5 * P).rearrange("p (j c) -> p j c", j=5)
        TT, QS = cut(P), cut(640)
        TAIL = cut(642)
        xs = nc.dram_tensor("x_spill", [P, KT, TOK], F32).ap()

        s_in = [sem(f"x_loaded{t}") for t in range(NT)]
        s_rows = sem("rows_loaded")
        s_const = sem("constants_written")
        s_rowT = sem("rows_transposed")
        s_cols = sem("cols_copied")
        s_ct = sem("silu_c_written")
        s_xT = sem("x_transposed")
        s_xcA = sem("x_copied_scalar")
        s_xcV = sem("x_copied_vector")
        s_stage = [sem("stage_loaded0"), sem("stage_loaded1")]
        s_hi = sem("weights_hi")
        s_lo = sem("weights_lo")
        s_al = [sem("ada_loaded0"), sem("ada_loaded1")]
        s_ax = [sem(f"ada_early{m}") for m in range(ADA_X)]
        s_amm = sem("ada_partials")
        s_aev = sem("ada_partials_copied")
        s_asel = sem("ada_summed")
        s_mod = sem("mod_written")
        s_sq = sem("norm_squares")
        s_sqa = sem("norm_square_added")
        s_col = sem("norm_sums_by_token")
        s_root = sem("norm_root")
        s_rinv = sem("norm_root_inverted")
        s_diag = sem("norm_diagonal")
        s_bc = sem("norm_inverse_broadcast")
        s_xn = sem("norm_scaled")
        s_hhi = sem("h_hi_written")
        s_hlo = sem("h_lo_written")
        s_spill = sem("x_spilled")
        s_back = sem("x_reloaded")
        s_tab = sem("dft_tables_loaded")
        s_proj = sem("proj_psum_ready")
        s_pevA = sem("proj_psum_read_scalar")
        s_pevV = sem("proj_psum_read_vector")
        s_fold = sem("fourier_folded")
        s_ch = sem("channel_dft_ready")
        s_chA = sem("channel_dft_copied")
        s_ld = sem("seq_dft_ready")
        s_qs = sem("seq_dft_sine_copied")
        s_fy = sem("fourier_written")
        s_mhi = sem("mix_hi")
        s_mlo = sem("mix_lo")
        s_res = sem("residual_added")
        s_v = sem("vector_chain")
        s_out = sem("out_stored")
        s_fg = sem("ffn_gate_copied")
        s_fc = sem("ffn_conv_done")
        s_fs = sem("ffn_silu_done")
        s_fp = sem("ffn_product")
        s_ahi = sem("ffn_act_hi")
        s_alo = sem("ffn_act_lo")
        s_down = sem("down_psum_ready")

        def cols_of(w, c):
            return w[:, c * P:(c + 1) * P].rearrange("(k p) c -> p k c", p=P)

        even_tiles = [12, 13, 14, 15]
        for j in range(4):
            even_tiles += [4 + j, 8 + j, j]
        NEV = len(even_tiles)
        J_OUT0, J_FFN0 = NEV, NEV + KT
        PAIRS = FT // 2
        FY = 6
        st3 = [stage[:, s, :].rearrange("p (k c) -> p k c", k=KT) for s in range(2)]
        RES_OUT0 = 3 * KT
        RES_FFN0 = RES_OUT0 + PAIRS * KT * 3

        class Ffn:
            def __init__(self, layer, job, blocks, proj, res, down, tiles, ws):
                self.layer, self.job, self.blocks, self.nb = layer, job, blocks, len(blocks)
                self.proj, self.res, self.down = proj, res, down
                self.tiles = tiles
                self.ws = ws
                self.sp = job % 2
                self.fc0 = 2 * PAIRS * layer
                self.cw = TOK + 1 if layer == 0 else SEQ
        F0 = Ffn(0, J_FFN0, BLOCKS, 3 * J_FFN0, RES_OUT0, 0, (0, 0), J_FFN0 % 2)

        block = es.enter_context(nc.Block())

        def load_job(sp, j, src):
            if j >= 2:
                sp.wait_ge(s_lo, j - 1)
            sp.dma_start(st3[j % 2], src).then_inc(s_stage[j % 2], 16)

        def ffn_loads(sp, F):
            up, down = a["ffn_w_up"][F.layer], a["ffn_w_down"][F.layer]

            def up_view(c):
                return up[:, bass.ds(c, P)].rearrange("(k p) c -> p k c", p=P)

            def one(j, n, dst, view):
                sp.wait_ge(s_lo, j - 1)
                slot = (F.sp + n) % 2
                sp.dma_start(dst[slot], view).then_inc(s_stage[slot], 16)
            one(F.job, 0, st3, up_view(0))
            st2 = [stage[:, s, :] for s in range(2)]
            with sp.Fori(0, PAIRS) as i:
                j = i * 6 + (F.job + 1)
                one(j, 1, st3, up_view(i * 256 + DFF))
                one(j + 1, 2, st3, up_view(i * 256 + P))
                one(j + 2, 3, st3, up_view(i * 256 + (DFF + P)))
                one(j + 3, 4, st2, down[bass.ds(i * 256, P), :])
                one(j + 4, 5, st2, down[bass.ds(i * 256 + P, P), :])
                one(j + 5, 6, st3, up_view(i * 256 + 256))

        CONST = 10

        def block_mm(pe, blk, bank, wslot, ready=None, hook=None, ready_sem=None, hook_at=6):
            c0, w, _ = blk
            for k in range(KT):
                if k == hook_at and hook is not None:
                    hook()
                if ready is not None:
                    pe.wait_ge(ready_sem or s_hlo, ready + k + 1)
                for q, (wt, ht) in enumerate(((w_hi, h_hi), (w_hi, h_lo), (w_lo, h_hi))):
                    last = nc.tensor.matmul(PS[:, bank, 0:w], wt[:, wslot, k, :], ht[:, k, c0:c0 + w],
                                            start=(k == 0 and q == 0), stop=(k == KT - 1 and q == 2))
            last.then_inc(s_proj, 1)

        def ada_step(pe, j, loaded, slot, sum_last=True):
            early = isinstance(j, int) and 2 <= j < 2 + ADA_X
            src = ada_x[:, j - 2] if early else ada_st[:, slot]
            if early:
                pe.wait_ge(s_ax[j - 2], 16)
            else:
                pe.wait_ge(s_al[slot], loaded)
            if not (isinstance(j, int) and j < 2):
                pe.wait_ge(s_mod, j - 1)
            for k in range(KT):
                q = k % 4
                last = nc.tensor.matmul(PS[32 * q:32 * q + 32, 6 + slot, 0:P], cT[:, k, :], src[:, k, :],
                                        start=(k < 4), stop=(k >= 4), tile_position=(0, 32 * q))
            last.then_inc(s_amm, 1)
            if sum_last:
                ada_sum(pe, j - 1, 1 - slot)

        def ada_at(pe, j, sum_last=True):
            ada_step(pe, j, 16 * (j // 2 + 1 - (ADA_X // 2 if j >= 2 + ADA_X else 0)), j % 2, sum_last)

        def first_ada(pe, g):
            for m in range(4 * g, 4 * g + 4):
                early = 2 <= m < 2 + ADA_X
                src = ada_x[:, m - 2] if early else ada_st[:, m % 2]
                if early:
                    pe.wait_ge(s_ax[m - 2], 16)
                else:
                    pe.wait_ge(s_al[m % 2], 16 * (m // 2 + 1 - (ADA_X // 2 if m >= 2 + ADA_X else 0)))
                if m == 0:
                    pe.wait_ge(s_xcA, NT)
                    pe.wait_ge(s_xcV, NT)
                for k in range(KT):
                    q = k % 4
                    last = nc.tensor.matmul(PS[32 * q:32 * q + 32, 3 + g, (m % 4) * P:(m % 4 + 1) * P], cT[:, k, :],
                                            src[:, k, :], start=(k < 4), stop=(k >= 4), tile_position=(0, 32 * q))
                last.then_inc(s_amm, 1)

        def first_ada_sum(pe, g):
            pe.wait_ge(s_aev, 4 * g + 4)
            if g:
                pe.wait_ge(s_mod, 4 * g)
            for m in range(4):
                last = nc.tensor.matmul(PS[:, 7, 2 * m:2 * m + 2], ada4[:, g, m * P:(m + 1) * P], pick[:, :], start=True, stop=True)
            last.then_inc(s_asel, 4)

        def ada_sum(pe, j, slot):
            pe.wait_ge(s_aev, j + 1)
            nc.tensor.matmul(PS[:, 6 + slot, P:P + 2], ada_sb[:, slot, :], pick[:, :],
                             start=True, stop=True).then_inc(s_asel, 1)

        def sq_seq(q):
            nb = NORM_NB[q]
            if q % 2:
                return [(k, n) for k in range(KT) for n in range(nb)]
            return [(k, n) for n in range(nb) for k in range(KT)]

        def sq_at(q, k, n):
            return NORM_AT[q] * KT + sq_seq(q).index((k, n))

        def norm_cols(pe, q, n):
            c0, w, _ = BLOCKS[n]
            pe.wait_ge(s_sqa, sq_at(q, KT - 1, n) + 1)
            if q == 0:
                pe.wait_ge(s_xcA, NT)
                pe.wait_ge(s_xcV, NT)
            elif n:
                pe.wait_ge(s_root, NORM_AT[q] + n)
            for t in range(w // P):
                last = nc.tensor.matmul(PS[:, cols_bank(q, n), 4 * n + t:4 * n + t + 1], ssum[:, c0 + t * P:c0 + (t + 1) * P], ones[:, 0:1],
                                        start=True, stop=True)
            last.then_inc(s_col, 1)

        def cols_bank(q, n):
            return 6 if q else n

        def norm_bank(n):
            return 6 if n == 1 else 7

        def norm_bcast(pe, q, n):
            w = BLOCKS[n][1]
            if n == 1:
                pe.wait_ge(s_root, NORM_AT[q] + NORM_NB[q])
            if n == 2:
                pe.wait_ge(s_xn, (NORM_AT[q] + 1) * KT)
            pe.wait_ge(s_diag, NORM_AT[q] + n + 1)
            diag = diagA if q < 2 else diagB
            nc.tensor.matmul(PS[:, norm_bank(n), 0:w], ones[:, :],
                             diag[:, 0:w // P, :].rearrange("p t c -> p (t c)"), start=True, stop=True).then_inc(s_bc, 1)

        def first_pair(pe, q, weights, slots, free):
            nb = NORM_NB[q]
            for n in range(nb):
                for t in range(2):
                    if n == 0:
                        pe.wait_ge(*weights[t])
                    if free is not None:
                        pe.wait_ge(*free[t])
                    block_mm(pe, BLOCKS[n], 3 * t + n, slots[t], (NORM_AT[q] + n) * KT if t == 0 else None,
                             (lambda: norm_bcast(pe, q, n + 1)) if t == 0 and n + 1 < nb else None)
        NORM_NB = (3, 3, 3, 2)
        NORM_AT = (0, 3, 6, 9)

        def fourier_pe(pe, g, stage):
            if stage == 0:
                if g == 0:
                    pe.wait_ge(s_tab, 32)
                    pe.wait_ge(s_xn, 3 * KT)
                pe.wait_ge(s_fold, g + 1)
                if g >= 1:
                    pe.wait_ge(s_fy, FY * g)
                    pe.wait_ge(s_qs, 2 * g)
            if stage < 2:
                src, tab = ((FE, CC), (FO, CS))[stage]
                if stage:
                    pe.wait_ge(s_chA, 5 * g + 3)
                for j in range(5):
                    c0 = j * P if j < 4 else (516 if stage == 0 else 512)
                    dst = PS[:, 6, j * P:(j + 1) * P] if j < 4 else PS[:, 7, 0:P]
                    last = nc.tensor.matmul(dst, src[:, c0:c0 + P], tab, start=True, stop=True)
                if stage == 0:
                    last = nc.tensor.matmul(PS[0:2, 7, P:2 * P], FE[:, 512:645:132], CC, start=True, stop=True)
                last.then_inc(s_ch, 1)
            elif stage == 2:
                pe.wait_ge(s_chA, 5 * g + 5)
                for j in range(4):
                    nc.tensor.matmul(PS[:, 6, :], TA[:, j, :], CL[:, j, :], start=(j == 0), stop=False)
                nc.tensor.matmul(PS[:, 6, :], TT[0:2, :], TAIL[0:2, 0:512], start=False, stop=True)
                for j in range(4):
                    last = nc.tensor.matmul(PS[:, 7, :], TB[:, j, :], SL[:, j, :], start=(j == 0), stop=(j == 3))
                last.then_inc(s_ld, 1)
            else:
                pe.wait_ge(s_fy, FY * g + 2)
                pe.wait_ge(s_qs, 2 * g + 1)
                nc.tensor.matmul(PS[:, 6, 0:P], TA[:, 4, :], CX, start=True, stop=False)
                nc.tensor.matmul(PS[:, 6, 0:P], TT[0:2, :], TAIL[0:2, 512:640], start=False, stop=True)
                for j in range(4):
                    nc.tensor.matmul(PS[:, 6, P:P + 1], TA[:, j, :], ALT[:, 0:1], start=(j == 0), stop=False)
                nc.tensor.matmul(PS[:, 6, P:P + 1], TT[0:2, :], TAIL[0:2, 640:641], start=False, stop=True)
                nc.tensor.matmul(PS[:, 6, P + 1:P + 2], TA[:, 4, :], ALT[:, 1:2], start=True, stop=False)
                nc.tensor.matmul(PS[:, 6, P + 1:P + 2], TT[0:2, :], TAIL[0:2, 641:642], start=False, stop=True)
                nc.tensor.matmul(PS[:, 7, 0:P], TB[:, 4, :], SX, start=True, stop=True).then_inc(s_ld, 1)

        DOWN_BANK = (6, 7, 2)

        def ffn_pe(pe, F, ada_from=None):
            nb = F.nb

            def tile(job, wslot, bank0, free, after=None, bank2=None):
                pe.wait_ge(s_lo, job + 1)
                for n in range(nb):
                    if free is not None:
                        pe.wait_ge(free[0], free[1] + (n + 1))
                    if n == 2 and bank2 is not None:
                        pe.wait_ge(s_res, bank2)
                    block_mm(pe, F.blocks[n], bank0 + n, wslot)
                    if after is not None:
                        after(n)

            def down(i, last=False):
                pe.wait_ge(s_lo, i * 6 + F.job)
                pe.wait_ge(s_alo, i * (2 * nb) + F.tiles[1])
                if ada_from is not None:
                    pe.wait_ge(s_mod, i * 4 + ada_from)
                for o in range(KT):
                    for n in range(nb):
                        c = o * nb + n
                        c0, w, _ = F.blocks[n]
                        if o == 0 and n == 2:
                            pe.wait_ge(s_fg, i * (2 * nb) + (F.tiles[0] + (0 if last else nb)))
                        pe.wait_ge(s_res, i * (KT * nb) + (F.res - KT * nb + c - nb + 1))
                        mm = 0
                        for f in range(2):
                            for wt, at_ in ((d_hi, a_hi), (d_hi, a_lo), (d_lo, a_hi)):
                                ins = nc.tensor.matmul(PS[:, DOWN_BANK[n], 0:w], wt[:, f, o * P:(o + 1) * P],
                                                       at_[:, f, c0:c0 + w], start=(mm == 0), stop=(mm == 5))
                                mm += 1
                        ins.then_inc(s_down, 1)

            def ada(i, m):
                if m == 0:
                    pe.wait_ge(s_res, i * (KT * nb) + F.res)
                ada_step(pe, i * 4 + (ada_from + m), i * 32 + 16 * ((ada_from + m) // 2 + 1 - ADA_X // 2), m % 2, m > 0)

            def pair(i, first):
                j = i * 6 + F.job
                t = i * (2 * nb)

                def last_sum(n):
                    if ada_from is not None and n == 0 and not first:
                        ada_sum(pe, i * 4 + (ada_from - 1), 1)

                def in_gate(n):
                    if ada_from is not None and n in (0, 2):
                        ada(i, n // 2)

                def in_value(n):
                    if ada_from is not None and n in (0, 2):
                        ada(i, 2 + n // 2)
                if first:
                    first_pair(pe, 2 * F.layer + 1, ((s_lo, j + 1), (s_lo, j + 2)), (F.ws, 1 - F.ws), None)
                else:
                    tile(j, F.ws, 0, (s_fg, t + F.tiles[0] - nb), after=last_sum)
                    tile(j + 1, 1 - F.ws, 3, (s_fp, t + F.tiles[0] - nb))
                    down(i)
                tile(j + 2, F.ws, 0, (s_fg, t + F.tiles[0]), after=in_gate, bank2=None if first else i * (KT * nb) + F.res)
                tile(j + 3, 1 - F.ws, 3, (s_fp, t + F.tiles[0]), after=in_value)
            pe.wait_ge(s_res, F.res)
            pair(0, True)
            with pe.Fori(1, PAIRS) as i:
                pair(i, False)
            if ada_from is not None:
                ada_sum(pe, 4 * PAIRS + ada_from - 1, 1)
            if F.layer == 1:
                down(PAIRS, last=True)
                return
            pe.wait_ge(s_lo, PAIRS * 6 + F.job)
            pe.wait_ge(s_alo, PAIRS * (2 * nb) + F.tiles[1])
            pe.wait_ge(s_mod, 2 * ADA)
            for c in range(KT * nb):
                n, o = divmod(c, KT)
                c0, w, _ = F.blocks[n]
                if c < 3:
                    pe.wait_ge(s_fg, PAIRS * (2 * nb) + F.tiles[0])
                else:
                    pe.wait_ge(s_res, (PAIRS - 1) * (KT * nb) + F.res + c - 2)
                for f in range(2):
                    for q, (wt, at_) in enumerate(((d_hi, a_hi), (d_hi, a_lo), (d_lo, a_hi))):
                        ins = nc.tensor.matmul(PS[:, c % 3, 0:w], wt[:, f, o * P:(o + 1) * P],
                                               at_[:, f, c0:c0 + w], start=(f == 0 and q == 0), stop=(f == 1 and q == 2))
                ins.then_inc(s_down, 1)
                if c == 10:
                    norm_cols(pe, 2, 0)
                elif c == 15:
                    norm_bcast(pe, 2, 0)
                elif c == 20:
                    norm_cols(pe, 2, 1)
            norm_cols(pe, 2, 2)


        def conv_free(act, jj):
            if jj:
                act.wait_ge(s_v, 7 + 3 * jj)

        def hi_job(act, j, dst, used=None, slot=None, count=None):
            slot = j % 2 if slot is None else slot
            act.wait_ge(s_stage[slot], 16 * (j // 2 + 1) if count is None else count)
            if used is not None:
                act.wait_ge(s_proj, used)
            nc.scalar.activation(dst, st3[slot], ACT.Copy).then_inc(s_hi, 1)

        def ada_copy(act, j, slot=None):
            slot = j % 2 if slot is None else slot
            act.wait_ge(s_amm, j + 1)
            if not (isinstance(j, int) and j < 2):
                act.wait_ge(s_asel, j - 1)
            nc.scalar.activation(ada_sb[:, slot, :], PS[:, 6 + slot, 0:P], ACT.Copy).then_inc(s_aev, 1)

        def sq_act(act, q, k, n):
            c0, w, _ = BLOCKS[n]
            at_ = sq_at(q, k, n)
            x_ready(act, q, n, k)
            if at_ >= 2:
                act.wait_ge(s_sqa, at_ - 1)
            nc.scalar.activation(sq[:, at_ % 2, 0:w], X[:, k, c0:c0 + w], ACT.Square).then_inc(s_sq, 1)

        def root_act(act, q, n):
            act.wait_ge(s_col, NORM_AT[q] + n + 1)
            cnt = BLOCKS[n][1] // P
            nc.scalar.activation(rms[:, 0, 4 * n:4 * n + cnt], PS[:, cols_bank(q, n), 4 * n:4 * n + cnt], ACT.Sqrt,
                                 bias=eps_t[:, 0:1], scale=1.0 / DM).then_inc(s_root, 1)

        def h_act(act, q, n, hooks=()):
            c0, w, v = BLOCKS[n]
            at_ = (NORM_AT[q] + n) * KT
            xn = xnA if q < 2 else xnB
            for k in range(KT):
                if k in hooks:
                    hooks[k]()
                act.wait_ge(s_xn, at_ + k + 1)
                nc.scalar.activation(h_hi[:, k, c0:c0 + w], xn[:, (at_ + k) % 3, 0:w], ACT.Identity,
                                     bias=shift_of(q, k, v)).then_inc(s_hhi, 1)

        def x_ready(eng, q, n, k):
            if q == 0:
                if k == 0:
                    eng.wait_ge(s_xcA, min(4 * n + 4, NT))
                    eng.wait_ge(s_xcV, min(4 * n + 4, NT))
            elif q == 1:
                eng.wait_ge(s_res, 3 * k + n + 1)
            elif q == 2:
                eng.wait_ge(s_res, RES_FFN0 - 3 * KT + KT * n + k + 1)
            else:
                eng.wait_ge(s_res, RES_FFN0 + 2 * k + n + 1)

        def shift_of(q, k, v):
            m = (q // 2) * ADA + (SH1, SH2)[q % 2] + k
            return mod[:, m, v:v + 1]

        def fourier_act(act, g, last):
            if last:
                act.wait_ge(s_ld, 2 * g + 2)
                nc.scalar.activation(QS[:, 512:640], PS[:, 7, 0:P], ACT.Copy).then_inc(s_qs, 1)
                return
            act.wait_ge(s_ch, 2 * g + 1)
            if g:
                act.wait_ge(s_ld, 2 * g)
            nc.scalar.activation(TA[:, 0:4, :], PS[:, 6, :].rearrange("p (j c) -> p j c", j=4), ACT.Copy).then_inc(s_chA, 1)
            nc.scalar.activation(TA[:, 4, :], PS[:, 7, 0:P], ACT.Copy).then_inc(s_chA, 1)
            nc.scalar.activation(TT[0:2, :], PS[0:2, 7, P:2 * P], ACT.Copy).then_inc(s_chA, 1)
            act.wait_ge(s_ch, 2 * g + 2)
            nc.scalar.activation(TB[:, 0:4, :], PS[:, 6, :].rearrange("p (j c) -> p j c", j=4), ACT.Copy).then_inc(s_chA, 1)
            nc.scalar.activation(TB[:, 4, :], PS[:, 7, 0:P], ACT.Copy).then_inc(s_chA, 1)
            act.wait_ge(s_ld, 2 * g + 1)
            if g:
                act.wait_ge(s_fy, FY * g)
            nc.scalar.activation(QS[:, 0:512], PS[:, 7, :], ACT.Copy).then_inc(s_qs, 1)

        def mix_hi(act, proj):
            for n, (c0, w, _) in enumerate(BLOCKS):
                for k in range(KT):
                    if n == 0 and k == 0:
                        act.wait_ge(s_proj, proj)
                        act.wait_ge(s_fy, 4 * FY)
                        act.wait_ge(s_pevV, 24)
                    nc.scalar.activation(h_hi[:, k, c0:c0 + w], Y[:, k, c0:c0 + w], ACT.Copy).then_inc(s_mhi, 1)

        def ffn_act(act, F, ada_from=None):
            nb = F.nb
            d_hi_slots = [d_hi[:, s, :] for s in range(2)]

            def hi(i, n, wslot, used):
                jn = F.sp + 1 + n
                slot = jn % 2
                before = (F.job + 1 + n) // 2 + 1
                act.wait_ge(s_stage[slot], i * 48 + 16 * before)
                if used is not None:
                    act.wait_ge(*used)
                if wslot is None:
                    nc.scalar.activation(d_hi_slots[n - 3], stage[:, slot, :], ACT.Copy).then_inc(s_hi, 1)
                else:
                    nc.scalar.activation(w_hi[:, wslot, :, :], st3[slot], ACT.Copy).then_inc(s_hi, 1)

            def gate(i, half, after=None):
                if not (isinstance(i, int) and i * 2 + F.fc0 + half == 0):
                    act.wait_ge(s_fc, i * 2 + (F.fc0 + half))
                for n in range(nb):
                    c0, w, _ = F.blocks[n]
                    if isinstance(i, int) and i == half == 0:
                        act.wait_ge(s_proj, F.proj + 2 * n + 1)
                    else:
                        act.wait_ge(s_proj, i * (4 * nb) + (F.proj + 2 * nb * half + n + 1))
                    g0 = c0 + 1 if n < 2 else c0 + 2
                    nc.scalar.activation(fpad[:, g0:g0 + w], PS[:, n, 0:w], ACT.Copy).then_inc(s_fg, 1)
                    if after is not None:
                        after(n)

            def silu(i, half):
                act.wait_ge(s_fc, i * 2 + (F.fc0 + half + 1))
                nc.scalar.activation(fcv[:, 0:F.cw], fcv[:, 0:F.cw], ACT.Silu).then_inc(s_fs, 1)

            def a_half(i, half):
                if half == 0 and not isinstance(i, int):
                    act.wait_ge(s_down, i * (KT * nb) + F.down)
                for n in range(nb):
                    c0, w, _ = F.blocks[n]
                    s0 = c0 if n < 2 else c0 + 1
                    act.wait_ge(s_fp, i * (2 * nb) + (F.tiles[0] + nb * half + n + 1))
                    nc.scalar.activation(a_hi[:, half, c0:c0 + w], fcv[:, s0:s0 + w], ACT.Copy).then_inc(s_ahi, 1)

            def pair(i, first):
                pb = F.proj

                def ada(m):
                    if ada_from is not None:
                        ada_copy(act, i * 4 + (ada_from + m), (ada_from + m) % 2)

                def in_gate(n):
                    if n in (0, 2):
                        ada(n // 2)
                if not first:
                    hi(i, 0, 1 - F.ws, (s_proj, i * (4 * nb) + pb))
                gate(i, 0)
                hi(i, 1, F.ws, (s_proj, pb + 2 * nb - 1) if first else (s_proj, i * (4 * nb) + (pb + nb)))
                silu(i, 0)
                hi(i, 2, 1 - F.ws, (s_proj, i * (4 * nb) + (pb + 2 * nb)))
                a_half(i, 0)
                hi(i, 3, None, None if first else (s_down, i * (KT * nb) + F.down))
                hi(i, 4, None, None)
                gate(i, 1, in_gate)
                hi(i, 5, F.ws, (s_proj, i * (4 * nb) + (pb + 3 * nb)))
                ada(2)
                silu(i, 1)
                ada(3)
                a_half(i, 1)
            act.wait_ge(s_hlo, (NORM_AT[2 * F.layer + 1] + nb) * KT)
            pair(0, True)
            with act.Fori(1, PAIRS) as i:
                pair(i, False)
            if F.layer == 1:
                return
            for n in range(2):
                hi_job(act, J_ODD + n, w_hi[:, (n + 1) % 2, :, :], PR_ODD)
            for c in range(KT * nb):
                sq_act(act, 2, c % KT, c // KT)
                if c == 11:
                    root_act(act, 2, 0)
                elif c == 22:
                    root_act(act, 2, 1)
            root_act(act, 2, 2)

        vn = [0]

        def chain(dve, ins):
            vn[0] += 1
            ins.then_inc(s_v, 1)
            dve.wait_ge(s_v, vn[0])

        def lo_job(dve, j, wslot):
            dve.wait_ge(s_hi, j + 1)
            nc.vector.tensor_tensor(w_lo[:, wslot, :, :], st3[j % 2], w_hi[:, wslot, :, :].bitcast(F32),
                                    ALU.subtract).then_inc(s_lo, 1)

        def ada_write(dve, j, slot=None):
            slot = j % 2 if slot is None else slot
            dve.wait_ge(s_asel, j + 1)
            src = PS[:, 6 + slot, P:P + 2]
            if isinstance(j, int):
                nc.vector.tensor_scalar(mod[:, j, :], src, cols[:, j:j + 1], None, ALU.add).then_inc(s_mod, 1)
            else:
                nc.vector.tensor_tensor(mod[:, bass.ds(j, 1), :].rearrange("p a v -> p (a v)"), src,
                                        cols[:, bass.ds(j, 1)].broadcast_to((P, 2)), ALU.add).then_inc(s_mod, 1)

        def gains_vec(dve, q):
            sc = (q // 2) * ADA + (SC1, SC2)[q % 2]
            dve.wait_ge(s_mod, sc + KT)
            for v in range(2):
                chain(dve, nc.vector.scalar_tensor_tensor(gsc[:, q, v, :], mod[:, sc:sc + KT, v], 1.0,
                                                          cols[:, 96 + q * KT:96 + (q + 1) * KT], ALU.add, ALU.mult))

        def sum_vec(dve, q, k, n):
            c0, w, _ = BLOCKS[n]
            at_ = sq_at(q, k, n)
            dve.wait_ge(s_sq, at_ + 1)
            if k == 0:
                if q:
                    dve.wait_ge(s_col, NORM_AT[q])
                nc.vector.tensor_copy(ssum[:, c0:c0 + w], sq[:, at_ % 2, 0:w]).then_inc(s_sqa, 1)
            else:
                dve.wait_ge(s_sqa, sq_at(q, k - 1, n) + 1)
                nc.vector.tensor_tensor(ssum[:, c0:c0 + w], ssum[:, c0:c0 + w], sq[:, at_ % 2, 0:w], ALU.add).then_inc(s_sqa, 1)

        def diag_vec(dve, q, n):
            at_, cnt = NORM_AT[q] + n, BLOCKS[n][1] // P
            dve.wait_ge(s_root, at_ + 1)
            nc.vector.reciprocal(rms[:, 1, 4 * n:4 * n + cnt], rms[:, 0, 4 * n:4 * n + cnt]).then_inc(s_rinv, 1)
            dve.wait_ge(s_rinv, at_ + 1)
            if at_:
                dve.wait_ge(s_bc, at_)
            diag = diagA if q < 2 else diagB
            nc.vector.tensor_tensor(diag[:, 0:cnt, :],
                                    ident[:, :].rearrange("p (o c) -> p o c", o=1).broadcast_to((P, cnt, P)),
                                    rms[:, 1, 4 * n:4 * n + cnt].rearrange("p (t o) -> p t o", o=1).broadcast_to((P, cnt, P)),
                                    ALU.mult).then_inc(s_diag, 1)

        def h_vec(dve, q, n, hooks=()):
            c0, w, v = BLOCKS[n]
            at_ = (NORM_AT[q] + n) * KT
            xn = xnA if q < 2 else xnB
            dve.wait_ge(s_bc, NORM_AT[q] + n + 1)
            for k in range(KT + 2):
                if k in hooks:
                    hooks[k]()
                if k < KT:
                    if at_ + k >= 3:
                        dve.wait_ge(s_hlo, at_ + k - 2)
                    nc.vector.scalar_tensor_tensor(xn[:, (at_ + k) % 3, 0:w], X[:, k, c0:c0 + w], gsc[:, q, v, k:k + 1],
                                                   PS[:, norm_bank(n), 0:w], ALU.mult, ALU.mult).then_inc(s_xn, 1)
                if k == 5 and n + 1 < NORM_NB[q]:
                    diag_vec(dve, q, n + 1)
                if k >= 2:
                    kk = k - 2
                    dve.wait_ge(s_hhi, at_ + kk + 1)
                    nc.vector.scalar_tensor_tensor(h_lo[:, kk, c0:c0 + w], xn[:, (at_ + kk) % 3, 0:w], shift_of(q, kk, v),
                                                   h_hi[:, kk, c0:c0 + w].bitcast(F32), ALU.add, ALU.subtract).then_inc(s_hlo, 1)

        def fold(dve, u, e, o, half, last=False):
            nc.vector.tensor_copy(e[:, 0:half + 1:half], u[:, 0:half + 1:half])
            nc.vector.tensor_tensor(e[:, 1:half], u[:, 1:half], u[:, 2 * half - 1:half:-1], ALU.add)
            ins = nc.vector.tensor_tensor(o[:, 1:half], u[:, 1:half], u[:, 2 * half - 1:half:-1], ALU.subtract)
            if last:
                ins.then_inc(s_fold, 1)

        def conv3(dve, out, src, tap, width):
            chain(dve, nc.vector.tensor_scalar(out[:, 0:width], src[:, 0:width], tap(0), None, ALU.mult))
            chain(dve, nc.vector.scalar_tensor_tensor(out[:, 0:width], src[:, 1:1 + width], tap(1), out[:, 0:width],
                                                      ALU.mult, ALU.add))
            chain(dve, nc.vector.scalar_tensor_tensor(out[:, 0:width], src[:, 2:2 + width], tap(2), out[:, 0:width],
                                                      ALU.mult, ALU.add))

        def fourier_vec(dve, g, last):
            y = Y[:, 4 + g, :]
            if not last:
                dve.wait_ge(s_ld, 2 * g + 1)
                dve.wait_ge(s_qs, 2 * g + 1)
                nc.vector.tensor_tensor(y[:, 0:512], PS[:, 6, 0:512], QS[:, 0:512], ALU.subtract).then_inc(s_fy, 1)
                nc.vector.tensor_tensor(y[:, 1023:512:-1], PS[:, 6, 1:512], QS[:, 1:512], ALU.add).then_inc(s_fy, 1)
                return
            dve.wait_ge(s_ld, 2 * g + 2)
            dve.wait_ge(s_qs, 2 * g + 2)
            nc.vector.tensor_tensor(y[:, 1024:1152], PS[:, 6, 0:P], QS[:, 512:640], ALU.subtract).then_inc(s_fy, 1)
            nc.vector.tensor_tensor(y[:, 1279:1152:-1], PS[:, 6, 1:P], QS[:, 513:640], ALU.add).then_inc(s_fy, 1)
            nc.vector.tensor_copy(y[:, 512:513], PS[:, 6, P:P + 1]).then_inc(s_fy, 1)
            nc.vector.tensor_copy(y[:, 1152:1153], PS[:, 6, P + 1:P + 2]).then_inc(s_fy, 1)

        def mix_lo(dve):
            for n, (c0, w, _) in enumerate(BLOCKS):
                for k in range(KT):
                    dve.wait_ge(s_mhi, n * KT + k + 1)
                    nc.vector.tensor_tensor(h_lo[:, k, c0:c0 + w], Y[:, k, c0:c0 + w],
                                            h_hi[:, k, c0:c0 + w].bitcast(F32), ALU.subtract).then_inc(s_mlo, 1)

        def add_residual(dve, bank, o, c0, w, gate_):
            nc.vector.scalar_tensor_tensor(X[:, o, c0:c0 + w], PS[:, bank, 0:w], gate_, X[:, o, c0:c0 + w],
                                           ALU.mult, ALU.add).then_inc(s_res, 1)

        def ffn_vec(dve, F, ada_from=None):
            nb = F.nb
            m0 = F.layer * ADA + G2
            taps = P + F.layer * 3 * FT

            def lo(i, n, wslot):
                slot = (F.sp + 1 + n) % 2
                dve.wait_ge(s_hi, i * 6 + (F.job + n + 2))
                if wslot is None:
                    nc.vector.tensor_tensor(d_lo[:, n - 3, :], stage[:, slot, :], d_hi[:, n - 3, :].bitcast(F32),
                                            ALU.subtract).then_inc(s_lo, 1)
                else:
                    nc.vector.tensor_tensor(w_lo[:, wslot, :, :], st3[slot], w_hi[:, wslot, :, :].bitcast(F32),
                                            ALU.subtract).then_inc(s_lo, 1)

            def conv(i, half):
                dve.wait_ge(s_fg, i * (2 * nb) + (F.tiles[0] + nb * (half + 1)))
                if not (isinstance(i, int) and i == half == F.tiles[1] == 0):
                    dve.wait_ge(s_alo, i * (2 * nb) + (F.tiles[1] + nb * half))
                f = i * 2 + half
                for t_ in range(3):
                    tap = cols[:, bass.ds(f + (taps + FT * t_), 1)]
                    src = fpad[:, t_:t_ + F.cw]
                    if t_ == 0:
                        ins = nc.vector.tensor_scalar(fcv[:, 0:F.cw], src, tap, None, ALU.mult)
                    else:
                        ins = nc.vector.scalar_tensor_tensor(fcv[:, 0:F.cw], src, tap, fcv[:, 0:F.cw], ALU.mult, ALU.add)
                    if t_ < 2:
                        ins.then_inc(s_v, 1)
                        dve.wait_ge(s_v, i * 4 + (F.v0 + 2 * half + t_ + 1))
                    else:
                        ins.then_inc(s_fc, 1)

            def product(i, half):
                dve.wait_ge(s_fs, i * 2 + (F.fc0 + half + 1))
                for n in range(nb):
                    c0, w, _ = F.blocks[n]
                    s0 = c0 if n < 2 else c0 + 1
                    if isinstance(i, int) and i == half == 0:
                        dve.wait_ge(s_proj, F.proj + 2 * n + 2)
                    else:
                        dve.wait_ge(s_proj, i * (4 * nb) + (F.proj + nb * (2 * half + 1) + n + 1))
                    nc.vector.tensor_tensor(fcv[:, s0:s0 + w], fcv[:, s0:s0 + w], PS[:, 3 + n, 0:w],
                                            ALU.mult).then_inc(s_fp, 1)

            def product_lo(i, half):
                for n in range(nb):
                    c0, w, _ = F.blocks[n]
                    s0 = c0 if n < 2 else c0 + 1
                    dve.wait_ge(s_ahi, i * (2 * nb) + (F.tiles[0] + nb * half + n + 1))
                    nc.vector.tensor_tensor(a_lo[:, half, c0:c0 + w], fcv[:, s0:s0 + w],
                                            a_hi[:, half, c0:c0 + w].bitcast(F32), ALU.subtract).then_inc(s_alo, 1)

            def down(i):
                for o in range(KT):
                    for n, (c0, w, v) in enumerate(F.blocks):
                        c = o * nb + n
                        dve.wait_ge(s_down, i * (KT * nb) + (F.down - KT * nb + c + 1))
                        add_residual(dve, DOWN_BANK[n], o, c0, w, mod[:, m0 + o, v:v + 1])

            def pair(i, first):
                def ada(m):
                    if ada_from is not None:
                        ada_write(dve, i * 4 + (ada_from + m), (ada_from + m) % 2)
                if not first:
                    lo(i, 0, 1 - F.ws)
                    ada(-1)
                conv(i, 0)
                lo(i, 1, F.ws)
                product(i, 0)
                lo(i, 2, 1 - F.ws)
                if not first:
                    down(i)
                product_lo(i, 0)
                lo(i, 3, None)
                lo(i, 4, None)
                ada(0)
                conv(i, 1)
                lo(i, 5, F.ws)
                ada(1)
                product(i, 1)
                ada(2)
                product_lo(i, 1)
            for c_ in (0, 1025, TOK + 2):
                chain(dve, nc.vector.memset(fpad[:, c_:c_ + 1], 0.0))
            F.v0 = vn[0]
            pair(0, True)
            with dve.Fori(1, PAIRS) as i:
                pair(i, False)
            vn[0] += 4 * PAIRS
            if ada_from is not None:
                ada_write(dve, ada_from + 4 * PAIRS - 1)
            if F.layer == 1:
                down(PAIRS)
                return
            gains_vec(dve, 2)
            for n in range(2):
                lo_job(dve, J_ODD + n, (n + 1) % 2)
            for c in range(KT * nb):
                n, o = divmod(c, KT)
                c0, w, v = F.blocks[n]
                dve.wait_ge(s_down, PAIRS * (KT * nb) - KT * nb + c + 1)
                add_residual(dve, c % 3, o, c0, w, mod[:, m0 + o, v:v + 1])
                if c:
                    sum_vec(dve, 2, (c - 1) % KT, (c - 1) // KT)
                if c == 12:
                    diag_vec(dve, 2, 0)
            sum_vec(dve, 2, KT - 1, nb - 1)


        C_QA, C_KA, C_VA, C_QM, C_KM, C_VM, C_OM, C_G = 0, 512, 640, 768, 1024, 1280, 1792, 2304
        odd_tiles = ([("ka", 0), ("va", 0), ("g", 0)] + [("qa", j) for j in range(4)] + [("km", j) for j in range(2)]
                     + [("vm", j) for j in range(4)] + [("qm", j) for j in range(2)] + [("om", j) for j in range(4)])
        odd_nb = [2 if t in ("qa", "qm", "om") else 3 for t, _ in odd_tiles]
        odd_cum = [0]
        for n_ in odd_nb:
            odd_cum.append(odd_cum[-1] + n_)
        NODD = len(odd_tiles)
        J_ODD = J_FFN0 + 6 * PAIRS + 1
        odd_job = [J_ODD + n if n < 2 else J_ODD + n - 1 for n in range(NODD)]
        odd_job[2] = None
        J_OUT1 = J_ODD + NODD - 1
        J_FFN1 = J_OUT1 + KT
        PR_ODD = 3 * J_FFN0 + 12 * PAIRS
        PR_OUT1 = PR_ODD + odd_cum[-1]
        PR_FFN1 = PR_OUT1 + 2 * KT
        PEV_ODD = 24
        RES_OUT1 = RES_FFN0 + 2 * KT
        RES_END = RES_OUT1 + PAIRS * KT * 2
        LAT = BLOCKS[:2]
        F1 = Ffn(1, J_FFN1, LAT, PR_FFN1, RES_OUT1, PAIRS * KT * 3, (6 * PAIRS, 6 * PAIRS), 0)

        s_gz = sem("gate_weights_zeroed")
        s_gw = sem("gate_weights_loaded")
        s_ghl = sem("gate_weights_hi")
        s_gll = sem("gate_weights_lo")
        s_small = sem("small_columns_loaded")
        s_vt = sem("v_transposed")
        s_vc = sem("v_copied")
        s_rtab = sem("rope_tables_loaded")
        s_ones = sem("pads_written")
        s_amk = sem("attention_masks_loaded")
        s_kbd = sem("head_sum_table_loaded")
        s_kq = sem("key_square")
        s_ks = sem("key_sum")
        s_kr = sem("key_root")
        s_kn = sem("key_normalised")
        s_rg = sem("rope_gain_folded")
        s_rc = sem("rope_cosine_part")
        s_ro = sem("rope_rotated")
        s_rd = sem("rope_done")
        s_rq = sem("query_square")
        s_rs = sem("query_sums_by_token")
        s_rr = sem("query_root")
        s_ri = sem("query_scales_written")
        s_kctx = sem("context_keys_copied")
        s_sl = sem("block_operands_copied")
        s_slv = sem("block_values_copied")
        s_slr = sem("block_scales_copied")
        s_S = sem("scores_ready")
        s_nm = sem("score_max_ready")
        s_ex = sem("probs_ready")
        s_pn = sem("probs_normalised")
        s_pt = sem("probs_transposed")
        s_pcA = sem("probs_copied_scalar")
        s_pcV = sem("probs_copied_vector")
        s_O = sem("attention_out_ready")
        s_yA = sem("attention_hi")
        s_yV = sem("attention_lo")
        s_att = sem("attention_chain")
        s_tick = sem("attention_scores_waited_for")
        s_rst = sem("row_tables_loaded")
        s_lnr = sem("scan_resets_loaded")
        s_zr = sem("rows_zeroed")
        s_mx = sem("running_maximum_done")
        s_gxp = sem("minus_m_made")
        s_mr = sem("mlstm_inverse_ready")
        s_hs = sem("mlstm_first_sums")
        s_g1 = sem("log_gate_part")
        s_gexp = sem("gate_rows_exponentiated")
        s_gx = sem("gate_exponents_made")
        s_gt = sem("gate_rows_transposed")
        s_gc = sem("gate_columns_copied")
        s_mA = sem("mlstm_scores_ready")
        s_mB = sem("mlstm_exponents_made")
        s_mC = sem("mlstm_exponentiated")
        s_mD = sem("mlstm_weights_made")
        s_mE = sem("mlstm_out_ready")
        s_wv = sem("mlstm_values_weighted")
        s_mF = sem("mlstm_out_read")
        s_fT = sem("mlstm_out_transposed")
        s_fm = sem("mlstm_gated")
        s_fhi = sem("mlstm_mix_hi")
        s_flo = sem("mlstm_mix_lo")
        s_qh = [sem("query_half_loaded0"), sem("query_half_loaded1")]
        s_wo = [sem("out_rows_loaded0"), sem("out_rows_loaded1")]
        s_oT = sem("out_transposed")
        s_ocA = sem("out_copied_scalar")
        s_ocV = sem("out_copied_vector")
        s_act = sem("scalar_chain")
        an = [0]

        def achain(act, ins):
            an[0] += 1
            ins.then_inc(s_act, 1)
            act.wait_ge(s_act, an[0])

        def odd_view(kind, j):
            w = a["odd_w_in"][0]
            c = {"ka": C_KA, "va": C_VA, "qm": C_QM, "km": C_KM, "vm": C_VM, "om": C_OM}[kind] + j * P
            return w[:, c:c + P].rearrange("(k p) c -> p k c", p=P)

        def layer1_loads(sp):
            for n in range(NODD):
                j = odd_job[n]
                if j is None:
                    sp.wait_ge(s_hlo, 9 * KT)
                    sp.dma_start(kbd[:, :], a["rope_tables"][:, 2176:2304]).then_inc(s_kbd, 16)
                    continue
                kind, t = odd_tiles[n]
                sp.wait_ge(s_lo, j - 1)
                if kind == "qa":
                    wq = a["odd_w_in"][0][:, 0:512].rearrange("(k p) c -> p k c", p=P)
                    sp.dma_start(st3[j % 2][:, :, 0:64], wq[:, :, 64 * t:64 * t + 64]).then_inc(s_qh[j % 2], 16)
                    sp.dma_start(st3[j % 2][:, :, 64:128], wq[:, :, 256 + 64 * t:320 + 64 * t]).then_inc(s_stage[j % 2], 16)
                else:
                    sp.dma_start(st3[j % 2], odd_view(kind, t)).then_inc(s_stage[j % 2], 16)
                if n == 1:
                    sp.wait_ge(s_res, RES_FFN0 - KT)
                    sp.dma_start(xs[:, :, 0:SEQ], X[:, :, 0:SEQ]).then_inc(s_spill, 16)
            sp.wait_ge(s_proj, PR_OUT1)
            sp.dma_start(rtab[:, :], a["rope_tables"]).then_inc(s_rtab, 16)
            sp.dma_start(amask[:, :, :], a["att_masks"]).then_inc(s_amk, 16)
            sp.wait_ge(s_rd, 10)
            sp.dma_start(lnr[0:64, :], a["scan_resets"]).then_inc(s_lnr, 16)
            sp.wait_ge(s_yV, 8)
            sp.dma_start(sel[:, :, :], a["row_select"]).then_inc(s_rst, 16)
            sp.dma_start(mm_mask[:, :, :], a["mlstm_masks"]).then_inc(s_rst, 16)
            for o in range(KT):
                if o == 2:
                    sp.wait_ge(s_flo, 8)
                    sp.dma_start(X[:, :, 0:SEQ], xs[:, :, 0:SEQ]).then_inc(s_back, 16)
                j = J_OUT1 + o
                w = a["odd_w_out"][0][:, o * P:(o + 1) * P]
                sp.wait_ge(s_lo, j - 1)
                for h in range(2):
                    sp.dma_start(st3[j % 2][64 * h:64 * h + 64, 0:4, :],
                                 w[256 * h:256 * h + 256, :].rearrange("(t d) c -> d t c", t=4)).then_inc(s_wo[j % 2], 16)
                sp.dma_start(st3[j % 2][:, 4:8, :], w[512:1024, :].rearrange("(k p) c -> p k c", p=P)).then_inc(s_stage[j % 2], 16)
            ffn_loads(sp, F1)
            for t in range(8):
                sp.wait_ge(s_ocA, t + 1)
                sp.wait_ge(s_ocV, t + 1)
                sp.dma_start(a["out"][0, t * P:(t + 1) * P, :], out_tm[:, t, :]).then_inc(s_out, 16)
            sp.wait_ge(s_out, 8 * 16)

        def layer1_pool(gp):
            for n, (dst, src) in enumerate((
                    (sink[:, :], a["odd_sink"][0:1, :].broadcast_to((P, 8))),
                    (head_g[0:64, 0:1], a["odd_q_g"].rearrange("a d -> d a")), (head_g[64:128, 0:1], a["odd_q_g"].rearrange("a d -> d a")),
                    (head_g[0:64, 1:2], a["odd_k_g"].rearrange("a d -> d a")), (head_g[64:128, 1:2], a["odd_k_g"].rearrange("a d -> d a")))):
                gp.dma_start(dst, src).then_inc(s_small, 16)
            gp.memset(gate_b[:, :], 0.0).then_inc(s_gz, 1)
            gp.wait_ge(s_down, PAIRS * KT * 3)
            gp.wait_ge(s_res, RES_FFN0)
            gp.memset(gw[:, :, :], 0.0).then_inc(s_gz, 1)
            gp.wait_ge(s_gz, 2)
            for q, row in enumerate((0, 64, 32, 96)):
                gp.dma_start(gw[:, :, row:row + 4],
                             a["odd_w_in"][0][:, C_G + 4 * q:C_G + 4 * q + 4].rearrange("(k p) c -> p k c", p=P)).then_inc(s_gw, 16)
                gp.dma_start(gate_b[row:row + 4, :], a["odd_gate_b"][0, q:q + 1, :].rearrange("a h -> h a")).then_inc(s_gw, 16)
            gp.wait_ge(s_rtab, 16)
            gp.wait_ge(s_kn, 3)
            gp.wait_ge(s_pevA, PEV_ODD + odd_cum[-1])
            for u, (src, c0, _, _) in enumerate(rope_units):
                if u >= 2:
                    gp.wait_ge(s_rd, u - 1)
                gp.tensor_tensor(rt[u % 2][:, :], src, COS[:, c0:c0 + 512], ALU.mult).then_inc(s_rc, 1)
            gp.wait_ge(s_rd, 2)
            gp.tensor_copy(k_s[:, 384:640], kA[:, 1024:1280]).then_inc(s_kctx, 1)
            gp.wait_ge(s_kctx, 1)
            gp.wait_ge(s_vc, 3)
            gp.tensor_copy(v_s[:, 3:5, :], vAt[:, 10:12, :]).then_inc(s_kctx, 1)
            gp.memset(q_s[:, :, :], 0.0).then_inc(s_kctx, 1)
            gp.wait_ge(s_kctx, 3)
            gp.wait_ge(s_rd, 10)
            gp.wait_ge(s_ri, 2)

            def block_copies(b, first):
                if not first:
                    gp.wait_ge(s_S, b * 8 - 4)
                    gp.wait_ge(s_slv, b)
                gp.tensor_copy(q_s[0:64, 0:4, :], qA[0:64, :, bass.ds(b * P, P)]).then_inc(s_sl, 1)
                if not first:
                    gp.wait_ge(s_S, b * 8)
                gp.wait_ge(s_sl, b * 3 + 1)
                gp.tensor_copy(k_s[:, 0:384], kP[:, bass.ds(b * P, 384)]).then_inc(s_sl, 1)
                if not first:
                    gp.wait_ge(s_ex, b * 16)
                gp.tensor_copy(rq_s[:, :, :], rq[:, 0:2, bass.ds(b * 8, 8)]).then_inc(s_slr, 1)
                gp.wait_ge(s_slr, b + 1)
                gp.tensor_copy(q_s[64:128, 4:8, :], qA[64:128, :, bass.ds(b * P, P)]).then_inc(s_sl, 1)
                if not first:
                    gp.wait_ge(s_O, b * 4)
                gp.wait_ge(s_sl, b * 3 + 3)
                gp.tensor_copy(v_s[:, 0:3, :], vAt[:, bass.ds(b, 3), :]).then_inc(s_slv, 1)
            block_copies(0, True)
            with gp.Fori(1, 8) as b:
                block_copies(b, False)
            gp.wait_ge(s_yV, 8)
            gp.memset(R_rst[64:128, :], 0.0).then_inc(s_zr, 1)
            gp.memset(R_b[64:128, :], 0.0).then_inc(s_zr, 1)
            gp.wait_ge(s_mx, 1)
            gp.wait_ge(s_zr, 2)
            gp.tensor_tensor(R_del[0:64, :], R_b[0:64, :], R_m[0:64, :], ALU.add).then_inc(s_gxp, 1)

        def layer1_pe(pe):
            first_pair(pe, 2, ((s_lo, J_ODD + 1), (s_lo, J_ODD + 2)), (1, 0), ((s_res, RES_FFN0), (s_fp, 6 * PAIRS)))
            pend = (1, 0)
            for n in range(2, NODD):
                if odd_job[n] is None:
                    pe.wait_ge(s_gll, 1)
                else:
                    pe.wait_ge(s_lo, odd_job[n] + 1)
                for b in range(odd_nb[n]):
                    pe.wait_ge(s_pevA, PEV_ODD + odd_cum[n - 2] + min(b + 1, odd_nb[n - 2]))
                    block_mm(pe, BLOCKS[b], 3 * (n % 2) + b, (n + 1) % 2)
                if pend is not None:
                    if pend[1] == 1:
                        pe.wait_ge(s_kr, 3)
                    v_transposes(pe, *pend)
                if n in (3, 5, 7):
                    u, w = (n - 3) // 2, KN[(n - 3) // 2][1]
                    if u == 0:
                        pe.wait_ge(s_kbd, 16)
                        pe.wait_ge(s_vc, 3)
                    pe.wait_ge(s_kq, u + 1)
                    if u:
                        pe.wait_ge(s_kr, u)
                    nc.tensor.matmul(PS[:, 7, 0:w], kbd[:, :], kt[:, 0:w], start=True, stop=True).then_inc(s_ks, 1)
                pend = (n, V_TILES.index(n)) if n in V_TILES else None
            rope_pe(pe)
            att_pe(pe, 0, True)
            with pe.Fori(1, 8) as i:
                att_pe(pe, i, False)
            att_outputs(pe, 8, 3, 1)
            mlstm_pe(pe)
            for o in range(KT):
                pe.wait_ge(s_lo, J_OUT1 + o + 1)
                for n in range(2):
                    if o < 2:
                        pe.wait_ge(s_mF, MF_END)
                    else:
                        pe.wait_ge(s_res, RES_FFN0 + 2 * (o - 2) + n + 1)
                    block_mm(pe, LAT[n], 3 * (o % 2) + n, o % 2, hook_at=4,
                             hook=(lambda: pe.wait_ge(s_flo, 8)) if o == n == 0 else None)
            norm_cols(pe, 3, 0)
            norm_bcast(pe, 3, 0)
            norm_cols(pe, 3, 1)
            ffn_pe(pe, F1)
            for t in range(8):
                for half in range(2):
                    g = 2 * t + half
                    if g == 0:
                        pe.wait_ge(s_res, RES_END)
                    if g < 6:
                        pe.wait_ge(s_fp, 6 * PAIRS + 4 * PAIRS)
                    else:
                        pe.wait_ge(s_ocA if g % 2 == 0 else s_ocV, (g - 6) // 2 + 1)
                    for k in range(4):
                        last = nc.tensor.transpose(PS[:, g % 6, k * P:(k + 1) * P], X[:, 4 * half + k, t * P:(t + 1) * P], ident[:, :])
                    last.then_inc(s_oT, 1)

        V_TILES = [n for n, (k, _) in enumerate(odd_tiles) if k in ("va", "vm")]
        V_GROUPS = ((0, 4), (4, 4), (8, 2))

        def v_transposes(pe, n, q):
            pe.wait_ge(s_pevA, PEV_ODD + odd_cum[n + 1])
            for g, (t0, cnt) in enumerate(V_GROUPS):
                u = 3 * q + g
                if u >= 2:
                    pe.wait_ge(s_vc, u - 1)
                else:
                    pe.wait_ge(s_xn, 9 * KT)
                for t in range(cnt):
                    last = nc.tensor.transpose(PS[:, 6 + u % 2, t * P:(t + 1) * P], vtmp[:, (t0 + t) * P:(t0 + t + 1) * P], ident[:, :])
                last.then_inc(s_vt, 1)

        KN = ((0, 512), (512, 512), (1024, 256))

        rope_units = [(kA[:, c0:c0 + 512], c0, kP[:, P + c0:P + c0 + 512], None) for c0 in (0, 512)]
        for t in range(4):
            for c0 in (0, 512):
                rope_units.append((qA[:, t, c0:c0 + 512], c0, qA[:, t, c0:c0 + 512], t))

        def rope_pe(pe):
            pe.wait_ge(s_rtab, 16)
            pe.wait_ge(s_kn, 3)
            pe.wait_ge(s_pevA, PEV_ODD + odd_cum[-1])
            for u, (src, c0, _, t) in enumerate(rope_units):
                if u >= 2:
                    pe.wait_ge(s_rd, u - 1)
                elif u == 0:
                    pe.wait_ge(s_vc, 15)
                if t == 0:
                    pe.wait_ge(s_rg, 1)
                nc.tensor.matmul(PS[:, u % 2, :], ROT if t is None else rotg[:, :], src, start=True, stop=True).then_inc(s_ro, 1)
                if t is not None:
                    pe.wait_ge(s_rq, u - 1)
                    for c in range(4):
                        col = (c0 // P + c) * 8 + t
                        last = nc.tensor.matmul(PS[:, 2, col:col + 5:4], rt[3 + u % 2][:, c * P:(c + 1) * P], BD[:, 0:65:64],
                                                start=True, stop=True)
                    last.then_inc(s_rs, 1)

        def att_outputs(pe, i, g, back=0):
            kv, j = divmod(2 * g, 4)
            pe.wait_ge(s_pcA, i * 8 + (2 * g + 2 - 8 * back))
            pe.wait_ge(s_pcV, i * 8 + (2 * g + 2 - 8 * back))
            if g == 0:
                pe.wait_ge(s_slv, i + 1)
                if not isinstance(i, int):
                    pe.wait_ge(s_yV, i)
            for t in range(5):
                last = nc.tensor.matmul(PS[64 * kv:64 * kv + 64, 7, j * P:(j + 2) * P],
                                        v_s[:, t, 64 * kv:64 * kv + 64], pT[:, g % 2, t, :],
                                        start=(t == 0), stop=(t == 4))
            last.then_inc(s_O, 1)

        def att_pe(pe, i, first):
            pe.wait_ge(s_sl, i * 3 + 2)
            if first:
                pe.wait_ge(s_kctx, 3)

            def scores(u):
                if not (first and u < 2):
                    pe.wait_ge(s_nm, i * 8 + (u - 1))
                elif u == 0:
                    pe.wait_ge(s_rr, 1)
                    pe.wait_ge(s_rd, 10)
                if u == 4:
                    pe.wait_ge(s_sl, i * 3 + 3)
                for c in range(2):
                    last = nc.tensor.matmul(PS[:, 2 * (u % 2) + c, 0:320], q_s[:, u, :],
                                            k_s[:, 320 * c:320 * c + 320], start=True, stop=True)
                last.then_inc(s_S, 1)

            def outputs(g, back=0):
                att_outputs(pe, i, g, back)

            scores(0)
            scores(1)
            if not first:
                outputs(3, 1)
            for u in range(8):
                if u % 2 == 0 and u + 2 < 8:
                    scores(u + 2)
                pe.wait_ge(s_pn, i * 8 + (u + 1))
                if not (first and u < 2):
                    pe.wait_ge(s_pcA, i * 8 + (u - 1))
                if not (first and u < 1):
                    pe.wait_ge(s_pcV, i * 8 + u)
                for t in range(5):
                    dst = PS[:, 4 + u % 2, t * P:(t + 1) * P] if t < 4 else PS[:, 6, (u % 2) * P:(u % 2 + 1) * P]
                    last = nc.tensor.transpose(dst, pr[:, u % 3, t * P:(t + 1) * P], ident[:, :])
                last.then_inc(s_pt, 1)
                if u % 2 == 0 and u + 3 < 8:
                    scores(u + 3)
                if u >= 2 and u % 2 == 0:
                    outputs(u // 2 - 1)

        m_units = []
        for st_ in range(10):
            m_units.append((0, 8 + st_ if st_ < 2 else st_ - 2, st_ >= 2))
            m_units.append((1, 9 - st_, st_ >= 2))
        m_out = [n for n, u in enumerate(m_units) if u[2]]
        MF_END = len(m_units)
        m_first = [n for n in m_out if n < max(x for x in m_out if m_units[x][1] == m_units[n][1])]
        finals = sorted(((c, max(n for n, u in enumerate(m_units) if u[2] and u[1] == c)) for c in range(8)),
                        key=lambda f: f[1])

        def mlstm_pe(pe):
            pe.wait_ge(s_yV, 8)
            for g in range(5):
                if g >= 3:
                    pe.wait_ge(s_gc, g - 2)
                for q in range(4 * g, 4 * g + 4):
                    t, c = divmod(q, 10)
                    last = nc.tensor.transpose(PS[:, 3 + g % 3, (q % 4) * P:(q % 4 + 1) * P], kM[:, t, c * P:(c + 1) * P], ident[:, :])
                last.then_inc(s_gt, 1)
            pe.wait_ge(s_gexp, 4)
            srcs = [R_a, R_fl, R_del]
            for q in range(30):
                if q % 8 == 0 and q >= 16:
                    pe.wait_ge(s_gc, 5 + q // 8 - 1)
                kind, c = divmod(q, 10)
                last = nc.tensor.transpose(PS[:, (q // 8) % 2, (q % 8) * 64:(q % 8) * 64 + 64],
                                           srcs[kind][0:64, c * P:(c + 1) * P], ident[0:64, 0:64])
                if q % 8 == 7 or q == 29:
                    last.then_inc(s_gt, 1)
            pe.wait_ge(s_rst, 32)
            for dp in range(4):
                last = nc.tensor.matmul(PS[:, 2, dp * 10:dp * 10 + 10], sel[0:64, 8 + dp, :], m_rows[:, 2, :], start=True, stop=True)
            last.then_inc(s_gt, 1)
            pe.wait_ge(s_zr, 2)
            pe.wait_ge(s_gc, 10)
            order = []
            for n in range(len(m_units) + 1):
                if n < len(m_units) and m_units[n][2]:
                    order.append(("A", n))
                if n >= 1:
                    order.append(("E", n - 1))
                for i, (c, at_) in enumerate(finals):
                    if at_ + 2 == n:
                        order.append(("F", i))
            for what, n in order:
                if what == "F":
                    c, at_ = finals[n]
                    pe.wait_ge(s_mF, at_ + 1)
                    if n:
                        pe.wait_ge(s_fm, n)
                    for h in range(4):
                        last = nc.tensor.transpose(PS[:, 7, h * P:(h + 1) * P], hsum[:, c, h * P:(h + 1) * P], ident[:, :])
                    last.then_inc(s_fT, 1)
                    continue
                d, c, _ = m_units[n]
                o = m_out.index(n) if n in m_out else None
                if what == "A":
                    if o:
                        pe.wait_ge(s_mD, 2 * o)
                    cs = slice(c * P, (c + 1) * P)
                    for h in range(4):
                        r0 = 64 * (h % 2)
                        nc.tensor.matmul(PS[:, h % 2, (h // 2) * P:(h // 2 + 1) * P], kM[r0:r0 + 64, h // 2, cs],
                                         qM[r0:r0 + 64, h // 2, cs], start=True, stop=True)
                    for p2 in range(2):
                        nc.tensor.matmul(PS[:, 0, 256 + p2 * P:256 + (p2 + 1) * P], sel[:, 8 + 2 * d + p2, :],
                                         R_rst[:, cs], start=True, stop=True)
                    for h in range(4):
                        last = nc.tensor.matmul(PS[:, 2, h * P:(h + 1) * P], sel[:, 4 * d + h, :], R_b[:, cs], start=True, stop=True)
                    last.then_inc(s_mA, 1)
                else:
                    nb0 = 3 + 2 * d
                    if n >= 2:
                        pe.wait_ge(s_mF, n - 1)
                        if n - 2 in m_first:
                            pe.wait_ge(s_hs, m_first.index(n - 2) + 1)
                    pe.wait_ge(s_wv, 4 * (n + 1))
                    if o is not None:
                        pe.wait_ge(s_mD, 2 * o + 2)
                        pe.wait_ge(s_mF, n - 1)
                        for h in range(4):
                            r0 = 64 * (h % 2)
                            dst = PS[:, nb0 + h % 2, (h // 2) * 129:(h // 2 + 1) * 129]
                            nc.tensor.matmul(dst, WT[:, d, h, :], vMt[:, c, h, :], start=True, stop=False)
                            nc.tensor.matmul(dst, qt[r0:r0 + 64, d, h // 2, :], C[r0:r0 + 64, 2 * d + h // 2, :], start=False, stop=True)
                    for h in range(4):
                        r0 = 64 * (h % 2)
                        last = nc.tensor.matmul(PS[r0:r0 + 64, nb0 + h // 2, 258:387], kMt[:, c, h * 64:h * 64 + 64],
                                                wv[:, d, h, :], start=True, stop=True)
                    last.then_inc(s_mE, 1)
            c = finals[-1][0]
            pe.wait_ge(s_mF, MF_END)
            pe.wait_ge(s_fm, 7)
            for h in range(4):
                last = nc.tensor.transpose(PS[:, 7, h * P:(h + 1) * P], hsum[:, c, h * P:(h + 1) * P], ident[:, :])
            last.then_inc(s_fT, 1)

        def layer1_act(act):
            for n in range(3):
                h_act(act, 2, n)
            act.wait_ge(s_small, 5 * 16)
            for n, (kind, t) in enumerate(odd_tiles):
                if 1 <= n and n + 1 < NODD:
                    used = PR_ODD + (5 if n == 1 else odd_cum[n])
                    if odd_job[n + 1] is None:
                        act.wait_ge(s_gw, 8 * 16)
                        act.wait_ge(s_proj, used)
                        nc.scalar.activation(w_hi[:, n % 2, :, :], gw[:, :, :], ACT.Copy).then_inc(s_ghl, 1)
                    else:
                        if odd_tiles[n + 1][0] == "qa":
                            act.wait_ge(s_qh[odd_job[n + 1] % 2], 16 * (odd_tiles[n + 1][1] // 2 + 1))
                        hi_job(act, odd_job[n + 1], w_hi[:, n % 2, :, :], used)
                for b in range(odd_nb[n]):
                    c0, w, _ = BLOCKS[b]
                    if b == 0 and n in (4, 6, 8):
                        u = (n - 4) // 2
                        w_ = KN[u][1]
                        act.wait_ge(s_ks, u + 1)
                        nc.scalar.activation(kt[:, 0:w_], PS[:, 7, 0:w_], ACT.Sqrt, bias=eps_t[:, 0:1], scale=1.0 / 64).then_inc(s_kr, 1)
                    if b == 0 and n in (3, 5, 7):
                        u = (n - 3) // 2
                        k0, w_ = KN[u]
                        if u:
                            act.wait_ge(s_kn, u)
                        else:
                            act.wait_ge(s_pevA, PEV_ODD + 3)
                            act.wait_ge(s_hlo, 9 * KT)
                        nc.scalar.activation(kt[:, 0:w_], kA[:, k0:k0 + w_], ACT.Square).then_inc(s_kq, 1)
                    if n == 3 and b == 0:
                        act.wait_ge(s_spill, 32)
                        act.wait_ge(s_hlo, 9 * KT)
                    if kind == "qm" and t == 0 and b == 0:
                        act.wait_ge(s_gll, 1)
                    if n in V_TILES and V_TILES.index(n) and b == 0:
                        act.wait_ge(s_vt, 3 * V_TILES.index(n))
                    act.wait_ge(s_proj, PR_ODD + (2 * b + n + 1 if n < 2 else odd_cum[n] + b + 1))
                    src = PS[:, 3 * (n % 2) + b, 0:w]
                    if kind == "g":
                        ins = nc.scalar.activation(G[:, c0:c0 + w], src, ACT.Identity, bias=gate_b[:, 0:1])
                    elif kind == "om":
                        ins = nc.scalar.activation(oM[:, t, c0:c0 + w], src, ACT.Sigmoid)
                    elif kind == "km":
                        ins = nc.scalar.activation(kM[:, t, c0:c0 + w], src, ACT.Copy, scale=0.125)
                    else:
                        dst = {"ka": kA[:, c0:c0 + w], "qa": qA[:, t, c0:c0 + w] if b < 2 else None, "va": vtmp[:, c0:c0 + w],
                               "vm": vtmp[:, c0:c0 + w], "qm": qM[:, t % 2, c0:c0 + w] if b < 2 else None}[kind]
                        ins = nc.scalar.activation(dst, src, ACT.Copy)
                    ins.then_inc(s_pevA, 1)
            act.wait_ge(s_proj, PR_OUT1)
            act.wait_ge(s_pevA, PEV_ODD + odd_cum[-1])
            for u, (src, _, _, t) in enumerate(rope_units[2:]):
                if u >= 2:
                    act.wait_ge(s_rs, u - 1)
                nc.scalar.activation(rt[3 + u % 2][:, :], src, ACT.Square).then_inc(s_rq, 1)
            act.wait_ge(s_rs, 8)
            nc.scalar.activation(rq[:, 2, :], PS[:, 2, 0:64], ACT.Sqrt, bias=eps_t[:, 0:1], scale=1.0 / 64).then_inc(s_rr, 1)
            att_act(act, 0, True)
            act.wait_ge(s_rd, 10)
            achain(act, nc.scalar.activation(lnr[64:128, :], G[64:128, :], ACT.Abs))
            achain(act, nc.scalar.activation(lnr[64:128, :], lnr[64:128, :], ACT.Exp, scale=-1.0))
            nc.scalar.activation(lnr[64:128, :], lnr[64:128, :], ACT.Ln, bias=ones[64:128, 0:1]).then_inc(s_g1, 1)
            with act.Fori(1, 8) as i:
                att_act(act, i, False)
            att_hi(act, 8)
            mlstm_act(act)
            for o in range(KT):
                if o + 1 < KT:
                    if o:
                        out_hi(act, o + 1)
                else:
                    hi_job(act, F1.job, w_hi[:, F1.ws, :, :], PR_OUT1 + 14)
                for n in range(2):
                    sq_act(act, 3, o, n)
            root_act(act, 3, 0)
            root_act(act, 3, 1)
            h_act(act, 3, 0, {3: lambda: hi_job(act, F1.job + 1, w_hi[:, 1 - F1.ws, :, :], PR_FFN1)})
            h_act(act, 3, 1)
            ffn_act(act, F1)
            for g in range(0, 16, 2):
                act.wait_ge(s_oT, g + 1)
                nc.scalar.activation(out_tm[:, g // 2, 0:512], PS[:, g % 6, :], ACT.Copy).then_inc(s_ocA, 1)

        def out_hi(act, o):
            j = J_OUT1 + o
            act.wait_ge(s_wo[j % 2], 32 * (sum(1 for x in range(o + 1) if (J_OUT1 + x) % 2 == j % 2)))
            hi_job(act, j, w_hi[:, o % 2, :, :], PR_OUT1 - odd_nb[-1] if o == 0 else PR_OUT1 + 2 * (o - 1))

        def att_act(act, i, first):
            def exps(u):
                act.wait_ge(s_nm, i * 8 + (u + 1))
                nc.scalar.activation(st8[:, u, 2:3], sink[:, u:u + 1], ACT.Exp, bias=st8[:, u, 1:2]).then_inc(s_ex, 1)
                nc.scalar.activation(pr[:, u % 3, :], pr[:, u % 3, :], ACT.Exp, bias=st8[:, u, 1:2], scale=rq_s[:, 0, u:u + 1],
                                     accum_out=st8[:, u, 3:4]).then_inc(s_ex, 1)
            exps(0)
            exps(1)
            for u in range(8):
                act.wait_ge(s_pt, i * 8 + (u + 1))
                g = u // 2
                if not (first and g < 2):
                    act.wait_ge(s_O, i * 4 + (g - 1))
                nc.scalar.activation(pT[:, g % 2, 0:4, (u % 2) * P:(u % 2 + 1) * P],
                                     PS[:, 4 + u % 2, :].rearrange("p (t q) -> p t q", t=4), ACT.Copy).then_inc(s_pcA, 1)
                if u + 2 < 8:
                    exps(u + 2)
                if u == 0 and not first:
                    att_hi(act, i)

        def att_hi(act, i):
            act.wait_ge(s_O, i * 4)
            nc.scalar.activation(h_hi[:, 0:4, bass.ds(i * P - P, P)], PS[:, 7, :].rearrange("p (j q) -> p j q", j=4),
                                 ACT.Copy).then_inc(s_yA, 1)

        def mlstm_act(act):
            act.wait_ge(s_yV, 8)
            for g in range(5):
                act.wait_ge(s_gt, g + 1)
                for q in range(4):
                    t, c = divmod(4 * g + q, 10)
                    ins = nc.scalar.activation(kMt[:, c, t * P:(t + 1) * P], PS[:, 3 + g % 3, q * P:(q + 1) * P], ACT.Copy)
                ins.then_inc(s_gc, 1)
            out_hi(act, 0)
            out_hi(act, 1)
            for n, (t, sc) in enumerate(((R_rst, 1.0), (R_fl, 1.0), (R_del, -1.0))):
                act.wait_ge(*((s_gx, n + 1) if n < 2 else (s_gxp, 1)))
                nc.scalar.activation(t[0:64, :], t[0:64, :], ACT.Exp, scale=sc).then_inc(s_gexp, 1)
            act.wait_ge(s_gx, 3)
            nc.scalar.activation(m_rows[:, 2, :], m_rows[:, 2, :], ACT.Exp).then_inc(s_gexp, 1)
            for g in range(5):
                act.wait_ge(s_gt, g + 6)
                if g < 4:
                    cnt = 8 if g < 3 else 6
                    src = PS[:, g % 2, 0:cnt * 64].rearrange("p (s d r) -> p s d r", s=cnt, d=2)[:, :, :, 0:4]
                    nc.scalar.activation(gcol[:, 8 * g:8 * g + cnt, :].rearrange("p s (d r) -> p s d r", d=2), src,
                                         ACT.Copy).then_inc(s_gc, 1)
                else:
                    nc.scalar.activation(dec_bc[:, :, :], PS[:, 2, 0:40].rearrange("p (d c) -> p d c", d=4), ACT.Copy).then_inc(s_gc, 1)
            act.wait_ge(s_gc, 10)

            def values(n):
                d, c, _ = m_units[n]
                if n >= 2:
                    act.wait_ge(s_mE, n - 1)
                for h in range(4):
                    nc.scalar.activation(wv[:, d, h, :], vMt[:, c, h, :], ACT.Copy,
                                         scale=gcol[:, 10 + c, 4 * d + h:4 * d + h + 1]).then_inc(s_wv, 1)
            act.wait_ge(s_ones, 5)
            def final_hi(i):
                c = finals[i][0]
                act.wait_ge(s_fm, i + 1)
                nc.scalar.activation(h_hi[:, 4:8, c * P:(c + 1) * P], gated(c), ACT.Copy).then_inc(s_fhi, 1)

            for n in range(len(m_units) + 1):
                for i, (_, at_) in enumerate(finals):
                    if at_ + 3 == n:
                        final_hi(i)
                if n < len(m_units):
                    d, c, out = m_units[n]
                    values(n)
                    if out:
                        o = m_out.index(n)
                        act.wait_ge(s_mB, 4 * (o + 1))
                        nc.scalar.activation(XE[:, d, :, :], XE[:, d, :, :], ACT.Exp).then_inc(s_mC, 1)
                if n - 1 in m_first:
                    d, c, _ = m_units[n - 1]
                    act.wait_ge(s_mr, m_out.index(n - 1) + 1)
                    act.wait_ge(s_mF, n)
                    for h in range(4):
                        ins = nc.scalar.activation(hsum[:, c, h * P:(h + 1) * P],
                                                   PS[:, 3 + 2 * d + h % 2, (h // 2) * 129:(h // 2) * 129 + P],
                                                   ACT.Copy, scale=den[:, d, h, 1:2])
                    ins.then_inc(s_hs, 1)
            for i, (_, at_) in enumerate(finals):
                if at_ + 3 > len(m_units):
                    final_hi(i)

        def gated(c):
            return hsum[:, c, :].rearrange("p (h t) -> p h t", h=4)

        def layer1_vec(dve):
            for n in range(3):
                h_vec(dve, 2, n)
            dve.wait_ge(s_spill, 32)
            dve.wait_ge(s_hlo, 9 * KT)
            nc.vector.memset(vMt[:, :, :, 128:129], 1.0).then_inc(s_ones, 1)
            nc.vector.memset(vAt[:, 0:1, :], 0.0).then_inc(s_ones, 1)
            nc.vector.memset(vAt[:, 9:10, :], 0.0).then_inc(s_ones, 1)
            for n in range(1, NODD):
                if n + 1 < NODD and odd_job[n + 1] is None:
                    dve.wait_ge(s_ghl, 1)
                    nc.vector.tensor_tensor(w_lo[:, n % 2, :, :], gw[:, :, :], w_hi[:, n % 2, :, :].bitcast(F32),
                                            ALU.subtract).then_inc(s_gll, 1)
                elif n + 1 < NODD:
                    lo_job(dve, odd_job[n + 1], n % 2)
                if n in (4, 6, 8):
                    u = (n - 4) // 2
                    k0, w_ = KN[u]
                    dve.wait_ge(s_kr, u + 1)
                    chain(dve, nc.vector.reciprocal(kt[:, 0:w_], kt[:, 0:w_]))
                    nc.vector.scalar_tensor_tensor(kA[:, k0:k0 + w_], kA[:, k0:k0 + w_], head_g[:, 1:2], kt[:, 0:w_],
                                                   ALU.mult, ALU.mult).then_inc(s_kn, 1)
                if n - 1 in V_TILES:
                    q = V_TILES.index(n - 1)
                    for g, (t0, cnt) in enumerate(V_GROUPS):
                        dve.wait_ge(s_vt, 3 * q + g + 1)
                        src = PS[:, 6 + (3 * q + g) % 2, 0:cnt * P].rearrange("p (t c) -> p t c", t=cnt)
                        if q == 0:
                            r0 = (1, 5, 10)[g]
                            dst = vAt[:, r0:r0 + cnt, :]
                        else:
                            dst = vMt[:, t0:t0 + cnt, q - 1, 0:P]
                        nc.vector.tensor_copy(dst, src).then_inc(s_vc, 1)
            dve.wait_ge(s_proj, PR_OUT1)
            nc.vector.memset(kP[:, 0:P], 0.0).then_inc(s_ones, 1)
            nc.vector.memset(kP[:, P + SEQ:2 * P + SEQ], 0.0).then_inc(s_ones, 1)
            dve.wait_ge(s_rtab, 16)
            dve.wait_ge(s_small, 5 * 16)
            nc.vector.tensor_scalar(rotg[:, :], ROT, head_g[:, 0:1], None, ALU.mult).then_inc(s_rg, 1)
            chain(dve, nc.vector.tensor_scalar(nsink[:, :], sink[:, :], -1.0, None, ALU.mult))
            for u, (_, c0, dst, t) in enumerate(rope_units):
                if u:
                    dve.wait_ge(s_rd, u)
                dve.wait_ge(s_ro, u + 1)
                chain(dve, nc.vector.tensor_tensor(rt[2][:, :], PS[:, u % 2, :], SIN[:, c0:c0 + 512], ALU.mult))
                dve.wait_ge(s_rc, u + 1)
                if t is None:
                    nc.vector.tensor_tensor(dst, rt[u % 2][:, :], rt[2][:, :], ALU.add).then_inc(s_rd, 1)
                else:
                    dve.wait_ge(s_rq, u - 1)
                    nc.vector.scalar_tensor_tensor(dst, rt[u % 2][:, :], head_g[:, 0:1], rt[2][:, :], ALU.mult, ALU.add).then_inc(s_rd, 1)
            dve.wait_ge(s_rr, 1)
            chain(dve, nc.vector.reciprocal(rq[:, 1, :], rq[:, 2, :]))
            nc.vector.tensor_scalar(rq[:, 0, :], rq[:, 1, :], 0.125, None, ALU.mult).then_inc(s_ri, 1)
            dve.wait_ge(s_ri, 1)
            nc.vector.tensor_scalar(rq[:, 1, :], rq[:, 0, :], -1.0, None, ALU.mult).then_inc(s_ri, 1)
            dve.wait_ge(s_amk, 16)
            att_vec(dve, 0, 0, True)
            with dve.Fori(1, 7) as i:
                att_vec(dve, i, 1, False)
            att_vec(dve, 7, 2, False)
            att_lo(dve, 8)
            mlstm_vec(dve)
            for o in range(KT):
                if o + 1 < KT:
                    if o:
                        lo_job(dve, J_OUT1 + o + 1, (o + 1) % 2)
                else:
                    lo_job(dve, F1.job, F1.ws)
                for n, (c0, w, v) in enumerate(LAT):
                    if o == 0 and n == 0:
                        dve.wait_ge(s_back, 32)
                    dve.wait_ge(s_proj, PR_OUT1 + 2 * o + n + 1)
                    add_residual(dve, 3 * (o % 2) + n, o, c0, w, mod[:, ADA + G1 + o, 0:1])
                    if (o, n) != (0, 0):
                        sum_vec(dve, 3, *((o, 0) if n else (o - 1, 1)))
            sum_vec(dve, 3, KT - 1, 1)
            gains_vec(dve, 3)
            diag_vec(dve, 3, 0)
            h_vec(dve, 3, 0, {6: lambda: lo_job(dve, F1.job + 1, 1 - F1.ws)})
            h_vec(dve, 3, 1)
            ffn_vec(dve, F1)
            for g in range(1, 16, 2):
                dve.wait_ge(s_oT, g + 1)
                nc.vector.tensor_copy(out_tm[:, g // 2, 512:1024], PS[:, g % 6, :]).then_inc(s_ocV, 1)

        def att_vec(dve, i, var, first):
            def top(u):
                dve.wait_ge(s_S, i * 8 + (u + 1))
                if u == 0:
                    dve.wait_ge(s_slr, i + 1)
                if u >= 3:
                    dve.wait_ge(s_pt, i * 8 + (u - 2))
                elif not first:
                    dve.wait_ge(s_pt, i * 8)
                nc.vector.tensor_copy(tick[:, u:u + 1], eps_t[:, 0:1]).then_inc(s_tick, 1)
                dve.wait_ge(s_amk, 16)
                nc.vector.tensor_tensor_reduce(out=pr[:, u % 3, :].rearrange("p (c k) -> p c k", c=2),
                                               in0=PS[:, 2 * (u % 2):2 * (u % 2) + 2, 0:320],
                                               in1=amask[:, var, :].rearrange("p (c k) -> p c k", c=2),
                                               scale=1.0, scalar=-3.0e38, op0=ALU.add, op1=ALU.max,
                                               accum_out=st8[:, u, 0:1]).then_inc(s_att, 1)
                dve.wait_ge(s_att, i * 24 + att_n(u, 0))
                nc.vector.tensor_scalar(st8[:, u, 1:2], st8[:, u, 0:1], rq_s[:, 1, u:u + 1], nsink[:, u:u + 1],
                                        ALU.mult, ALU.min).then_inc(s_nm, 1)

            def att_n(u, what):
                return {0: (1, 2, 5, 8, 11, 14, 17, 20), 1: (3, 6, 9, 12, 15, 18, 21, 23), 2: (4, 7, 10, 13, 16, 19, 22, 24)}[what][u]
            top(0)
            top(1)
            for u in range(8):
                dve.wait_ge(s_ex, i * 16 + (2 * u + 2))
                nc.vector.tensor_tensor(st8[:, u, 4:5], st8[:, u, 3:4], st8[:, u, 2:3], ALU.add).then_inc(s_att, 1)
                dve.wait_ge(s_att, i * 24 + att_n(u, 1))
                nc.vector.reciprocal(st8[:, u, 5:6], st8[:, u, 4:5]).then_inc(s_att, 1)
                dve.wait_ge(s_att, i * 24 + att_n(u, 2))
                nc.vector.tensor_scalar(pr[:, u % 3, :], pr[:, u % 3, :], st8[:, u, 5:6], None, ALU.mult).then_inc(s_pn, 1)
                if u + 2 < 8:
                    top(u + 2)
                dve.wait_ge(s_pt, i * 8 + (u + 1))
                g = u // 2
                if not (first and g < 2):
                    dve.wait_ge(s_O, i * 4 + (g - 1))
                nc.vector.tensor_copy(pT[:, g % 2, 4, (u % 2) * P:(u % 2 + 1) * P], PS[:, 6, (u % 2) * P:(u % 2 + 1) * P]).then_inc(s_pcV, 1)
                if u == 0 and not first:
                    att_lo(dve, i)

        def att_lo(dve, i):
            dve.wait_ge(s_yA, i)
            nc.vector.tensor_tensor(h_lo[:, 0:4, bass.ds(i * P - P, P)], PS[:, 7, :].rearrange("p (j q) -> p j q", j=4),
                                    h_hi[:, 0:4, bass.ds(i * P - P, P)].bitcast(F32), ALU.subtract).then_inc(s_yV, 1)

        def mlstm_vec(dve):
            v = nc.vector
            fw, bw, rows_ = slice(0, 32), slice(32, 64), slice(0, 64)
            dve.wait_ge(s_lnr, 16)
            dve.wait_ge(s_rst, 32)
            dve.wait_ge(s_g1, 1)
            chain(dve, v.scalar_tensor_tensor(R_fl[0:64, :], G[64:128, :], 0.0, lnr[64:128, :], ALU.min, ALU.subtract))
            chain(dve, v.tensor_tensor_scan(R_b[fw, :], lnr[fw, :], R_fl[fw, :], 0.0, ALU.mult, ALU.add))
            chain(dve, v.tensor_tensor_scan(R_b[bw, ::-1], lnr[bw, ::-1], R_fl[bw, ::-1], 0.0, ALU.mult, ALU.add))
            chain(dve, v.memset(R_del[0:64, :], 0.0))
            for dst, src in ((R_del[fw, 128:1024:128], R_b[fw, 127:1023:128]), (R_del[fw, 1152:1153], R_b[fw, 1151:1152]),
                             (R_del[fw, 0:1], R_b[fw, 1279:1280]), (R_del[bw, 127:1023:128], R_b[bw, 128:1024:128]),
                             (R_del[bw, 1023:1024], R_b[bw, 1024:1025]), (R_del[bw, 1151:1152], R_b[bw, 1152:1153])):
                chain(dve, v.tensor_copy(dst, src))
            chain(dve, v.tensor_tensor(R_a[rows_, :], G[rows_, :], R_b[rows_, :], ALU.subtract))
            chain(dve, v.tensor_tensor_scan(R_m[fw, 1024:1280], R_del[fw, 1024:1280], R_a[fw, 1024:1280], 0.0, ALU.add, ALU.max))
            chain(dve, v.tensor_tensor_scan(R_m[fw, 0:1024], R_del[fw, 0:1024], R_a[fw, 0:1024], R_m[fw, 1279:1280], ALU.add, ALU.max))
            chain(dve, v.tensor_tensor_scan(R_m[bw, 1279:1023:-1], R_del[bw, 1279:1023:-1], R_a[bw, 1279:1023:-1], 0.0, ALU.add, ALU.max))
            v.tensor_tensor_scan(R_m[bw, 1023::-1], R_del[bw, 1023::-1], R_a[bw, 1023::-1], R_m[bw, 1024:1025],
                                 ALU.add, ALU.max).then_inc(s_mx, 1)
            dve.wait_ge(s_mx, 1)
            chain(dve, v.memset(m_rows[:, :, :], 0.0))
            for dst, x, y in ((m_rows[fw, 0, 1:8], R_m[fw, 127:1023:128], R_b[fw, 127:1023:128]),
                              (m_rows[fw, 0, 0:1], R_m[fw, 1279:1280], R_b[fw, 1279:1280]),
                              (m_rows[fw, 0, 9:10], R_m[fw, 1151:1152], R_b[fw, 1151:1152]),
                              (m_rows[bw, 0, 0:7], R_m[bw, 128:1024:128], R_b[bw, 128:1024:128]),
                              (m_rows[bw, 0, 7:9], R_m[bw, 1024:1153:128], R_b[bw, 1024:1153:128])):
                chain(dve, v.tensor_tensor(dst, x, y, ALU.add))
            chain(dve, v.tensor_copy(m_rows[fw, 1, :], R_m[fw, 127:1280:128]))
            chain(dve, v.tensor_copy(m_rows[bw, 1, :], R_m[bw, 0:1280:128]))
            ch = lambda t: t[0:64, :].rearrange("p (c t) -> p c t", t=P)
            bc = lambda n: m_rows[:, n, :].rearrange("p (c o) -> p c o", o=1).broadcast_to((64, 10, P))
            v.tensor_tensor(ch(R_rst), bc(0), ch(R_m), ALU.subtract).then_inc(s_gx, 1)
            v.tensor_tensor(ch(R_fl), ch(R_a), bc(1), ALU.subtract).then_inc(s_gx, 1)
            v.tensor_tensor(m_rows[:, 2, :], m_rows[:, 0, :], m_rows[:, 1, :], ALU.subtract).then_inc(s_gx, 1)
            dve.wait_ge(s_gx, 3)
            dve.wait_ge(s_gxp, 1)
            chain(dve, v.tensor_scalar(R_b[0:64, :], R_m[0:64, :], -1.0, None, ALU.mult))
            lo_job(dve, J_OUT1, 0)
            lo_job(dve, J_OUT1 + 1, 1)
            dve.wait_ge(s_gc, 10)

            def gate(i):
                c = finals[i][0]
                dve.wait_ge(s_fT, i + 1)
                v.tensor_tensor(gated(c), PS[:, 7, :].rearrange("p (h t) -> p h t", h=4), oM[:, :, c * P:(c + 1) * P],
                                ALU.mult).then_inc(s_fm, 1)

            for n in range(len(m_units) + 1):
                if n < len(m_units) and m_units[n][2]:
                    d, c, _ = m_units[n]
                    o = m_out.index(n)
                    dve.wait_ge(s_mA, o + 1)
                    if o >= 2:
                        dve.wait_ge(s_mE, n - 1)
                        dve.wait_ge(s_mD, 2 * o - 2)
                    for h in range(4):
                        v.scalar_tensor_tensor(XE[:, d, h, :], PS[:, 2, h * P:(h + 1) * P], gcol[:, c, 4 * d + h:4 * d + h + 1],
                                               mm_mask[:, d, :], ALU.add, ALU.add).then_inc(s_mB, 1)
                    v.tensor_tensor(qt[:, d, :, :], qM[:, :, c * P:(c + 1) * P],
                                    PS[:, 0, 256:512].rearrange("p (a b) -> p a b", a=2), ALU.mult)
                    dve.wait_ge(s_mC, o + 1)
                    v.tensor_tensor(WT[:, d, :, :].rearrange("p (a e) t -> p e a t", e=2),
                                    XE[:, d, :, :].rearrange("p (a e) t -> p e a t", e=2),
                                    PS[:, 0:2, 0:256].rearrange("p e (a b) -> p e a b", a=2), ALU.mult).then_inc(s_mD, 2)
                if n >= 1:
                    mlstm_read(dve, n - 1)
                for i, (_, at_) in enumerate(finals):
                    if at_ + 2 == n:
                        gate(i)
            gate(7)
            for i, (c, _) in enumerate(finals):
                dve.wait_ge(s_fhi, i + 1)
                v.tensor_tensor(h_lo[:, 4:8, c * P:(c + 1) * P], gated(c), h_hi[:, 4:8, c * P:(c + 1) * P].bitcast(F32),
                                ALU.subtract).then_inc(s_flo, 1)

        def mlstm_read(dve, n):
            v = nc.vector
            d, c, out = m_units[n]
            nb0 = 3 + 2 * d
            dve.wait_ge(s_mE, n + 1)
            if out:
                dn = PS[:, nb0:nb0 + 2, 128:258:129]
                dst = den[:, d, :, 0].rearrange("p (a e) -> p e a", e=2)
                gm = gcol[:, 20 + c, 4 * d:4 * d + 4].rearrange("p (a e) -> p e a", e=2)
                if n - 2 in m_first:
                    dve.wait_ge(s_hs, m_first.index(n - 2) + 1)
                chain(dve, v.tensor_tensor(dst, dn, gm, ALU.max))
                chain(dve, v.scalar_tensor_tensor(dst, dn, -1.0, dst, ALU.mult, ALU.max))
                v.reciprocal(den[:, d, :, 1], den[:, d, :, 0]).then_inc(s_mr, 1)
                if n not in m_first:
                    dve.wait_ge(s_mr, m_out.index(n) + 1)
                    other = next(x for x in m_first if m_units[x][1] == c)
                    dve.wait_ge(s_hs, m_first.index(other) + 1)
                    for h in range(4):
                        dst = hsum[:, c, h * P:(h + 1) * P]
                        v.scalar_tensor_tensor(dst, PS[:, nb0 + h % 2, (h // 2) * 129:(h // 2) * 129 + P], den[:, d, h, 1:2],
                                               dst, ALU.mult, ALU.add)
            for p2 in range(2):
                src = PS[:, nb0 + p2, 258:387]
                if n < 2:
                    ins = v.tensor_copy(C[:, 2 * d + p2, :], src)
                else:
                    ins = v.scalar_tensor_tensor(C[:, 2 * d + p2, :], C[:, 2 * d + p2, :], dec_bc[:, 2 * d + p2, c:c + 1], src, ALU.mult, ALU.add)
            ins.then_inc(s_mF, 1)

        @block.sync
        def _(sp):
            fc = a["ffn_conv"].rearrange("l w (m p) -> (l w m) p", p=P)
            for dst, src in (
                (rows[0:96, 0, :], a["ada_b"].rearrange("l (m p) -> (l m) p", p=P)),
                (rows[96:128, 0, :], a["norm_g"].rearrange("l s (k p) -> (l s k) p", p=P)),
                (rows[:, 1, :], fc[0:P, :]),
                (rows[0:4, 2, :], fc[P:P + 4, :]),
                (rows[4:16, 2, :], a["even_conv"][0].rearrange("w (m p) -> (w m) p", p=P)),
                (rows[16:24, 2, :], a["c"].rearrange("b (k p) -> (b k) p", p=P)),
                (rows[24:32, 2, :], a["c_ctx"].rearrange("(k p) -> k p", p=P)),
            ):
                sp.dma_start(dst, src).then_inc(s_rows, 16)
            for t in range(NT):
                src = a["x"][0, t * P:(t + 1) * P, :] if t < 8 else a["ctx"][0, (t - 8) * P:(t - 7) * P, :]
                sp.dma_start(x_in[:, t, :], src).then_inc(s_in[t], 16)
            for j in range(NEV):
                load_job(sp, j, cols_of(a["even_w_in"][0], even_tiles[j]))
                if j == 1:
                    sp.wait_ge(s_xcA, NT)
                    sp.wait_ge(s_xcV, NT)
                    sp.wait_ge(s_amm, 16)
                    sp.dma_start(xs, X[:, :, :]).then_inc(s_spill, 16)
                if j == 3:
                    sp.wait_ge(s_spill, 16)
                    sp.wait_ge(s_hlo, 3 * KT)
                    sp.dma_start(xf[:, 0:n_tab], a["dft_tables"]).then_inc(s_tab, 16)
                    sp.dma_start(TAIL[0:2, :], a["dft_tails"]).then_inc(s_tab, 16)
            for o in range(KT):
                load_job(sp, J_OUT0 + o, cols_of(a["even_w_out"][0], o))
                if o == 1:
                    sp.wait_ge(s_fy, 4 * FY)
                    sp.wait_ge(s_pevV, 24)
                    sp.dma_start(X[:, :, :], xs).then_inc(s_back, 16)
            ffn_loads(sp, F0)
            layer1_loads(sp)

        @block.gpsimd
        def _(gp):
            done = 0

            def step(ins):
                nonlocal done
                done += 1
                ins.then_inc(s_const, 1)
                gp.wait_ge(s_const, done)
            step(gp.memset(ident[:, :], 0.0))
            step(gp.memset(ones[:, :], 1.0))
            step(gp.memset(eps_t[:, :], EPS))
            step(gp.memset(cT[:, :, :], 0.0))
            step(gp.memset(pick[:, :], 0.0))
            step(gp.affine_select(out=ident[:, :], in_=ident[:, :], compare_op=ALU.not_equal, fill=1.0,
                                  base=0, pattern=[[-1, P]], channel_multiplier=1))
            for q in range(4):
                step(gp.affine_select(out=pick[:, :], in_=pick[:, :], compare_op=ALU.not_equal, fill=1.0,
                                      base=-32 * q, pattern=[[-1, 2]], channel_multiplier=1))
            for j in range(2 * ADA):
                src = cols_of(a["ada_w"][j // ADA], j % ADA)
                if 2 <= j < 2 + ADA_X:
                    gp.dma_start(ada_x[:, j - 2, :, :], src).then_inc(s_ax[j - 2], 16)
                    continue
                if j >= 2 + ADA_X:
                    gp.wait_ge(s_amm, j - 1 if j >= 4 + ADA_X else j - ADA_X - 1)
                gp.dma_start(ada_st[:, j % 2, :, :], src).then_inc(s_al[j % 2], 16)
            layer1_pool(gp)

        @block.tensor
        def _(pe):
            pe.wait_ge(s_const, CONST)
            pe.wait_ge(s_rows, 7 * 16)
            for r, n in enumerate((P, P, 32)):
                last = nc.tensor.transpose(PS[:, 7, r * P:r * P + n], rows[0:n, r, :], ident[0:n, 0:n])
            last.then_inc(s_rowT, 1)
            for t in range(NT):
                pe.wait_ge(s_in[t], 16)
                for half in range(2):
                    g = 2 * t + half
                    if g >= 6:
                        pe.wait_ge(s_xcA if g % 2 == 0 else s_xcV, (g - 6) // 2 + 1)
                    for k in range(4):
                        last = nc.tensor.transpose(PS[:, g % 6, k * P:(k + 1) * P],
                                                   x_in[:, t, (4 * half + k) * P:(4 * half + k + 1) * P], ident[:, :])
                    last.then_inc(s_xT, 1)
            pe.wait_ge(s_ct, 1)
            pe.wait_ge(s_cols, 1)
            first_ada(pe, 0)
            for g in range(4):
                if g < 3:
                    first_ada(pe, g + 1)
                first_ada_sum(pe, g)
                if g < 3:
                    norm_cols(pe, 0, g)
            pe.wait_ge(s_mod, 16)
            norm_bcast(pe, 0, 0)
            first_pair(pe, 0, ((s_lo, 1), (s_lo, 2)), (0, 1), ((s_xcA, NT), (s_xcV, NT)))
            for j in range(2, NEV):
                if 3 <= j <= 6:
                    fourier_pe(pe, j - 3, 3)
                pe.wait_ge(s_lo, j + 1)
                for n in range(3):
                    if 2 <= j < 6:
                        pe.wait_ge(s_pevA, 3 * (j - 2) + n + 1)
                    elif j >= 6:
                        jj, kind = divmod(j - 6, 3)
                        if kind == 0:
                            pe.wait_ge(s_pevA, 12 + 3 * jj + n + 1)
                        else:
                            pe.wait_ge(s_pevV, 6 * jj + 3 * (kind - 1) + n + 1)
                    block_mm(pe, BLOCKS[n], 3 * (j % 2) + n, j % 2,
                             hook=(lambda: fourier_pe(pe, j - 2, n)) if j <= 5 else None)
                    if j >= 6:
                        m = 16 + 3 * (j - 6) + n
                        if m < ADA - 2:
                            if m == 16:
                                pe.wait_ge(s_fy, 4 * FY)
                            ada_at(pe, m, m > 16)
            for o in range(KT):
                pe.wait_ge(s_lo, J_OUT0 + o + 1)
                for n in range(3):
                    if o < 2:
                        if n == 0:
                            pe.wait_ge(s_pevV, 24)
                    else:
                        pe.wait_ge(s_res, 3 * (o - 2) + n + 1)
                    block_mm(pe, BLOCKS[n], 3 * (o % 2) + n, o % 2, KT * n if o == 0 else None, ready_sem=s_mlo)
                    if n == 0 and 1 <= o <= 6:
                        ada_at(pe, ADA + o - 3)
                    elif n == 0 and o == 7:
                        ada_sum(pe, ADA + 3, 1)
                    elif (o, n) == (7, 1):
                        pe.wait_ge(s_mod, ADA + 4)
                        norm_cols(pe, 1, 0)
            norm_bcast(pe, 1, 0)
            norm_cols(pe, 1, 1)
            norm_cols(pe, 1, 2)
            ffn_pe(pe, F0, ADA + 4)
            layer1_pe(pe)

        @block.scalar
        def _(act):
            act.wait_ge(s_rowT, 1)
            nc.scalar.activation(cols[:, :], PS[:, 7, 0:288], ACT.Copy).then_inc(s_cols, 1)
            act.wait_ge(s_cols, 1)
            act.wait_ge(s_const, CONST)
            nc.scalar.activation(cT[:, :, 0:2].rearrange("p k v -> p v k"),
                                 cols[:, 272:288].rearrange("p (v k) -> p v k", v=2), ACT.Silu).then_inc(s_ct, 1)
            for g in range(0, 2 * NT, 2):
                act.wait_ge(s_xT, g + 1)
                nc.scalar.activation(X[:, 0:4, (g // 2) * P:(g // 2 + 1) * P],
                                     PS[:, g % 6, :].rearrange("p (k t) -> p k t", k=4), ACT.Copy).then_inc(s_xcA, 1)
            for g in range(6):
                for q in range(4 * g, 4 * g + 4):
                    sq_act(act, 0, q % KT, q // KT)
                if g == 3:
                    root_act(act, 0, 0)
                if g in (1, 2, 3, 5):
                    m = min(g - 1, 3)
                    act.wait_ge(s_amm, 4 * m + 4)
                    nc.scalar.activation(ada4[:, m, :], PS[:, 3 + m, :], ACT.Copy).then_inc(s_aev, 4)
                if g >= 4:
                    root_act(act, 0, g - 3)
            hi_job(act, 0, w_hi[:, 0, :, :])
            hi_job(act, 1, w_hi[:, 1, :, :])
            for n in range(3):
                h_act(act, 0, n)
            for j in range(NEV):
                if j == 0:
                    hi_job(act, 2, w_hi[:, 0, :, :], 5)
                elif j > 1:
                    hi_job(act, j + 1, w_hi[:, (j + 1) % 2, :, :], 3 * j)
                if 3 <= j <= 6:
                    fourier_act(act, j - 3, True)
                if 2 <= j <= 5:
                    fourier_act(act, j - 2, False)
                for n, (c0, w, _) in enumerate(BLOCKS):
                    bank = 3 * (j % 2) + n
                    if j < 4:
                        if j == 0 and n == 0:
                            act.wait_ge(s_spill, 16)
                            act.wait_ge(s_hlo, 3 * KT)
                        if j and n == 0:
                            act.wait_ge(s_fold, j)
                        act.wait_ge(s_proj, 2 * n + j + 1 if j < 2 else 3 * j + n + 1)
                        nc.scalar.activation(U[:, c0:c0 + w], PS[:, bank, 0:w], ACT.Copy).then_inc(s_pevA, 1)
                    elif (j - 4) % 3 == 0:
                        if n == 0:
                            conv_free(act, (j - 4) // 3)
                        act.wait_ge(s_proj, 3 * j + n + 1)
                        g0 = c0 + 1 if n < 2 else c0 + 2
                        nc.scalar.activation(gpad[:, g0:g0 + w], PS[:, bank, 0:w], ACT.Copy).then_inc(s_pevA, 1)
                    if j >= 6:
                        ada_copy(act, 16 + 3 * (j - 6) + n)
            mix_hi(act, 3 * NEV)
            for o in range(1, KT):
                hi_job(act, J_OUT0 + o, w_hi[:, o % 2, :, :], 3 * (J_OUT0 + o - 1))
                for n in range(3):
                    sq_act(act, 1, o - 1, n)
                if 1 <= o <= 6:
                    ada_copy(act, ADA + o - 3)
            hi_job(act, F0.job, w_hi[:, F0.ws, :, :], 3 * (J_OUT0 + 7))
            sq_act(act, 1, KT - 1, 0)
            sq_act(act, 1, KT - 1, 1)
            root_act(act, 1, 0)
            sq_act(act, 1, KT - 1, 2)
            root_act(act, 1, 1)
            root_act(act, 1, 2)
            h_act(act, 1, 0, {3: lambda: hi_job(act, F0.job + 1, w_hi[:, 1 - F0.ws, :, :], F0.proj)})
            h_act(act, 1, 1)
            h_act(act, 1, 2)
            ffn_act(act, F0, ADA + 4)
            layer1_act(act)

        @block.vector
        def _(dve):
            for g in range(1, 2 * NT, 2):
                dve.wait_ge(s_xT, g + 1)
                nc.vector.tensor_copy(X[:, 4:8, (g // 2) * P:(g // 2 + 1) * P],
                                      PS[:, g % 6, :].rearrange("p (k t) -> p k t", k=4)).then_inc(s_xcV, 1)
            dve.wait_ge(s_cols, 1)
            for g in range(6):
                for q in range(4 * g, 4 * g + 4):
                    sum_vec(dve, 0, q % KT, q // KT)
                if g == 4:
                    diag_vec(dve, 0, 0)
                if g in (1, 3, 4, 5):
                    m = (1, 3, 4, 5).index(g)
                    dve.wait_ge(s_asel, 4 * m + 4)
                    nc.vector.tensor_tensor(mod[:, 4 * m:4 * m + 4, :], PS[:, 7, 0:8].rearrange("p (m v) -> p m v", v=2),
                                            cols[:, 4 * m:4 * m + 4].rearrange("p (m o) -> p m o", o=1).broadcast_to((P, 4, 2)),
                                            ALU.add).then_inc(s_mod, 4)
            gains_vec(dve, 0)
            lo_job(dve, 0, 0)
            lo_job(dve, 1, 1)
            for n in range(3):
                h_vec(dve, 0, n)
            for c_ in (0, 1025, TOK + 2):
                chain(dve, nc.vector.memset(gpad[:, c_:c_ + 1], 0.0))
            dve.wait_ge(s_spill, 16)
            dve.wait_ge(s_hlo, 3 * KT)
            chain(dve, nc.vector.memset(FO[:, 0:1], 0.0))
            chain(dve, nc.vector.memset(FO[:, 512:513], 0.0))
            for j in range(NEV):
                if j != 1:
                    lo_job(dve, j + 1 if j else 2, (j + 1) % 2 if j else 0)
                if 3 <= j <= 6:
                    fourier_vec(dve, j - 3, True)
                if 1 <= j <= 4:
                    dve.wait_ge(s_pevA, 3 * j)
                    if j > 1:
                        dve.wait_ge(s_ch, 2 * (j - 1))
                    fold(dve, U[:, 0:1024], FE[:, 0:513], FO[:, 0:512], 512)
                    fold(dve, U[:, 1024:1280], FE[:, 516:645], FO[:, 512:640], 128, last=True)
                if 2 <= j <= 5:
                    fourier_vec(dve, j - 2, False)
                jj, kind = divmod(j - 4, 3)
                for n, (c0, w, _) in enumerate(BLOCKS):
                    bank = 3 * (j % 2) + n
                    s0 = c0 if n < 2 else c0 + 1
                    if j >= 4 and kind == 1:
                        dve.wait_ge(s_pevA, 12 + 3 * jj + n + 1)
                        dve.wait_ge(s_proj, 3 * j + n + 1)
                        nc.vector.tensor_tensor(gpad[:, s0 + 1:s0 + 1 + w], gpad[:, s0 + 1:s0 + 1 + w],
                                                PS[:, bank, 0:w], ALU.mult).then_inc(s_pevV, 1)
                    elif j >= 4 and kind == 2:
                        dve.wait_ge(s_proj, 3 * j + n + 1)
                        nc.vector.tensor_tensor(Y[:, jj, c0:c0 + w], conv_e[:, s0:s0 + w],
                                                PS[:, bank, 0:w], ALU.mult).then_inc(s_pevV, 1)
                    if j >= 6 and (j, n) != (6, 0):
                        ada_write(dve, 16 + 3 * (j - 6) + n - 1)
                if j >= 4 and kind == 1:
                    dve.wait_ge(s_pevV, 6 * jj + 3)
                    dve.wait_ge(s_ch, 8)
                    conv3(dve, conv_e, gpad, lambda w_: cols[:, 260 + 4 * w_ + jj:261 + 4 * w_ + jj], TOK + 1)
            mix_lo(dve)
            for o in range(KT):
                if o + 1 < KT:
                    lo_job(dve, J_OUT0 + o + 1, (o + 1) % 2)
                else:
                    lo_job(dve, F0.job, F0.ws)
                for n, (c0, w, v) in enumerate(BLOCKS):
                    if o == 0 and n == 0:
                        dve.wait_ge(s_back, 16)
                    dve.wait_ge(s_proj, 3 * (J_OUT0 + o) + n + 1)
                    add_residual(dve, 3 * (o % 2) + n, o, c0, w, mod[:, G1 + o, v:v + 1])
                    if (o, n) != (0, 0):
                        sum_vec(dve, 1, *((o, n - 1) if n else (o - 1, 2)))
                    if n == 0 and 1 <= o <= 7:
                        ada_write(dve, ADA + o - 4)
                    if (o, n) == (7, 1):
                        gains_vec(dve, 1)
                    if (o, n) == (7, 2):
                        diag_vec(dve, 1, 0)
            sum_vec(dve, 1, KT - 1, 2)
            h_vec(dve, 1, 0, {6: lambda: lo_job(dve, F0.job + 1, 1 - F0.ws)})
            h_vec(dve, 1, 1)
            h_vec(dve, 1, 2)
            ffn_vec(dve, F0, ADA + 4)
            layer1_vec(dve)


def dft_tables():
    def cs(rows, cols_, length, scale):
        x = 2 * np.pi * ((rows[:, None] * cols_[None, :]) % length) / length
        return np.cos(x) * scale, np.sin(x) * scale
    t, k = np.arange(P), np.arange(512)
    channel = list(cs(t, t, P, P ** -0.5))
    latent = [cs(t + P * j, k, SEQ, SEQ ** -0.5) for j in range(4)]
    alt = np.where(t % 2 == 0, 1.0, -1.0)
    parts = channel + [c for c, _ in latent] + [s for _, s in latent]
    parts += list(cs(t, t, CTX, CTX ** -0.5)) + [np.stack([alt / 32, alt / 16], 1)]
    tails = np.zeros((2, 642), np.float32)
    tails[0, 0:512] = np.where(k % 2 == 0, 1, -1) / 32
    tails[1, 512:640] = alt / 16
    tails[0, 640], tails[1, 641] = 1 / 32, 1 / 16
    return np.concatenate(parts, 1).astype(np.float32), tails


def rope_tables():
    f32 = np.float32
    row, col = np.repeat(np.arange(SEQ // 64, dtype=f32), 64), np.tile(np.arange(64, dtype=f32), SEQ // 64)
    inv = (f32(10000.0) ** (-np.arange(0, 32, 2, dtype=f32) / f32(32))).astype(f32)
    rope = np.zeros((P, 2304), f32)
    for p in range(P):
        d = p % 64
        angle = ((row if d < 32 else col) * inv[d % 16]).astype(f32)
        rope[p, 0:1024], rope[p, 1024:2048] = np.cos(angle), np.sin(angle)
        if (d % 32) < 16:
            rope[p + 16, 2048 + p] = -1
        else:
            rope[p - 16, 2048 + p] = 1
        rope[(p // 64) * 64:(p // 64) * 64 + 64, 2176 + p] = 1
    return rope


def mask_tables():
    f32, neg = np.float32, np.float32(-1e30)
    q, k = np.arange(P)[:, None], np.arange(384)[None, :]
    att = np.zeros((P, 3, 640), f32)
    att[:, :, 0:384] = np.where(np.abs(k - (q + P)) <= P, 0, neg)[:, None, :]
    att[:, 0, 0:P] = neg
    att[:, 2, 2 * P:3 * P] = neg
    resets = np.ones((64, TOK), f32)
    resets[0:32, 0::P] = 0
    resets[32:64, P - 1::P] = 0
    sel = np.zeros((P, 12, P), f32)
    for d in range(2):
        for h in range(4):
            sel[32 * d + h, 4 * d + h, :] = 1
        for pair in range(2):
            sel[32 * d + 2 * pair, 8 + 2 * d + pair, 0:64] = 1
            sel[32 * d + 2 * pair + 1, 8 + 2 * d + pair, 64:128] = 1
    s, t = np.arange(P)[:, None], np.arange(P)[None, :]
    causal = np.stack([np.where(s <= t, 0, neg), np.where(s >= t, 0, neg)], 1).astype(f32)
    return att, resets, sel, causal


INPUTS = ["x", "c", "ctx", "c_ctx", "ada_w", "ada_b", "norm_g", "even_w_in", "even_conv", "even_w_out", "odd_w_in",
          "odd_gate_b", "odd_q_g", "odd_k_g", "odd_sink", "odd_w_out", "ffn_w_up", "ffn_conv", "ffn_w_down"]


def kernel(**inputs):
    import concourse.bacc as bacc
    from concourse.bass_utils import run_bass_kernel_spmd

    laid = {name: np.ascontiguousarray(inputs[name]) for name in INPUTS}
    laid["dft_tables"], laid["dft_tails"] = dft_tables()
    laid["rope_tables"] = rope_tables()
    laid["att_masks"], laid["scan_resets"], laid["row_select"], laid["mlstm_masks"] = mask_tables()
    nc = bacc.Bacc("TRN2", target_bir_lowering=False, num_devices=1)
    arrays, args = {}, {}
    for name, value in laid.items():
        arrays[f"in_{name}_dram"] = value
        args[name] = nc.dram_tensor(f"in_{name}_dram", value.shape, mybir.dt.from_np(value.dtype),
                                    kind="ExternalInput").ap()
    args["out"] = nc.dram_tensor("out_0_dram", (1, SEQ, DM), F32, kind="ExternalOutput").ap()
    program(nc, args)
    result = run_bass_kernel_spmd(nc, [arrays], core_ids=[0])
    return result.results[0]["out_0_dram"]
```
